# Optimizing a Trainium2 kernel written in Bass

```python
import math
import jax, jax.numpy as jnp
from jax import lax
import numpy as np

D_MODEL = 1024
BATCH = 1
SEQ = 1024
DEPTH = 2
DEC_BATCH = 8
DEC_SEQ = 4
PAST_LEN = 1024
PAGE_SIZE = 128

N_EVEN = (DEPTH + 1) // 2
N_ODD = DEPTH // 2
HEAD_DIM = 64
MIX_WIDTH = D_MODEL
S5_WIDTH = MIX_WIDTH // 2
S5_GROUP = 16
S5_GROUPS = S5_WIDTH // S5_GROUP
S5_STATE = 64
SB_HEADS = (MIX_WIDTH - S5_WIDTH) // HEAD_DIM
SB_WIDTH = SB_HEADS * HEAD_DIM
EVEN_IN = S5_WIDTH + 3 * SB_WIDTH
RWKV_HEADS = (MIX_WIDTH // 2) // HEAD_DIM
RWKV_WIDTH = RWKV_HEADS * HEAD_DIM
RWKV_DECAY_RANK = 64
RWKV_A_RANK = 64
RWKV_GATE_RANK = 128
RWKV_IN = 3 * RWKV_WIDTH + RWKV_DECAY_RANK + RWKV_A_RANK + RWKV_GATE_RANK
RWKV_DECAY_SCALE = 0.606531
RWKV_GN_EPS = 64e-5
DSA_HEADS = (MIX_WIDTH - RWKV_WIDTH) // HEAD_DIM
DSA_WIDTH = DSA_HEADS * HEAD_DIM
IDX_HEADS = 8
IDX_DIM = 32
TOPK_MAX = 256
ODD_IN = RWKV_IN + 3 * DSA_WIDTH + IDX_HEADS * IDX_DIM + IDX_HEADS + IDX_DIM
REL_BUCKETS = 32
REL_MAX_DIST = 128
D_FF = 2816
CONV_W = 3
Q_BLOCK = 128
RMS_EPS = 1e-6

kernel_name = 'hybrid_s5_stickbreak_rwkv7_dsa_step'

def rmsnorm(x, g):
    x32 = x.astype(jnp.float32)
    y = x32 * lax.rsqrt(jnp.mean(x32 * x32, axis=-1, keepdims=True) + RMS_EPS)
    return y.astype(x.dtype) * g

def split_cols(p, widths):
    return jnp.split(p, np.cumsum(widths)[:-1].tolist(), axis=-1)

def to_blocks(t):
    n_b = t.shape[1] // Q_BLOCK
    return t.reshape((t.shape[0], n_b, Q_BLOCK) + t.shape[2:]).swapaxes(0, 1)

def from_blocks(o):
    return o.swapaxes(0, 1).reshape((o.shape[1], o.shape[0] * o.shape[2]) + o.shape[3:])

def gather_pages(pool, page_table):
    g = pool[page_table]
    return g.reshape((g.shape[0], g.shape[1] * g.shape[2]) + g.shape[3:])

def take_rows(rows, idx):
    return jax.vmap(lambda r, i: r[i])(rows, idx)

def s5_mixer(u, h0_re, h0_im, lam_re, lam_im, log_step, b_re, b_im, c_re, c_im, d, w_glu, b_glu):
    bsz, t_len, _ = u.shape
    ug = u.reshape(bsz, t_len, S5_GROUPS, S5_GROUP)
    step = jnp.exp(log_step)[:, None]
    mag = jnp.exp(lam_re * step)
    lb_re = mag * jnp.cos(lam_im * step)
    lb_im = mag * jnp.sin(lam_im * step)
    den = lam_re * lam_re + lam_im * lam_im
    cf_re = ((lb_re - 1) * lam_re + lb_im * lam_im) / den
    cf_im = (lb_im * lam_re - (lb_re - 1) * lam_im) / den
    bb_re = cf_re[..., None] * b_re - cf_im[..., None] * b_im
    bb_im = cf_re[..., None] * b_im + cf_im[..., None] * b_re
    bu_re = jnp.einsum('gph,btgh->btgp', bb_re, ug)
    bu_im = jnp.einsum('gph,btgh->btgp', bb_im, ug)
    a_re = jnp.broadcast_to(lb_re, bu_re.shape)
    a_im = jnp.broadcast_to(lb_im, bu_im.shape)

    def combine(e1, e2):
        a1r, a1i, b1r, b1i = e1
        a2r, a2i, b2r, b2i = e2
        return (a1r * a2r - a1i * a2i, a1r * a2i + a1i * a2r,
                a2r * b1r - a2i * b1i + b2r, a2r * b1i + a2i * b1r + b2i)

    ac_re, ac_im, hs_re, hs_im = lax.associative_scan(combine, (a_re, a_im, bu_re, bu_im), axis=1)
    h_re = hs_re + ac_re * h0_re[:, None] - ac_im * h0_im[:, None]
    h_im = hs_im + ac_re * h0_im[:, None] + ac_im * h0_re[:, None]
    y = (jnp.einsum('ghp,btgp->btgh', c_re, h_re) - jnp.einsum('ghp,btgp->btgh', c_im, h_im) + d * ug)
    y = jax.nn.gelu(y.reshape(bsz, t_len, S5_WIDTH))
    out = y * jax.nn.sigmoid(y @ w_glu + b_glu)
    return out, h_re[:, -1], h_im[:, -1]

def stick_breaking_block(q, k, v, q_pos, k_pos):
    logit = jnp.einsum('bqhd,bkhd->bhqk', q, k).astype(jnp.float32) * (HEAD_DIM ** -0.5)
    before = k_pos[None, :] < q_pos[:, None]
    log_beta = jax.nn.log_sigmoid(logit)
    log_keep = jnp.where(before, jax.nn.log_sigmoid(-logit), 0.0)
    log_between = lax.cumsum(log_keep, axis=3, reverse=True) - log_keep
    w = jnp.where(before, jnp.exp(log_beta + log_between), 0.0)
    return jnp.einsum('bhqk,bkhd->bqhd', w.astype(v.dtype), v)

def stick_breaking_prompt(q, k, v):
    k_pos = jnp.arange(q.shape[1], dtype=jnp.int32)
    out = lax.map(lambda a: stick_breaking_block(a[0], k, v, a[1], k_pos),
                  (to_blocks(q), k_pos.reshape(-1, Q_BLOCK)))
    return from_blocks(out)

def rwkv7_mixer(cols, shift_prev, s0, mu, w0, w2, a0, a2, g2, k_k, k_a, r_k, ln_g, ln_b):
    bsz, t_len, _ = cols.shape
    dt = cols.dtype
    prev = jnp.concatenate([shift_prev[:, None].astype(dt), cols[:, :-1]], axis=1)
    xs = cols + (prev - cols) * mu
    r, k, v, xw, xa, xg = split_cols(xs, [RWKV_WIDTH] * 3 + [RWKV_DECAY_RANK, RWKV_A_RANK, RWKV_GATE_RANK])
    decay = jnp.exp(-RWKV_DECAY_SCALE * jax.nn.sigmoid(w0 + jnp.tanh(xw) @ w2))
    a = jax.nn.sigmoid(a0 + xa @ a2)
    g = jax.nn.sigmoid(xg) @ g2

    def heads(t):
        return t.reshape(bsz, t_len, RWKV_HEADS, HEAD_DIM)

    kk = heads(k * k_k).astype(jnp.float32)
    kk = (kk / jnp.maximum(jnp.sqrt(jnp.sum(kk * kk, axis=-1, keepdims=True)), 1e-12)).astype(dt)
    k = k * (1 + (a - 1) * k_a)
    r_h, w_h, k_h, v_h, a_h = heads(r), heads(decay), heads(k), heads(v), heads(a)

    def step(s, inp):
        r_t, w_t, k_t, v_t, kk_t, a_t = inp
        s_kk = jnp.einsum('bhvk,bhk->bhv', s, kk_t)
        s = (s * w_t[:, :, None, :] - s_kk[..., None] * (kk_t * a_t)[:, :, None, :]
             + v_t[..., None] * k_t[:, :, None, :]).astype(s.dtype)
        return s, jnp.einsum('bhvk,bhk->bhv', s, r_t)

    s_last, y = lax.scan(step, s0, tuple(t.swapaxes(0, 1) for t in (r_h, w_h, k_h, v_h, kk, a_h)))
    y = y.swapaxes(0, 1).astype(jnp.float32)
    mean = jnp.mean(y, axis=-1, keepdims=True)
    var = jnp.mean(jnp.square(y - mean), axis=-1, keepdims=True)
    y = ((y - mean) * lax.rsqrt(var + RWKV_GN_EPS)).astype(dt).reshape(bsz, t_len, RWKV_WIDTH) * ln_g + ln_b
    bonus = jnp.sum(r_h * k_h * r_k, axis=-1, keepdims=True) * v_h
    out = (y + bonus.reshape(bsz, t_len, RWKV_WIDTH)) * g
    return out, cols[:, -1], s_last

def t5_bucket(dist):
    exact = REL_BUCKETS // 2
    d = jnp.maximum(dist, 0)
    far = exact + (jnp.log(jnp.maximum(d, 1).astype(jnp.float32) / exact)
                   / math.log(REL_MAX_DIST / exact) * (REL_BUCKETS - exact)).astype(jnp.int32)
    return jnp.where(d < exact, d, jnp.minimum(far, REL_BUCKETS - 1))

def indexer_topk(iq, iw, ik, q_pos, k_pos, n_sel):
    rel = jax.nn.relu(jnp.einsum('bqhd,bld->bqhl', iq, ik).astype(jnp.float32))
    score = jnp.einsum('bqh,bqhl->bql', iw.astype(jnp.float32), rel)
    score = jnp.where(k_pos[None, None, :] <= q_pos[None, :, None], score, -jnp.inf)
    return lax.top_k(score, n_sel)[1]

def dsa_attend(q, k_sel, v_sel, q_pos, idx, rel_bias):
    logit = jnp.einsum('bqhd,bqkhd->bhqk', q, k_sel).astype(jnp.float32) * (HEAD_DIM ** -0.5)
    dist = q_pos[None, :, None] - idx
    bias = jnp.moveaxis(rel_bias[t5_bucket(dist)], -1, 1).astype(jnp.float32)
    logit = jnp.where((dist >= 0)[:, None], logit + bias, -jnp.inf)
    p = jax.nn.softmax(logit, axis=-1)
    return jnp.einsum('bhqk,bqkhd->bqhd', p.astype(v_sel.dtype), v_sel)

def dsa_prompt(q, k, v, iq, iw, ik, rel_bias):
    n_keys = q.shape[1]
    n_sel = min(TOPK_MAX, n_keys // 4)
    k_pos = jnp.arange(n_keys, dtype=jnp.int32)

    def block(args):
        qb, iqb, iwb, qp = args
        idx = indexer_topk(iqb, iwb, ik, qp, k_pos, n_sel)
        return dsa_attend(qb, take_rows(k, idx), take_rows(v, idx), qp, idx, rel_bias)

    return from_blocks(lax.map(block, (to_blocks(q), to_blocks(iq), to_blocks(iw), k_pos.reshape(-1, Q_BLOCK))))

def gather_selected(pool, new_rows, page_table, idx):
    in_past = idx < PAST_LEN
    pidx = jnp.minimum(idx, PAST_LEN - 1)
    phys = jnp.take_along_axis(page_table, (pidx // PAGE_SIZE).reshape(idx.shape[0], -1), axis=1).reshape(idx.shape)
    past_rows = pool[phys, pidx % PAGE_SIZE].astype(new_rows.dtype)
    cur_rows = take_rows(new_rows, jnp.clip(idx - PAST_LEN, 0, new_rows.shape[1] - 1))
    return jnp.where(in_past[..., None, None], past_rows, cur_rows)

def dsa_sample(q, k, v, iq, iw, ik, q_pos, pool_k, pool_v, pool_ik, page_table, rel_bias):
    n_keys = PAST_LEN + q.shape[1]
    n_sel = min(TOPK_MAX, n_keys // 4)
    ik_all = jnp.concatenate([gather_pages(pool_ik, page_table).astype(ik.dtype), ik], axis=1)
    idx = indexer_topk(iq, iw, ik_all, q_pos, jnp.arange(n_keys, dtype=jnp.int32), n_sel)
    k_sel = gather_selected(pool_k, k, page_table, idx)
    v_sel = gather_selected(pool_v, v, page_table, idx)
    return dsa_attend(q, k_sel, v_sel, q_pos, idx, rel_bias)

def conv_ffn(x, g, w_in, conv_w, w_out, buf):
    h = rmsnorm(x, g) @ w_in
    t_len = h.shape[1]
    padded = jnp.concatenate([buf.astype(h.dtype), h], axis=1)
    c = sum(padded[:, i:i + t_len] * conv_w[i] for i in range(CONV_W))
    gate, val = jnp.split(c, 2, axis=-1)
    return (jax.nn.silu(gate) * val) @ w_out, padded[:, t_len:]

def setup_inputs(seed: int = 0) -> dict:
    key = jax.random.key(seed)
    keys = iter(jax.random.split(key, 64))

    def nrm(shape, scale):
        return jax.random.normal(next(keys), shape, jnp.float32) * scale

    def gain(shape):
        return 1.0 + nrm(shape, 0.05)

    n_pages = PAST_LEN // PAGE_SIZE
    n_used = DEC_BATCH * n_pages
    n_pool = n_used + max(n_used // 4, 1)
    page_table = jax.random.permutation(next(keys), n_pool)[:n_used].reshape(DEC_BATCH, n_pages).astype(jnp.int32)
    s5_n = jnp.arange(S5_STATE, dtype=jnp.float32)
    return {
        'x_prompt': nrm((BATCH, SEQ, D_MODEL), 1.0),
        'x_sample': nrm((DEC_BATCH, DEC_SEQ, D_MODEL), 1.0),
        'cache_sb_k': nrm((N_EVEN, n_pool, PAGE_SIZE, SB_HEADS, HEAD_DIM), 1.0),
        'cache_sb_v': nrm((N_EVEN, n_pool, PAGE_SIZE, SB_HEADS, HEAD_DIM), 1.0),
        'cache_dsa_k': nrm((N_ODD, n_pool, PAGE_SIZE, DSA_HEADS, HEAD_DIM), 1.0),
        'cache_dsa_v': nrm((N_ODD, n_pool, PAGE_SIZE, DSA_HEADS, HEAD_DIM), 1.0),
        'cache_dsa_idx_k': nrm((N_ODD, n_pool, PAGE_SIZE, IDX_DIM), 1.0),
        'state_s5_re': nrm((N_EVEN, DEC_BATCH, S5_GROUPS, S5_STATE), 0.5),
        'state_s5_im': nrm((N_EVEN, DEC_BATCH, S5_GROUPS, S5_STATE), 0.5),
        'state_rwkv': nrm((N_ODD, DEC_BATCH, RWKV_HEADS, HEAD_DIM, HEAD_DIM), 0.5),
        'state_rwkv_shift': nrm((N_ODD, DEC_BATCH, RWKV_IN), 1.0),
        'state_ffn_conv': nrm((DEPTH, DEC_BATCH, CONV_W - 1, 2 * D_FF), 1.0),
        'page_table': page_table,
        'rel_bias': nrm((REL_BUCKETS, DSA_HEADS), 0.5),
        'ev_norm_g': gain((N_EVEN, D_MODEL)),
        'ev_w_in': nrm((N_EVEN, D_MODEL, EVEN_IN), D_MODEL ** -0.5),
        'ev_w_out': nrm((N_EVEN, MIX_WIDTH, D_MODEL), MIX_WIDTH ** -0.5),
        's5_lambda_re': -0.5 + nrm((N_EVEN, S5_GROUPS, S5_STATE), 0.01),
        's5_lambda_im': jnp.pi * s5_n + nrm((N_EVEN, S5_GROUPS, S5_STATE), 0.01),
        's5_log_step': jax.random.uniform(next(keys), (N_EVEN, S5_GROUPS), jnp.float32, math.log(1e-3), math.log(1e-1)),
        's5_b_re': nrm((N_EVEN, S5_GROUPS, S5_STATE, S5_GROUP), (2 * S5_GROUP) ** -0.5),
        's5_b_im': nrm((N_EVEN, S5_GROUPS, S5_STATE, S5_GROUP), (2 * S5_GROUP) ** -0.5),
        's5_c_re': nrm((N_EVEN, S5_GROUPS, S5_GROUP, S5_STATE), (2 * S5_STATE) ** -0.5),
        's5_c_im': nrm((N_EVEN, S5_GROUPS, S5_GROUP, S5_STATE), (2 * S5_STATE) ** -0.5),
        's5_d': nrm((N_EVEN, S5_GROUPS, S5_GROUP), 1.0),
        's5_w_glu': nrm((N_EVEN, S5_WIDTH, S5_WIDTH), S5_WIDTH ** -0.5),
        's5_b_glu': nrm((N_EVEN, S5_WIDTH), 0.01),
        'od_norm_g': gain((N_ODD, D_MODEL)),
        'od_w_in': nrm((N_ODD, D_MODEL, ODD_IN), D_MODEL ** -0.5),
        'od_w_out': nrm((N_ODD, MIX_WIDTH, D_MODEL), MIX_WIDTH ** -0.5),
        'rwkv_mu': jax.random.uniform(next(keys), (N_ODD, RWKV_IN), jnp.float32),
        'rwkv_w0': nrm((N_ODD, RWKV_WIDTH), 0.5),
        'rwkv_w2': nrm((N_ODD, RWKV_DECAY_RANK, RWKV_WIDTH), 0.5 * RWKV_DECAY_RANK ** -0.5),
        'rwkv_a0': nrm((N_ODD, RWKV_WIDTH), 0.5),
        'rwkv_a2': nrm((N_ODD, RWKV_A_RANK, RWKV_WIDTH), 0.5 * RWKV_A_RANK ** -0.5),
        'rwkv_g2': nrm((N_ODD, RWKV_GATE_RANK, RWKV_WIDTH), RWKV_GATE_RANK ** -0.5),
        'rwkv_k_k': 0.85 + nrm((N_ODD, RWKV_WIDTH), 0.05),
        'rwkv_k_a': gain((N_ODD, RWKV_WIDTH)),
        'rwkv_r_k': nrm((N_ODD, RWKV_HEADS, HEAD_DIM), 0.1),
        'rwkv_ln_g': gain((N_ODD, RWKV_WIDTH)),
        'rwkv_ln_b': nrm((N_ODD, RWKV_WIDTH), 0.01),
        'dsa_q_norm_g': gain((N_ODD, HEAD_DIM)),
        'dsa_k_norm_g': gain((N_ODD, HEAD_DIM)),
        'ffn_norm_g': gain((DEPTH, D_MODEL)),
        'ffn_w_in': nrm((DEPTH, D_MODEL, 2 * D_FF), D_MODEL ** -0.5),
        'ffn_conv': nrm((DEPTH, CONV_W, 2 * D_FF), CONV_W ** -0.5),
        'ffn_w_out': nrm((DEPTH, D_FF, D_MODEL), D_FF ** -0.5),
    }

def reference(x_prompt, x_sample, cache_sb_k, cache_sb_v, cache_dsa_k, cache_dsa_v, cache_dsa_idx_k,
              state_s5_re, state_s5_im, state_rwkv, state_rwkv_shift, state_ffn_conv, page_table,
              rel_bias, ev_norm_g, ev_w_in, ev_w_out, s5_lambda_re, s5_lambda_im, s5_log_step,
              s5_b_re, s5_b_im, s5_c_re, s5_c_im, s5_d, s5_w_glu, s5_b_glu,
              od_norm_g, od_w_in, od_w_out, rwkv_mu, rwkv_w0, rwkv_w2, rwkv_a0, rwkv_a2, rwkv_g2,
              rwkv_k_k, rwkv_k_a, rwkv_r_k, rwkv_ln_g, rwkv_ln_b, dsa_q_norm_g, dsa_k_norm_g,
              ffn_norm_g, ffn_w_in, ffn_conv, ffn_w_out):

    def run(x, sample):
        bsz, t_len, _ = x.shape
        dt = x.dtype
        q_pos = (PAST_LEN if sample else 0) + jnp.arange(t_len, dtype=jnp.int32)
        new = {n: [] for n in ('sb_k', 'sb_v', 's5_re', 's5_im', 'dsa_k', 'dsa_v', 'dsa_idx',
                               'rwkv', 'rwkv_shift', 'ffn')}
        for i in range(DEPTH):
            j = i // 2
            if i % 2 == 0:
                u, q, k, v = split_cols(rmsnorm(x, ev_norm_g[j]) @ ev_w_in[j],
                                        [S5_WIDTH, SB_WIDTH, SB_WIDTH, SB_WIDTH])
                q = q.reshape(bsz, t_len, SB_HEADS, HEAD_DIM)
                k = k.reshape(bsz, t_len, SB_HEADS, HEAD_DIM)
                v = v.reshape(bsz, t_len, SB_HEADS, HEAD_DIM)
                if sample:
                    h0_re, h0_im = state_s5_re[j].astype(dt), state_s5_im[j].astype(dt)
                else:
                    h0_re = h0_im = jnp.zeros((bsz, S5_GROUPS, S5_STATE), dt)
                a_out, h_re, h_im = s5_mixer(u, h0_re, h0_im, s5_lambda_re[j], s5_lambda_im[j], s5_log_step[j],
                                             s5_b_re[j], s5_b_im[j], s5_c_re[j], s5_c_im[j], s5_d[j],
                                             s5_w_glu[j], s5_b_glu[j])
                if sample:
                    k_all = jnp.concatenate([gather_pages(cache_sb_k[j], page_table).astype(dt), k], axis=1)
                    v_all = jnp.concatenate([gather_pages(cache_sb_v[j], page_table).astype(dt), v], axis=1)
                    b_out = stick_breaking_block(q, k_all, v_all, q_pos,
                                                 jnp.arange(PAST_LEN + t_len, dtype=jnp.int32))
                else:
                    b_out = stick_breaking_prompt(q, k, v)
                mix = jnp.concatenate([a_out, b_out.reshape(bsz, t_len, SB_WIDTH)], axis=-1)
                x = x + mix @ ev_w_out[j]
                new['sb_k'].append(k)
                new['sb_v'].append(v)
                new['s5_re'].append(h_re)
                new['s5_im'].append(h_im)
            else:
                cols, q, k, v, iq, iw, ik = split_cols(
                    rmsnorm(x, od_norm_g[j]) @ od_w_in[j],
                    [RWKV_IN, DSA_WIDTH, DSA_WIDTH, DSA_WIDTH, IDX_HEADS * IDX_DIM, IDX_HEADS, IDX_DIM])
                if sample:
                    shift0, s0 = state_rwkv_shift[j].astype(dt), state_rwkv[j].astype(dt)
                else:
                    shift0 = jnp.zeros((bsz, RWKV_IN), dt)
                    s0 = jnp.zeros((bsz, RWKV_HEADS, HEAD_DIM, HEAD_DIM), dt)
                c_out, shift_new, s_new = rwkv7_mixer(cols, shift0, s0, rwkv_mu[j], rwkv_w0[j], rwkv_w2[j],
                                                      rwkv_a0[j], rwkv_a2[j], rwkv_g2[j], rwkv_k_k[j],
                                                      rwkv_k_a[j], rwkv_r_k[j], rwkv_ln_g[j], rwkv_ln_b[j])
                q = rmsnorm(q.reshape(bsz, t_len, DSA_HEADS, HEAD_DIM), dsa_q_norm_g[j])
                k = rmsnorm(k.reshape(bsz, t_len, DSA_HEADS, HEAD_DIM), dsa_k_norm_g[j])
                v = v.reshape(bsz, t_len, DSA_HEADS, HEAD_DIM)
                iq = iq.reshape(bsz, t_len, IDX_HEADS, IDX_DIM)
                if sample:
                    d_out = dsa_sample(q, k, v, iq, iw, ik, q_pos, cache_dsa_k[j], cache_dsa_v[j],
                                       cache_dsa_idx_k[j], page_table, rel_bias)
                else:
                    d_out = dsa_prompt(q, k, v, iq, iw, ik, rel_bias)
                mix = jnp.concatenate([c_out, d_out.reshape(bsz, t_len, DSA_WIDTH)], axis=-1)
                x = x + mix @ od_w_out[j]
                new['dsa_k'].append(k)
                new['dsa_v'].append(v)
                new['dsa_idx'].append(ik)
                new['rwkv'].append(s_new)
                new['rwkv_shift'].append(shift_new)
            buf = state_ffn_conv[i] if sample else jnp.zeros((bsz, CONV_W - 1, 2 * D_FF), dt)
            f, buf_new = conv_ffn(x, ffn_norm_g[i], ffn_w_in[i], ffn_conv[i], ffn_w_out[i], buf)
            x = x + f
            new['ffn'].append(buf_new)
        return x, {n: jnp.stack(l) for n, l in new.items()}

    y_prompt, st_p = run(x_prompt, False)
    y_sample, st_s = run(x_sample, True)
    return (y_prompt, y_sample,
            st_p['sb_k'], st_p['sb_v'], st_s['sb_k'], st_s['sb_v'],
            st_p['dsa_k'], st_p['dsa_v'], st_p['dsa_idx'], st_s['dsa_k'], st_s['dsa_v'], st_s['dsa_idx'],
            st_p['s5_re'], st_p['s5_im'], st_s['s5_re'], st_s['s5_im'],
            st_p['rwkv'], st_p['rwkv_shift'], st_s['rwkv'], st_s['rwkv_shift'],
            st_p['ffn'], st_s['ffn'])


_drawn_inputs = setup_inputs


def setup_inputs(seed=0):
    import zlib

    import numpy as np

    out = dict(_drawn_inputs(seed))
    spreads = {}
    factors = {'s5_lambda_re': 16.171,
     's5_b_glu': 8.0,
     'rwkv_k_k': 20.886,
     'rwkv_ln_g': 3.515,
     'rwkv_ln_b': 26.308,
     'dsa_q_norm_g': 8.0}
    for name, (base, spread) in spreads.items():
        noise = np.random.default_rng([zlib.crc32(name.encode()), seed]).standard_normal(out[name].shape)
        drawn = base * np.exp(spread * noise) if base else spread * noise
        out[name] = __import__('jax').numpy.asarray(drawn.astype(out[name].dtype))
    for name, factor in factors.items():
        out[name] = (out[name] * factor).astype(out[name].dtype)
    return out
```

```python
import math
from contextlib import ExitStack

import numpy as np
import concourse.bass as bass
from concourse import mybir

ALU = mybir.AluOpType
ACT = mybir.ActivationFunctionType
AX_X = mybir.AxisListType.X
F32 = mybir.dt.float32
I32 = mybir.dt.int32

P = 128
D_MODEL = 1024
SEQ = 1024
DEC_BATCH = 8
DEC_SEQ = 4
NS = DEC_BATCH * DEC_SEQ
PAST_LEN = 1024
PAGE = 128
N_PAGES = PAST_LEN // PAGE
HEADS = 8
HEAD_DIM = 64
HALF = D_MODEL // 2
TOK = SEQ + NS
PT = SEQ // P
TT = PT + 1
KT = D_MODEL // P
EVEN_IN = 4 * HALF
RWKV_IN = 3 * HALF + 64 + 64 + 128
IDX_HEADS = 8
IDX_DIM = 32
ODD_IN = RWKV_IN + 3 * HALF + IDX_HEADS * IDX_DIM + IDX_HEADS + IDX_DIM
D_FF = 2816
FT = D_FF // P
TOPK = 256
RMS_EPS = 1e-6
NC_COLS = 512
SCALE = HEAD_DIM ** -0.5


def rows_of(t):
    return P if t < PT else NS


def at_least(eng, sem, value):
    if not isinstance(value, int) or value > 0:
        eng.wait_ge(sem, value)


class Phase:

    def __init__(self, nc, name):
        self.nc, self.name, self.ctx = nc, name, ExitStack()

    def __enter__(self):
        self.ctx.__enter__()
        return self

    def __exit__(self, *e):
        return self.ctx.__exit__(*e)

    def sb(self, name, shape, dt=F32):
        return self.ctx.enter_context(self.nc.sbuf_tensor(f"{self.name}_{name}", shape, dt))

    def ps(self, name, shape, dt=F32):
        return self.ctx.enter_context(self.nc.psum_tensor(f"{self.name}_{name}", shape, dt))

    def sem(self, name):
        return self.nc.alloc_semaphore(name=f"{self.name}_{name}")

    def block(self):
        return self.ctx.enter_context(self.nc.Block())


class Chain:

    def __init__(self, eng, sem):
        self.eng, self.sem, self.n = eng, sem, 0

    def __call__(self, ins):
        self.n += 1
        ins.then_inc(self.sem, 1)
        self.eng.wait_ge(self.sem, self.n)


def token_rows(prompt, sample, t):
    return prompt[t * P:(t + 1) * P, :] if t < PT else sample[:, :]


def normed_transpose(nc, ph, src, gain, xT, ident, ident_src, xT_ready, norm=True, spare=None):
    if spare is None:
        spare = ph.sb("norm_rows", [P, 5, D_MODEL])
    xin, xn, sq = spare[:, 0:2, 0:D_MODEL], spare[:, 2:4, 0:D_MODEL], spare[:, 4, 0:D_MODEL]
    stat = ph.sb("stat", [P, TT, 4])
    gain_b = ph.sb("gain_b", [P, D_MODEL])
    epsc = ph.sb("epsc", [P, 1])
    trp = ph.ps("trp", [P, 2, NC_COLS])
    const_ld = ph.sem("const_ld")
    x_ld = [ph.sem(f"x_ld{i}") for i in range(2)]
    ss_ready = ph.sem("ss_ready")
    root_ready = ph.sem("root_ready")
    inv_ready = ph.sem("inv_ready")
    xn_ready = ph.sem("xn_ready")
    tr_ready = ph.sem("tr_ready")
    eps_set = ph.sem("eps_set")

    def sync_part(sp):
        sp.dma_start(ident[:, :], ident_src).then_inc(const_ld, 16)
        if norm:
            sp.dma_start(gain_b[:, :], gain.broadcast_to([P, D_MODEL])).then_inc(const_ld, 16)
        for t in range(TT):
            if t >= 2:
                if norm:
                    sp.wait_ge(xn_ready, t - 1)
                else:
                    sp.wait_ge(tr_ready, 2 * (t - 1))
            sp.dma_start(xin[0:rows_of(t), t % 2, :], src(t)).then_inc(x_ld[t % 2], 16)

    def scalar_part(act):
        if not norm:
            return
        act.wait_ge(eps_set, 1)
        for t in range(TT):
            r = rows_of(t)
            act.wait_ge(x_ld[t % 2], 16 * (t // 2 + 1))
            at_least(act, ss_ready, t)
            nc.scalar.activation(sq[0:r, :], xin[0:r, t % 2, :], ACT.Square,
                                 accum_out=stat[0:r, t, 0:1]).then_inc(ss_ready, 1)
            act.wait_ge(ss_ready, t + 1)
            nc.scalar.activation(stat[0:r, t, 1:2], stat[0:r, t, 0:1], ACT.Sqrt, bias=epsc[0:r, :],
                                 scale=1.0 / D_MODEL).then_inc(root_ready, 1)

    def vector_part(dve):
        if norm:
            nc.vector.memset(epsc[:, :], RMS_EPS).then_inc(eps_set, 1)
        dve.wait_ge(const_ld, 32 if norm else 16)
        for t in range(TT):
            r = rows_of(t)
            if norm:
                dve.wait_ge(root_ready, t + 1)
                nc.vector.reciprocal(stat[0:r, t, 2:3], stat[0:r, t, 1:2]).then_inc(inv_ready, 1)
                dve.wait_ge(inv_ready, t + 1)
                if t >= 2:
                    dve.wait_ge(tr_ready, 2 * (t - 1))
                nc.vector.scalar_tensor_tensor(xn[0:r, t % 2, :], xin[0:r, t % 2, :], stat[0:r, t, 2:3],
                                               gain_b[0:r, :], ALU.mult, ALU.mult).then_inc(xn_ready, 1)
            for h in range(2):
                dve.wait_ge(tr_ready, 2 * t + h + 1)
                nc.vector.tensor_copy(xT[:, 4 * h:4 * h + 4, t * P:t * P + r],
                                      trp[:, h, :].rearrange("p (k c) -> p k c", c=P)[:, :, 0:r]).then_inc(xT_ready, 1)

    def tensor_part(pe):
        xs = xn if norm else xin
        pe.wait_ge(const_ld, 32 if norm else 16)
        for t in range(TT):
            r = rows_of(t)
            if norm:
                pe.wait_ge(xn_ready, t + 1)
            else:
                pe.wait_ge(x_ld[t % 2], 16 * (t // 2 + 1))
            for h in range(2):
                at_least(pe, xT_ready, 2 * (t - 1) + h + 1)
                for k in range(4):
                    last = nc.tensor.transpose(trp[:, h, k * P:k * P + r],
                                               xs[0:r, t % 2, (4 * h + k) * P:(4 * h + k + 1) * P], ident[0:r, 0:r])
                last.then_inc(tr_ready, 1)

    return sync_part, scalar_part, vector_part, tensor_part


def project(nc, name, src, gain, weight, n_cols, dst, ident_src, resid=None, norm=True):
    full = n_cols // NC_COLS
    rest = n_cols - full * NC_COLS
    NB = 3
    with Phase(nc, name) as ph:
        xT = ph.sb("xT", [P, KT, TOK])
        w = ph.sb("w", [P, 2, KT, NC_COLS])
        stage = ph.sb("stage", [P, NB, NC_COLS])
        res = ph.sb("res", [P, NB, NC_COLS]) if resid else None
        acc = ph.ps("acc", [P, NB, NC_COLS])
        xT_ready = ph.sem("xT_ready")
        w_ld = [ph.sem(f"w_ld{i}") for i in range(2)]
        mm_done = ph.sem("mm_done")
        ev_done = ph.sem("ev_done")
        st_done = [ph.sem(f"st_done{i}") for i in range(NB)]
        r_ld = [ph.sem(f"r_ld{i}") for i in range(NB)]
        ident = ph.sb("ident", [P, P])
        t_sync, t_scalar, t_vector, t_tensor = normed_transpose(
            nc, ph, src, gain, xT, ident, ident_src, xT_ready, norm)
        w_view = weight[:, 0:full * NC_COLS].rearrange("(k p) (c n) -> c p k n", p=P, n=NC_COLS)
        loop_end = full - full % 2
        tail = [(c, NC_COLS) for c in range(loop_end, full)] + ([(full, rest)] if rest else [])
        steps = full * TT + (TT if rest else 0)
        block = ph.block()

        def load_chunk(eng, c, s, width):
            at_least(eng, mm_done, (c - 1) * TT)
            src_w = w_view[c] if width == NC_COLS else \
                weight[:, full * NC_COLS:n_cols].rearrange("(k p) n -> p k n", p=P)
            eng.dma_start(w[:, s, :, 0:width], src_w).then_inc(w_ld[s], 16)

        @block.gpsimd
        def _(pool):
            load_chunk(pool, 0, 0, NC_COLS)
            load_chunk(pool, 1, 1, NC_COLS)
            if loop_end > 2:
                with pool.Fori(1, loop_end // 2) as i:
                    load_chunk(pool, i * 2, 0, NC_COLS)
                    load_chunk(pool, i * 2 + 1, 1, NC_COLS)
            for c, width in tail:
                load_chunk(pool, c, c % 2, width)

        def store_chunk(eng, c, width):
            for t in range(TT):
                eng.wait_ge(ev_done, c * TT + t + 1)
                eng.dma_start(dst(t, c, width), stage[0:rows_of(t), t % NB, 0:width]).then_inc(st_done[t % NB], 16)

        @block.sync
        def _(sp):
            t_sync(sp)
            if resid:
                for t in range(NB):
                    sp.dma_start(res[0:rows_of(t), t, :], resid(t, 0)).then_inc(r_ld[t], 16)
                for n in range(full * TT):
                    c, t = n // TT, n % TT
                    sp.wait_ge(ev_done, n + 1)
                    sp.dma_start(dst(t, c, NC_COLS), stage[0:rows_of(t), t % NB, :]).then_inc(st_done[t % NB], 16)
                    if n + NB < full * TT:
                        c2, t2 = (n + NB) // TT, (n + NB) % TT
                        sp.dma_start(res[0:rows_of(t2), t2 % NB, :], resid(t2, c2)).then_inc(r_ld[t2 % NB], 16)
            else:
                store_chunk(sp, 0, NC_COLS)
                store_chunk(sp, 1, NC_COLS)
                if loop_end > 2:
                    with sp.Fori(2, loop_end) as c:
                        store_chunk(sp, c, NC_COLS)
                for c, width in tail:
                    store_chunk(sp, c, width)
            for b in range(NB):
                sp.wait_ge(st_done[b], 16 * (steps // NB))

        def evacuate(act, c, width):
            for t in range(TT):
                r = rows_of(t)
                act.wait_ge(mm_done, c * TT + t + 1)
                if not isinstance(c, int) or c > 0 or t >= NB:
                    act.wait_ge(st_done[t % NB], (c * (TT // NB) + t // NB) * 16)
                nc.scalar.activation(stage[0:r, t % NB, 0:width], acc[0:r, t % NB, 0:width],
                                     ACT.Copy).then_inc(ev_done, 1)

        @block.scalar
        def _(act):
            t_scalar(act)
            if resid:
                return
            evacuate(act, 0, NC_COLS)
            evacuate(act, 1, NC_COLS)
            if loop_end > 2:
                with act.Fori(2, loop_end) as c:
                    evacuate(act, c, NC_COLS)
            for c, width in tail:
                evacuate(act, c, width)

        @block.vector
        def _(dve):
            t_vector(dve)
            if not resid:
                return
            for n in range(full * TT):
                t = n % TT
                r = rows_of(t)
                dve.wait_ge(mm_done, n + 1)
                dve.wait_ge(r_ld[t % NB], 16 * (n // NB + 1))
                at_least(dve, st_done[t % NB], 16 * (n // NB))
                nc.vector.tensor_tensor(stage[0:r, t % NB, :], acc[0:r, t % NB, :], res[0:r, t % NB, :],
                                        ALU.add).then_inc(ev_done, 1)

        def products(pe, c, s, width):
            if isinstance(c, int):
                pe.wait_ge(w_ld[s], 16 * (c // 2 + 1))
            else:
                pe.wait_ge(w_ld[s], (c - s) * 8 + 16)
            for t in range(TT):
                r = rows_of(t)
                at_least(pe, ev_done, c * TT + t + 1 - NB)
                for k in range(KT):
                    last = nc.tensor.matmul(acc[0:r, t % NB, 0:width], xT[:, k, t * P:t * P + r],
                                            w[:, s, k, 0:width], start=(k == 0), stop=(k == KT - 1))
                last.then_inc(mm_done, 1)

        @block.tensor
        def _(pe):
            t_tensor(pe)
            pe.wait_ge(xT_ready, 2 * TT)
            products(pe, 0, 0, NC_COLS)
            products(pe, 1, 1, NC_COLS)
            if loop_end > 2:
                with pe.Fori(1, loop_end // 2) as i:
                    products(pe, i * 2, 0, NC_COLS)
                    products(pe, i * 2 + 1, 1, NC_COLS)
            for c, width in tail:
                products(pe, c, c % 2, width)


def conv_ffn(nc, name, src, gain, w_in, conv_w, w_out, state, dst, tails, ident_src):
    GB = SEQ + 2
    SB = 2 + DEC_SEQ
    PADDED = GB + DEC_BATCH * SB
    TAPPED = PADDED - 2
    NR = 2 * DEC_BATCH + 3
    NT = 2 + 2 * DEC_BATCH
    with Phase(nc, name + "_act") as outer:
        actT = outer.sb("actT", [P, FT, TOK])
        with Phase(nc, name + "_up") as ph:
            xT = ph.sb("xT", [P, KT, TOK])
            w = ph.sb("w", [P, 2, 2, KT, P])
            rows = ph.sb("rows", [32, 2 * D_FF])
            cols = ph.sb("cols", [P, 2 * FT, NR])
            tail = ph.sb("tail", [P, 2 * FT, NT])
            hb = ph.sb("hb", [P, 2, 2, PADDED])
            cb = ph.sb("cb", [P, 2, PADDED])
            sg = ph.sb("sg", [P, PADDED])
            hp = ph.ps("hp", [P, 2, 3, NC_COLS])
            xT_ready = ph.sem("xT_ready")
            rows_ld = ph.sem("rows_ld")
            cols_tr = ph.sem("cols_tr")
            cols_ready = ph.sem("cols_ready")
            w_ld = [ph.sem(f"w_ld{i}") for i in range(2)]
            mm_done = [ph.sem("gate_mm"), ph.sem("value_mm")]
            ev_done = [ph.sem("gate_ev"), ph.sem("value_ev")]
            conv_done = [ph.sem("gate_conv"), ph.sem("value_conv")]
            silu_done = ph.sem("silu_done")
            act_done = ph.sem("act_done")
            pad_set = ph.sem("pad_set")
            dve_own = ph.sem("dve_own")
            tail_tr = ph.sem("tail_tr")
            tail_ready = ph.sem("tail_ready")
            tail_st = ph.sem("tail_st")
            ident = ph.sb("ident", [P, P])
            t_sync, t_scalar, t_vector, t_tensor = normed_transpose(
                nc, ph, src, gain, xT, ident, ident_src, xT_ready, spare=actT)
            w_view = w_in.rearrange("(k p) (f n) -> f p k n", p=P, n=P)
            block = ph.block()

            def load_pair(eng, j, s):
                at_least(eng, mm_done[1], j - 1)
                for q in range(2):
                    eng.dma_start(w[:, s, q, :, :], w_view[j + q * FT]).then_inc(w_ld[s], 16)

            @block.gpsimd
            def _(pool):
                load_pair(pool, 0, 0)
                load_pair(pool, 1, 1)
                with pool.Fori(1, FT // 2) as i:
                    load_pair(pool, i * 2, 0)
                    load_pair(pool, i * 2 + 1, 1)

            @block.sync
            def _(sp):
                sp.dma_start(rows[0:2 * DEC_BATCH, :], state).then_inc(rows_ld, 16)
                sp.dma_start(rows[2 * DEC_BATCH:NR, :], conv_w).then_inc(rows_ld, 16)
                t_sync(sp)
                sp.wait_ge(tail_ready, 11)
                for dram, r0, r1 in tails:
                    sp.dma_start(dram, rows[r0:r1, :]).then_inc(tail_st, 16)
                sp.wait_ge(tail_st, 16 * len(tails))

            def up(pe, j, s):
                pe.wait_ge(w_ld[s], (j - s) * 16 + 32)
                for q in range(2):
                    at_least(pe, ev_done[q], j * 3)
                    for b, (c0, n) in enumerate([(0, NC_COLS), (NC_COLS, NC_COLS), (SEQ, NS)]):
                        for k in range(KT):
                            last = nc.tensor.matmul(hp[:, q, b, 0:n], w[:, s, q, k, :], xT[:, k, c0:c0 + n],
                                                    start=(k == 0), stop=(k == KT - 1))
                    last.then_inc(mm_done[q], 1)

            @block.tensor
            def _(pe):
                pe.wait_ge(rows_ld, 32)
                t_tensor(pe)
                for f in range(2 * FT):
                    h, c = f // FT, f % FT
                    last = nc.tensor.transpose(hp[:, h, 0, c * NR:(c + 1) * NR], rows[0:NR, f * P:(f + 1) * P],
                                               ident[0:NR, 0:NR])
                last.then_inc(cols_tr, 1)
                pe.wait_ge(cols_ready, 2)
                pe.wait_ge(xT_ready, 2 * TT)
                up(pe, 0, 0)
                up(pe, 1, 1)
                with pe.Fori(1, FT // 2) as i:
                    up(pe, i * 2, 0)
                    up(pe, i * 2 + 1, 1)
                pe.wait_ge(act_done, FT)
                for g in range(11):
                    at_least(pe, tail_ready, g - 5)
                    for f in range(4):
                        last = nc.tensor.transpose(hp[0:NT, g % 6 // 3, g % 3, f * P:(f + 1) * P],
                                                   tail[:, 4 * g + f, :], ident[:, :])
                    last.then_inc(tail_tr, 1)

            def evacuate(act, j, s):
                for q in range(2):
                    act.wait_ge(mm_done[q], j + 1)
                    if not isinstance(j, int) or j >= 2:
                        act.wait_ge(conv_done[q], j - 1)
                    for b in range(2):
                        nc.scalar.activation(hb[:, q, s, 2 + b * NC_COLS:2 + (b + 1) * NC_COLS], hp[:, q, b, :],
                                             ACT.Copy).then_inc(ev_done[q], 1)
                    new = hb[:, q, s, GB:PADDED].rearrange("p (b r) -> p b r", r=SB)[:, :, 2:SB]
                    nc.scalar.activation(new, hp[:, q, 2, 0:NS].rearrange("p (b r) -> p b r", r=DEC_SEQ),
                                         ACT.Copy).then_inc(ev_done[q], 1)
                act.wait_ge(conv_done[0], j + 1)
                at_least(act, act_done, j)
                nc.scalar.activation(sg[:, 0:TAPPED], cb[:, 0, 0:TAPPED], ACT.Silu).then_inc(silu_done, 1)

            @block.scalar
            def _(act):
                t_scalar(act)
                evacuate(act, 0, 0)
                evacuate(act, 1, 1)
                with act.Fori(1, FT // 2) as i:
                    evacuate(act, i * 2, 0)
                    evacuate(act, i * 2 + 1, 1)

            OWN = 6

            def combine(dve, j, s):
                for q in range(2):
                    f = j + q * FT
                    kept = hb[:, q, s, GB:PADDED].rearrange("p (b r) -> p b r", r=SB)
                    dve.wait_ge(ev_done[q], j * 3 + 3)
                    nc.vector.tensor_copy(kept[:, :, 0:2], cols[:, f, 0:2 * DEC_BATCH]
                                          .rearrange("p (b r) -> p b r", r=2)).then_inc(dve_own, 1)
                    dve.wait_ge(dve_own, j * OWN + 3 * q + 1)
                    nc.vector.tensor_copy(tail[:, f, 0:2], hb[:, q, s, SEQ:SEQ + 2])
                    nc.vector.tensor_copy(tail[:, f, 2:NT].rearrange("p (b r) -> p b r", r=2), kept[:, :, DEC_SEQ:SB])
                    if q == 0:
                        at_least(dve, silu_done, j)
                    tap = [cols[:, f, 2 * DEC_BATCH + i:2 * DEC_BATCH + i + 1] for i in range(3)]
                    nc.vector.tensor_scalar(cb[:, q, 0:TAPPED], hb[:, q, s, 0:TAPPED], tap[0], None,
                                            ALU.mult).then_inc(dve_own, 1)
                    dve.wait_ge(dve_own, j * OWN + 3 * q + 2)
                    nc.vector.scalar_tensor_tensor(cb[:, q, 0:TAPPED], hb[:, q, s, 1:1 + TAPPED], tap[1], cb[:, q, 0:TAPPED],
                                                   ALU.mult, ALU.add).then_inc(dve_own, 1)
                    dve.wait_ge(dve_own, j * OWN + 3 * q + 3)
                    nc.vector.scalar_tensor_tensor(cb[:, q, 0:TAPPED], hb[:, q, s, 2:2 + TAPPED], tap[2], cb[:, q, 0:TAPPED],
                                                   ALU.mult, ALU.add).then_inc(conv_done[q], 1)
                dve.wait_ge(silu_done, j + 1)
                dve.wait_ge(conv_done[1], j + 1)
                grp = [x.rearrange("p (b r) -> p b r", r=SB)[:, :, 0:DEC_SEQ] for x in
                       (sg[:, GB:PADDED], cb[:, 1, GB:PADDED])]
                nc.vector.tensor_tensor(actT[:, j, 0:SEQ], sg[:, 0:SEQ], cb[:, 1, 0:SEQ], ALU.mult)
                nc.vector.tensor_tensor(actT[:, j, SEQ:TOK].rearrange("p (b r) -> p b r", r=DEC_SEQ), grp[0], grp[1],
                                        ALU.mult).then_inc(act_done, 1)

            @block.vector
            def _(dve):
                for q in range(2):
                    for s in range(2):
                        last = nc.vector.memset(hb[:, q, s, 0:2], 0.0)
                last.then_inc(pad_set, 1)
                t_vector(dve)
                dve.wait_ge(pad_set, 1)
                dve.wait_ge(cols_tr, 1)
                for h in range(2):
                    nc.vector.tensor_copy(cols[:, h * FT:(h + 1) * FT, :],
                                          hp[:, h, 0, 0:FT * NR].rearrange("p (f r) -> p f r", r=NR)
                                          ).then_inc(cols_ready, 1)
                dve.wait_ge(cols_ready, 2)
                combine(dve, 0, 0)
                combine(dve, 1, 1)
                with dve.Fori(1, FT // 2) as i:
                    combine(dve, i * 2, 0)
                    combine(dve, i * 2 + 1, 1)
                for g in range(11):
                    dve.wait_ge(tail_tr, g + 1)
                    nc.vector.tensor_copy(rows[0:NT, g * NC_COLS:(g + 1) * NC_COLS],
                                          hp[0:NT, g % 6 // 3, g % 3, :]).then_inc(tail_ready, 1)

        NB = 3
        NCH = D_MODEL // NC_COLS
        with Phase(nc, name + "_down") as ph:
            w2 = ph.sb("w2", [P, NCH, FT, NC_COLS])
            stage = ph.sb("stage", [P, NB, NC_COLS])
            res = ph.sb("res", [P, NB, NC_COLS])
            acc = ph.ps("acc", [P, NB, NC_COLS])
            w_ld = [[ph.sem(f"w_ld{c}_{i}") for i in range(2)] for c in range(NCH)]
            mm_done = ph.sem("mm_done")
            ev_done = ph.sem("ev_done")
            st_done = [ph.sem(f"st_done{i}") for i in range(NB)]
            r_ld = [ph.sem(f"r_ld{i}") for i in range(NB)]
            block = ph.block()
            groups = [(c, t) for c in range(NCH) for t in range(TT)]

            @block.gpsimd
            def _(pool):
                v = w_out.rearrange("(k p) (c n) -> c p k n", p=P, n=NC_COLS)
                for c in range(NCH):
                    for i in range(2):
                        k0, k1 = i * FT // 2, (i + 1) * FT // 2
                        pool.dma_start(w2[:, c, k0:k1, :], v[c, :, k0:k1, :]).then_inc(w_ld[c][i], 16)

            @block.sync
            def _(sp):
                def load_res(n):
                    c, t = groups[n]
                    sp.dma_start(res[0:rows_of(t), n % NB, :],
                                 src(t)[:, c * NC_COLS:(c + 1) * NC_COLS]).then_inc(r_ld[n % NB], 16)
                for n in range(NB):
                    load_res(n)
                for n, (c, t) in enumerate(groups):
                    sp.wait_ge(ev_done, n + 1)
                    sp.dma_start(dst(t)[:, c * NC_COLS:(c + 1) * NC_COLS],
                                 stage[0:rows_of(t), n % NB, :]).then_inc(st_done[n % NB], 16)
                    if n + NB < len(groups):
                        load_res(n + NB)
                for b in range(NB):
                    sp.wait_ge(st_done[b], 16 * len(groups) // NB)

            @block.tensor
            def _(pe):
                for n, (c, t) in enumerate(groups):
                    r = rows_of(t)
                    at_least(pe, ev_done, n + 1 - NB)
                    for k in range(FT):
                        if t == 0 and k % (FT // 2) == 0:
                            pe.wait_ge(w_ld[c][k // (FT // 2)], 16)
                        last = nc.tensor.matmul(acc[0:r, n % NB, :], actT[:, k, t * P:t * P + r], w2[:, c, k, :],
                                                start=(k == 0), stop=(k == FT - 1))
                    last.then_inc(mm_done, 1)

            @block.vector
            def _(dve):
                for n, (c, t) in enumerate(groups):
                    r = rows_of(t)
                    dve.wait_ge(mm_done, n + 1)
                    dve.wait_ge(r_ld[n % NB], 16 * (n // NB + 1))
                    at_least(dve, st_done[n % NB], 16 * (n // NB))
                    nc.vector.tensor_tensor(stage[0:r, n % NB, :], acc[0:r, n % NB, :], res[0:r, n % NB, :],
                                            ALU.add).then_inc(ev_done, 1)


S5_GROUPS = 32
S5_GROUP = 16
S5_STATE = 64
S5_STEPS = 8
S5_PAIRS = S5_GROUPS // 2
S5_CHUNKS = SEQ // S5_STEPS
PI = float(np.pi)


def wide(ap, shape):
    return ap.broadcast_to(shape)


def complex_product(nc, link, out_re, out_im, a_re, a_im, b_re, b_im, t1, t2, conj=False):
    link(nc.vector.tensor_tensor(t1, a_re, b_re, ALU.mult))
    link(nc.vector.tensor_tensor(t2, a_im, b_im, ALU.mult))
    link(nc.vector.tensor_tensor(out_re, t1, t2, ALU.add if conj else ALU.subtract))
    link(nc.vector.tensor_tensor(t1, a_re, b_im, ALU.mult))
    link(nc.vector.tensor_tensor(t2, a_im, b_re, ALU.mult))
    link(nc.vector.tensor_tensor(out_im, t1, t2, ALU.subtract if conj else ALU.add))


def s5(nc, A, proj, mix):
    NPW = 3 * S5_PAIRS
    J = S5_STEPS * S5_GROUP
    NK = S5_CHUNKS + 1
    NCOL = S5_CHUNKS + 2 * DEC_BATCH
    with Phase(nc, "s5") as keep:
        ident = keep.sb("ident", [P, P])
        Tm = keep.sb("T", [P, S5_GROUPS, J])
        WE = [keep.sb(f"WE{i}", [P, S5_PAIRS, P]) for i in range(2)]
        G = [keep.sb(f"G{i}", [P, S5_PAIRS, J]) for i in range(2)]
        R = [keep.sb(f"R{i}", [P, S5_PAIRS, NK]) for i in range(2)]
        pw = [keep.sb(f"pw{i}", [P, NPW, S5_STEPS]) for i in range(2)]
        rho = keep.sb("rho", [P, S5_PAIRS])
        with Phase(nc, "s5_setup") as ph:
            lam = ph.sb("lam", [P, 2, S5_PAIRS])
            step = ph.sb("step", [P, S5_PAIRS])
            m = ph.sb("m", [P, 24, S5_PAIRS])
            B = ph.sb("B", [P, 2, S5_PAIRS, S5_GROUP])
            bb = ph.sb("bb", [P, 2, S5_PAIRS, S5_GROUP])
            c_rows = ph.sb("c_rows", [P, 2, 4, 2, S5_STATE])
            CT = ph.sb("CT", [P, 2, S5_PAIRS, S5_GROUP])
            Bn = [ph.sb(f"Bn{i}", [P, S5_PAIRS, J]) for i in range(2)]
            t1 = ph.sb("t1", [P, S5_PAIRS * J])
            t2 = ph.sb("t2", [P, S5_PAIRS * J])
            dcol = ph.sb("dcol", [P, S5_GROUPS])
            bmask = ph.sb("bmask", [P, J])
            pst = ph.ps("pst", [P, 4, NC_COLS])
            ld = ph.sem("ld")
            own = ph.sem("own")
            angles = ph.sem("angles")
            sines = ph.sem("sines")
            exps = ph.sem("exps")
            c_tr = ph.sem("c_tr")
            ct_ready = ph.sem("ct_ready")
            maps_ready = ph.sem("maps_ready")
            bank_full = ph.sem("bank_full")
            bank_free = ph.sem("bank_free")
            masked = ph.sem("masked")
            block = ph.block()
            n_ld = 16 * (2 + 2 + 2 + 8 + S5_STEPS + 2)

            @block.sync
            def _(sp):
                for i, nm in enumerate(["s5_lambda_re", "s5_lambda_im"]):
                    sp.dma_start(lam[:, i, :], A[nm][0].rearrange("(i g) p -> (g p) i", g=2),
                                 allow_slow_non_contiguous=True).then_inc(ld, 16)
                for g in range(2):
                    sp.dma_start(step[g * 64:(g + 1) * 64, :],
                                 A["s5_log_step"].rearrange("a (i g) -> g a i", g=2)[g]
                                 .broadcast_to([64, S5_PAIRS]),
                                 allow_slow_non_contiguous=True).then_inc(ld, 16)
                for i, nm in enumerate(["s5_b_re", "s5_b_im"]):
                    sp.dma_start(B[:, i, :, :], A[nm][0].rearrange("(i g) p c -> (g p) i c", g=2)).then_inc(ld, 16)
                for i, nm in enumerate(["s5_c_re", "s5_c_im"]):
                    for dup in range(2):
                        for h in range(2):
                            sp.dma_start(c_rows[:, i, 2 * h:2 * h + 2, dup, :],
                                         A[nm][0].rearrange("(m g) c p -> (g c) m p", g=8)[:, 2 * h:2 * h + 2, :]
                                         ).then_inc(ld, 16)
                for s in range(S5_STEPS):
                    sp.dma_start(dcol[s * S5_GROUP:(s + 1) * S5_GROUP, :],
                                 A["s5_d"][0].rearrange("g c -> c g"),
                                 allow_slow_non_contiguous=True).then_inc(ld, 16)
                sp.dma_start(ident[:, :], A["c_ident"]).then_inc(ld, 16)
                sp.dma_start(bmask[:, :], A["c_block_mask"]).then_inc(ld, 16)

            @block.scalar
            def _(act):
                act.wait_ge(ld, n_ld)
                nc.scalar.activation(m[:, 0, :], step[:, :], ACT.Exp).then_inc(exps, 1)
                act.wait_ge(angles, 1)
                nc.scalar.activation(m[:, 2, :], m[:, 1, :], ACT.Exp).then_inc(exps, 1)
                act.wait_ge(angles, 2)
                nc.scalar.activation(m[:, 8, :], m[:, 6, :], ACT.Sin).then_inc(sines, 1)
                nc.scalar.activation(m[:, 9, :], m[:, 7, :], ACT.Sin).then_inc(sines, 1)

            @block.vector
            def _(dve):
                link = Chain(dve, own)
                tt = nc.vector.tensor_tensor
                tsc = nc.vector.tensor_scalar
                dve.wait_ge(ld, n_ld)
                dve.wait_ge(exps, 1)
                tt(m[:, 1, :], lam[:, 0, :], m[:, 0, :], ALU.mult).then_inc(angles, 1)
                link(tt(m[:, 3, :], lam[:, 1, :], m[:, 0, :], ALU.mult))
                two_pi_hi = float(np.float32(6.28125))
                two_pi_lo = 2 * PI - two_pi_hi
                link(tsc(m[:, 4, :], m[:, 3, :], 1 / (2 * PI), None, ALU.mult))
                link(tsc(m[:, 5, :], m[:, 4, :], 12582912.0, None, ALU.add))
                link(tsc(m[:, 4, :], m[:, 5, :], -12582912.0, None, ALU.add))
                link(nc.vector.scalar_tensor_tensor(m[:, 5, :], m[:, 4, :], -two_pi_hi, m[:, 3, :], ALU.mult, ALU.add))
                link(nc.vector.scalar_tensor_tensor(m[:, 10, :], m[:, 4, :], -two_pi_lo, m[:, 5, :], ALU.mult, ALU.add))
                link(tsc(m[:, 6, :], m[:, 10, :], 3.1415925, -3.1415925, ALU.min, ALU.max))
                link(tsc(m[:, 11, :], m[:, 10, :], PI / 2, None, ALU.add))
                link(tsc(m[:, 12, :], m[:, 11, :], PI, -2 * PI, ALU.is_gt, ALU.mult))
                link(tt(m[:, 13, :], m[:, 11, :], m[:, 12, :], ALU.add))
                tsc(m[:, 7, :], m[:, 13, :], 3.1415925, -3.1415925, ALU.min, ALU.max).then_inc(angles, 1)
                dve.wait_ge(exps, 2)
                dve.wait_ge(sines, 2)
                sin, cos, mag = m[:, 8, :], m[:, 9, :], m[:, 2, :]
                one = [pw[i][:, :, 0] for i in range(2)]
                L, V, U = (slice(k * S5_PAIRS, (k + 1) * S5_PAIRS) for k in range(3))
                link(nc.vector.reciprocal(m[:, 14, :], mag))
                link(tt(one[0][:, L], mag, cos, ALU.mult))
                link(tt(one[1][:, L], mag, sin, ALU.mult))
                link(tt(one[0][:, V], m[:, 14, :], cos, ALU.mult))
                link(nc.vector.scalar_tensor_tensor(one[1][:, V], m[:, 14, :], -1.0, sin, ALU.mult, ALU.mult))
                link(nc.vector.tensor_copy(one[0][:, U], cos))
                link(nc.vector.tensor_copy(one[1][:, U], sin))
                n = 1
                while n < S5_STEPS:
                    shape = [P, NPW, n]
                    tv = [t[:, 0:NPW * n].rearrange("p (a b) -> p a b", b=n) for t in (t1, t2)]
                    complex_product(nc, link, pw[0][:, :, n:2 * n], pw[1][:, :, n:2 * n],
                                    pw[0][:, :, 0:n], pw[1][:, :, 0:n],
                                    wide(pw[0][:, :, n - 1:n], shape), wide(pw[1][:, :, n - 1:n], shape), *tv)
                    n *= 2
                link(tt(m[:, 15, :], mag, mag, ALU.mult))
                link(tt(m[:, 16, :], m[:, 15, :], m[:, 15, :], ALU.mult))
                link(tt(rho[:, :], m[:, 16, :], m[:, 16, :], ALU.mult))
                link(nc.vector.memset(R[0][:, :, 0:1], 1.0))
                link(nc.vector.memset(R[1][:, :, 0:1], 0.0))
                for i in range(2):
                    link(nc.vector.tensor_copy(R[i][:, :, 1:2], pw[i][:, U, S5_STEPS - 1:S5_STEPS]))
                n = 1
                while n < S5_CHUNKS:
                    shape = [P, S5_PAIRS, n]
                    tv = [t[:, 0:S5_PAIRS * n].rearrange("p (a b) -> p a b", b=n) for t in (t1, t2)]
                    complex_product(nc, link, R[0][:, :, n + 1:2 * n + 1], R[1][:, :, n + 1:2 * n + 1],
                                    R[0][:, :, 1:n + 1], R[1][:, :, 1:n + 1],
                                    wide(R[0][:, :, n:n + 1], shape), wide(R[1][:, :, n:n + 1], shape), *tv)
                    n *= 2
                lr, li = lam[:, 0, :], lam[:, 1, :]
                link(tt(m[:, 15, :], lr, lr, ALU.mult))
                link(tt(m[:, 16, :], li, li, ALU.mult))
                link(tt(m[:, 17, :], m[:, 15, :], m[:, 16, :], ALU.add))
                link(nc.vector.reciprocal(m[:, 18, :], m[:, 17, :]))
                link(tsc(m[:, 19, :], one[0][:, L], -1.0, None, ALU.add))
                complex_product(nc, link, m[:, 20, :], m[:, 21, :], lr, li, m[:, 19, :], one[1][:, L],
                                m[:, 15, :], m[:, 16, :], conj=True)
                link(tt(m[:, 22, :], m[:, 20, :], m[:, 18, :], ALU.mult))
                link(tt(m[:, 23, :], m[:, 21, :], m[:, 18, :], ALU.mult))
                shape = [P, S5_PAIRS, S5_GROUP]
                tv = [t[:, 0:S5_PAIRS * S5_GROUP].rearrange("p (a b) -> p a b", b=S5_GROUP) for t in (t1, t2)]
                complex_product(nc, link, bb[:, 0], bb[:, 1], wide(m[:, 22, :].unsqueeze(2), shape),
                                wide(m[:, 23, :].unsqueeze(2), shape), B[:, 0], B[:, 1], *tv)
                shape = [P, S5_PAIRS, S5_STEPS, S5_GROUP]
                v4 = [x[:, :].rearrange("p (i s c) -> p i s c", i=S5_PAIRS, s=S5_STEPS) for x in (t1, t2)]

                def cols4(x):
                    return x[:, :, :].rearrange("p i (s c) -> p i s c", s=S5_STEPS)
                complex_product(nc, link, cols4(Bn[0]), cols4(Bn[1]),
                                wide(pw[0][:, V].unsqueeze(3), shape), wide(pw[1][:, V].unsqueeze(3), shape),
                                wide(bb[:, 0].unsqueeze(2), shape), wide(bb[:, 1].unsqueeze(2), shape), *v4)
                for i in range(2):
                    dve.wait_ge(c_tr, i + 1)
                    for g in range(2):
                        rows = slice(64 * g, 64 * g + 64)
                        src = pst[rows, i, :].rearrange("p (i g c) -> p i g c", g=2, c=S5_GROUP)[:, :, g, :]
                        last = nc.vector.tensor_copy(CT[rows, i, :, :], src)
                    last.then_inc(ct_ready, 1)
                dve.wait_ge(ct_ready, 2)
                complex_product(nc, link, cols4(G[0]), cols4(G[1]),
                                wide(pw[0][:, L].unsqueeze(3), shape), wide(pw[1][:, L].unsqueeze(3), shape),
                                wide(CT[:, 0].unsqueeze(2), shape), wide(CT[:, 1].unsqueeze(2), shape), *v4)
                tsc(G[1][:, :, :], G[1][:, :, :], -1.0, None, ALU.mult).then_inc(maps_ready, 1)
                for q in range(16):
                    dve.wait_ge(bank_full, q + 1)
                    b = pst[:, q % 4, :].rearrange("p (k c) -> p k c", c=P)
                    if q < 8:
                        nc.vector.tensor_copy(WE[q // 4][:, 4 * (q % 4):4 * (q % 4) + 4, :], b).then_inc(bank_free, 1)
                        continue
                    par, pr = q % 2, 4 * ((q - 8) // 2)
                    tt(Tm[:, :, :].rearrange("p (i g) j -> p i g j", g=2)[:, pr:pr + 4, par, :], b,
                       wide(bmask[:, :].unsqueeze(1), [P, 4, J]), ALU.mult).then_inc(bank_free, 1)
                    dve.wait_ge(bank_free, q + 1)
                    for g in range(2 * pr + par, 2 * pr + 8, 2):
                        nc.vector.scalar_tensor_tensor(Tm[:, g, :], ident[:, :], dcol[:, g:g + 1], Tm[:, g, :],
                                                       ALU.mult, ALU.add)

            @block.tensor
            def _(pe):
                pe.wait_ge(ld, n_ld)
                for i in range(2):
                    for t in range(4):
                        last = nc.tensor.transpose(pst[:, i, t * P:(t + 1) * P],
                                                   c_rows[:, i, t].rearrange("p a b -> p (a b)"), ident[:, :])
                    last.then_inc(c_tr, 1)
                pe.wait_ge(maps_ready, 1)
                for q in range(16):
                    at_least(pe, bank_free, q - 3)
                    for j in range(4):
                        o = pst[:, q % 4, j * P:(j + 1) * P]
                        if q < 8:
                            last = nc.tensor.transpose(o, Bn[q // 4][:, 4 * (q % 4) + j, :], ident[:, :])
                        else:
                            g = 2 * (4 * ((q - 8) // 2) + j) + q % 2
                            rows = slice(64 * (g % 2), 64 * (g % 2) + 64)
                            nc.tensor.matmul(o, Bn[0][rows, g // 2, :], G[0][rows, g // 2, :], start=True, stop=False)
                            last = nc.tensor.matmul(o, Bn[1][rows, g // 2, :], G[1][rows, g // 2, :], start=False, stop=True)
                    last.then_inc(bank_full, 1)

        with Phase(nc, "s5_scan") as ph:
            UT = ph.sb("UT", [P, S5_GROUPS, NCOL])
            H = [ph.sb(f"H{i}", [P, S5_PAIRS, NK]) for i in range(2)]
            h0 = [ph.sb(f"h0{i}", [P, S5_PAIRS, DEC_BATCH]) for i in range(2)]
            with Phase(nc, "s5_in") as ph2:
                flat = ph2.sb("flat", [P, 2, S5_PAIRS * NK])
                U2 = flat[:, :, :].rearrange("p a b -> p (a b)")[:, 0:S5_STEPS * HALF] \
                    .rearrange("p (s f) -> p s f", s=S5_STEPS)
                s1, s2 = flat[:, 0, :], flat[:, 1, :]
                Us = ph2.sb("Us", [2 * DEC_BATCH, S5_GROUPS, S5_STEPS, S5_GROUP])
                h_rows = ph2.sb("h_rows", [DEC_BATCH, 2, S5_GROUPS * S5_STATE])
                F = [ph2.sb(f"F{i}", [P, S5_PAIRS, NCOL]) for i in range(2)]
                turned = ph2.sb("turned", [P, 2, S5_PAIRS, NK])
                Gs = [turned[:, i] for i in range(2)]
                Ug = turned[:, :, :, :].rearrange("p a b c -> p (a b c)")[:, 0:S5_STEPS * HALF] \
                    .rearrange("p (g s c) -> p g s c", g=S5_GROUPS, s=S5_STEPS)
                hout = [ph2.sb(f"hout{i}", [P, S5_PAIRS, 1 + DEC_BATCH]) for i in range(2)]
                o_rows = ph2.sb("o_rows", [1 + DEC_BATCH, 2, S5_GROUPS * S5_STATE])
                pst = ph2.ps("pst", [P, 8, NC_COLS])
                zeroed = ph2.sem("zeroed")
                ordered = ph2.sem("ordered")
                ld = ph2.sem("ld")
                ut_tr = ph2.sem("ut_tr")
                ut_ready = ph2.sem("ut_ready")
                h_tr = ph2.sem("h_tr")
                h_ready = ph2.sem("h_ready")
                f_mm = ph2.sem("f_mm")
                f_ready = ph2.sem("f_ready")
                own = ph2.sem("own")
                out_ready = ph2.sem("out_ready")
                out_tr = ph2.sem("out_tr")
                out_cp = ph2.sem("out_cp")
                st = ph2.sem("st")
                block = ph2.block()
                n_ld = 16 * (3 + 2 * DEC_SEQ)

                @block.sync
                def _(sp):
                    sp.dma_start(U2[:, :, :], proj[0:SEQ, 0:HALF].rearrange("(k s) f -> k s f", s=S5_STEPS)
                                 ).then_inc(ld, 16)
                    for i, nm in enumerate(["state_s5_re", "state_s5_im"]):
                        sp.dma_start(h_rows[:, i, :], A[nm][0].rearrange("b g p -> b (g p)")).then_inc(ld, 16)
                    sp.wait_ge(zeroed, 1)
                    us = proj[SEQ:TOK, 0:HALF].rearrange("(b s) f -> b s f", s=DEC_SEQ)
                    for k in range(2):
                        for s in range(DEC_SEQ):
                            sp.dma_start(Us[k * DEC_BATCH:(k + 1) * DEC_BATCH, :, k * DEC_SEQ + s, :],
                                         us[:, s, :].rearrange("b (g c) -> b g c", c=S5_GROUP)).then_inc(ld, 16)
                    sp.wait_ge(out_cp, 8)
                    for i, (pn, sn) in enumerate([("o_s5_re_p", "o_s5_re_s"), ("o_s5_im_p", "o_s5_im_s")]):
                        sp.dma_start(A[pn], o_rows[0:1, i, :]).then_inc(st, 16)
                        sp.dma_start(A[sn], o_rows[1:1 + DEC_BATCH, i, :]).then_inc(st, 16)
                    sp.wait_ge(st, 64)

                @block.tensor
                def _(pe):
                    pe.wait_ge(ld, n_ld)
                    for i in range(2):
                        for j in range(S5_PAIRS):
                            last = nc.tensor.transpose(pst[:, 7, (i * S5_PAIRS + j) * 8:(i * S5_PAIRS + j + 1) * 8],
                                                       h_rows[:, i, j * P:(j + 1) * P], ident[0:8, 0:8])
                    last.then_inc(h_tr, 1)
                    for g in range(S5_GROUPS):
                        q = g % 6
                        at_least(pe, ut_ready, g - 5)
                        if g % 8 == 0:
                            pe.wait_ge(ordered, g // 8 + 1)
                        nc.tensor.transpose(pst[:, q, 0:P], Ug[:, g].rearrange("p s c -> p (s c)"), ident[:, :])
                        nc.tensor.transpose(pst[:, q, P:NCOL], Us[:, g].rearrange("p s c -> p (s c)"),
                                            ident[0:16, 0:16]).then_inc(ut_tr, 1)
                    pe.wait_ge(ut_ready, S5_GROUPS)
                    for j in range(2 * S5_PAIRS):
                        i, pr = j % 2, j // 2
                        at_least(pe, f_ready, j - 5)
                        for g in range(2):
                            rows = slice(64 * g, 64 * g + 64)
                            last = nc.tensor.matmul(pst[rows, j % 6, 0:NCOL], WE[i][:, pr, rows], UT[:, 2 * pr + g, :],
                                                    start=True, stop=True)
                        last.then_inc(f_mm, 1)
                    pe.wait_ge(out_ready, 1)
                    for n in range(8):
                        i, q = n // 4, n % 4
                        at_least(pe, out_cp, n - 3)
                        for k in range(4):
                            last = nc.tensor.transpose(pst[0:1 + DEC_BATCH, n % 4, k * P:(k + 1) * P],
                                                       hout[i][:, 4 * q + k, :], ident[:, :])
                        last.then_inc(out_tr, 1)

                @block.scalar
                def _(act):
                    act.wait_ge(h_tr, 1)
                    for i in range(2):
                        nc.scalar.activation(h0[i][:, :, :].rearrange("p a b -> p (a b)"),
                                             pst[:, 7, i * P:(i + 1) * P], ACT.Copy).then_inc(h_ready, 1)
                    for g in range(S5_GROUPS):
                        act.wait_ge(ut_tr, g + 1)
                        nc.scalar.activation(UT[:, g, :], pst[:, g % 6, 0:NCOL], ACT.Copy).then_inc(ut_ready, 1)
                    for j in range(2 * S5_PAIRS):
                        act.wait_ge(f_mm, j + 1)
                        nc.scalar.activation(F[j % 2][:, j // 2, :], pst[:, j % 6, 0:NCOL], ACT.Copy).then_inc(f_ready, 1)
                    for n in range(8):
                        act.wait_ge(out_tr, n + 1)
                        nc.scalar.activation(o_rows[:, n // 4, (n % 4) * NC_COLS:(n % 4 + 1) * NC_COLS],
                                             pst[0:1 + DEC_BATCH, n % 4, :], ACT.Copy).then_inc(out_cp, 1)

                @block.vector
                def _(dve):
                    nc.vector.memset(Us[:, :, :, :], 0.0).then_inc(zeroed, 1)
                    link = Chain(dve, own)
                    dve.wait_ge(ld, n_ld)
                    for q in range(4):
                        nc.vector.tensor_copy(Ug[:, 8 * q:8 * q + 8], U2[:, :, P * q:P * q + P]
                                              .rearrange("p s (g c) -> p g s c", c=S5_GROUP)).then_inc(ordered, 1)
                    dve.wait_ge(f_ready, 2 * S5_PAIRS)
                    for i in range(2):
                        link(nc.vector.memset(Gs[i][:, :, 0:1], 0.0))
                    K_ = S5_CHUNKS
                    tv = [t[:, 0:S5_PAIRS * K_].rearrange("p (a b) -> p a b", b=K_) for t in (s1, s2)]
                    x = [h[:, :, 0:K_] for h in H]
                    complex_product(nc, link, x[0], x[1], R[0][:, :, 0:K_], R[1][:, :, 0:K_],
                                    F[0][:, :, 0:K_], F[1][:, :, 0:K_], *tv, conj=True)
                    for i in range(2):
                        for j in range(S5_PAIRS):
                            last = nc.vector.tensor_tensor_scan(Gs[i][:, j, 1:NK], H[i][:, j, 0:K_],
                                                                wide(rho[:, j:j + 1], [P, K_]), 0.0, ALU.add, ALU.mult)
                        link(last)
                    tv = [t.rearrange("p (a b) -> p a b", b=NK) for t in (s1, s2)]
                    complex_product(nc, link, H[0][:, :, :], H[1][:, :, :], R[0][:, :, :], R[1][:, :, :],
                                    Gs[0][:, :, :], Gs[1][:, :, :], *tv)
                    shape = [P, S5_PAIRS, DEC_BATCH]
                    tv = [t[:, 0:P].rearrange("p (a b) -> p a b", b=DEC_BATCH) for t in (s1, s2)]
                    ac = [t[:, 2 * P:3 * P].rearrange("p (a b) -> p a b", b=DEC_BATCH) for t in (s1, s2)]
                    dve.wait_ge(h_ready, 2)
                    Lp = slice(0, S5_PAIRS)
                    complex_product(nc, link, hout[0][:, :, 1:], hout[1][:, :, 1:], wide(pw[0][:, Lp, 3:4], shape),
                                    wide(pw[1][:, Lp, 3:4], shape), h0[0][:, :, :], h0[1][:, :, :], *tv)
                    complex_product(nc, link, ac[0], ac[1], wide(pw[0][:, Lp, 7:8], shape),
                                    wide(pw[1][:, Lp, 7:8], shape), F[0][:, :, NCOL - 8:], F[1][:, :, NCOL - 8:], *tv)
                    for i in range(2):
                        link(nc.vector.tensor_tensor(hout[i][:, :, 1:], hout[i][:, :, 1:], ac[i], ALU.add))
                        last = nc.vector.tensor_copy(hout[i][:, :, 0:1], H[i][:, :, K_:NK])
                    last.then_inc(out_ready, 1)

            with Phase(nc, "s5_out") as ph2:
                Y = ph2.sb("Y", [P, S5_STEPS, HALF])
                Ys = ph2.sb("Ys", [DEC_BATCH, DEC_SEQ, HALF])
                w_glu = ph2.sb("w_glu", [P, 4, HALF])
                bias = ph2.sb("bias", [P, HALF])
                yT = ph2.sb("yT", [P, 2, 4, P])
                z = ph2.sb("z", [P, 2, HALF])
                zs = ph2.sb("zs", [P, 2, HALF])
                pst = ph2.ps("pst", [P, 6, NC_COLS])
                ld = ph2.sem("ld")
                y_mm = ph2.sem("y_mm")
                y_ready = ph2.sem("y_ready")
                y_tr = ph2.sem("y_tr")
                yT_ready = ph2.sem("yT_ready")
                z_mm = ph2.sem("z_mm")
                z_ready = ph2.sem("z_ready")
                sig = ph2.sem("sig")
                out_ready = ph2.sem("out_ready")
                st = ph2.sem("st")
                block = ph2.block()
                NG4 = S5_GROUPS // 4
                units = [(P, Y, s) for s in range(S5_STEPS)] + [(DEC_BATCH, Ys, s) for s in range(DEC_SEQ)]

                @block.sync
                def _(sp):
                    sp.dma_start(w_glu[:, :, :], A["s5_w_glu"][0].rearrange("(k p) n -> p k n", p=P)).then_inc(ld, 16)
                    sp.dma_start(bias[:, :], A["s5_b_glu"].broadcast_to([P, HALF])).then_inc(ld, 16)
                    mp = mix[0:SEQ, 0:HALF].rearrange("(k s) f -> k s f", s=S5_STEPS)
                    ms = mix[SEQ:TOK, 0:HALF].rearrange("(b s) f -> b s f", s=DEC_SEQ)
                    for n, (r, y, s) in enumerate(units):
                        sp.wait_ge(out_ready, n + 1)
                        sp.dma_start((mp if r == P else ms)[:, s, :], y[:, s, :]).then_inc(st, 16)
                    sp.wait_ge(st, 16 * len(units))

                @block.tensor
                def _(pe):
                    for q in range(2 * NG4):
                        at_least(pe, y_ready, q - 3)
                        r = P if q < NG4 else DEC_BATCH
                        for k in range(4):
                            g = 2 * (4 * (q % NG4 // 2) + k) + q % 2
                            o = pst[0:r, q % 4, k * J:(k + 1) * J]
                            rows = slice(64 * (g % 2), 64 * (g % 2) + 64)
                            u = UT[:, g, 0:P] if q < NG4 else UT[:, g, P:P + DEC_BATCH]
                            h = [(H[i][rows, g // 2, 0:P] if q < NG4 else h0[i][rows, g // 2, :]) for i in range(2)]
                            nc.tensor.matmul(o, u, Tm[:, g, :], start=True, stop=False)
                            nc.tensor.matmul(o, h[0], G[0][rows, g // 2, :], start=False, stop=False)
                            last = nc.tensor.matmul(o, h[1], G[1][rows, g // 2, :], start=False, stop=True)
                        last.then_inc(y_mm, 1)
                    pe.wait_ge(y_ready, 2 * NG4)
                    pe.wait_ge(ld, 32)
                    for n, (r, y, s) in enumerate(units):
                        at_least(pe, yT_ready, n - 1)
                        for k in range(4):
                            last = nc.tensor.transpose(pst[:, n % 2, k * P:k * P + r], y[0:r, s, k * P:(k + 1) * P],
                                                       ident[0:r, 0:r])
                        last.then_inc(y_tr, 1)
                        pe.wait_ge(yT_ready, n + 1)
                        at_least(pe, z_ready, n - 1)
                        for k in range(4):
                            last = nc.tensor.matmul(pst[0:r, 4 + n % 2, :], yT[:, n % 2, k, 0:r], w_glu[:, k, :],
                                                    start=(k == 0), stop=(k == 3))
                        last.then_inc(z_mm, 1)

                @block.scalar
                def _(act):
                    for q in range(2 * NG4):
                        act.wait_ge(y_mm, q + 1)
                        r, y, ns = (P, Y, S5_STEPS) if q < NG4 else (DEC_BATCH, Ys, DEC_SEQ)
                        src = pst[0:r, q % 4, :].rearrange("p (i s c) -> p i s c", i=4, s=S5_STEPS)[:, :, 0:ns, :]
                        dst = y[:, :, :].rearrange("p s (q i g c) -> p q g i s c", q=4, i=4, g=2)
                        nc.scalar.activation(dst[:, q % NG4 // 2, q % 2], src, ACT.Gelu_apprx_tanh).then_inc(y_ready, 1)
                    for n, (r, y, s) in enumerate(units):
                        act.wait_ge(z_ready, n + 1)
                        at_least(act, out_ready, n - 1)
                        nc.scalar.activation(zs[0:r, n % 2, :], z[0:r, n % 2, :], ACT.Sigmoid).then_inc(sig, 1)

                @block.vector
                def _(dve):
                    def finish(n):
                        r, y, s = units[n]
                        dve.wait_ge(sig, n + 1)
                        nc.vector.tensor_tensor(y[0:r, s, :], y[0:r, s, :], zs[0:r, n % 2, :], ALU.mult
                                                ).then_inc(out_ready, 1)
                    dve.wait_ge(ld, 32)
                    for n, (r, y, s) in enumerate(units):
                        dve.wait_ge(y_tr, n + 1)
                        at_least(dve, z_mm, n - 1)
                        nc.vector.tensor_copy(yT[:, n % 2, :, 0:r], pst[:, n % 2, :]
                                              .rearrange("p (k c) -> p k c", c=P)[:, :, 0:r]).then_inc(yT_ready, 1)
                        dve.wait_ge(z_mm, n + 1)
                        at_least(dve, sig, n - 1)
                        nc.vector.tensor_tensor(z[0:r, n % 2, :], pst[0:r, 4 + n % 2, :], bias[0:r, :], ALU.add
                                                ).then_inc(z_ready, 1)
                        if n:
                            finish(n - 1)
                    finish(len(units) - 1)


def unit_of(t):
    return 2 + (t if t < 4 else 4 + 2 * (t - 4))


def key_blocks(t):
    return [(b, min(4, t + 1 - b)) for b in range(0, t + 1, 4)]


def prompt_attention(nc, name, A, q_src, k_src, v_src, mix, softmax):
    UNITS = 14
    with Phase(nc, name) as ph:
        ident = ph.sb("ident", [P, P])
        raw = ph.sb("raw", [P, 2, PT, 3, HEAD_DIM])
        qkT = ph.sb("qkT", [HEAD_DIM, 2, SEQ])
        ex = ph.sb("ex", [P, 2, SEQ])
        cp = ph.sb("cp", [P, SEQ + 1])
        w = ph.sb("w", [P, 2, SEQ])
        wT = ph.sb("wT", [P, 2, SEQ])
        zero = ph.sb("zero", [P, 1])
        not_before = ph.sb("not_before", [P, P])
        stage = ph.sb("stage", [P, 2, PT, HEAD_DIM])
        if softmax:
            sel = ph.sb("sel", [P, PT, SEQ])
            near = ph.sb("near", [P, HEADS, 2 * P])
            stat = ph.sb("stat", [P, 4, PT])
        ps_s = ph.ps("ps_s", [P, 2, 2, NC_COLS])
        ps_t = ph.ps("ps_t", [P, 2, NC_COLS])
        ps_o = ph.ps("ps_o", [P, NC_COLS])
        const_ld = ph.sem("const_ld")
        ld = [ph.sem(f"ld{i}") for i in range(2)]
        s_mm = ph.sem("s_mm")
        keep_done = ph.sem("keep_done")
        diag_done = ph.sem("diag_done")
        scan_done = ph.sem("scan_done")
        set_up = ph.sem("set_up")
        logit_done = ph.sem("logit_done")
        max_done = ph.sem("max_done")
        sum_inv = ph.sem("sum_inv")
        w_done = ph.sem("w_done")
        tr_done = ph.sem("tr_done")
        u_ev = ph.sem("u_ev")
        pv_done = ph.sem("pv_done")
        o_ev = ph.sem("o_ev")
        st = [ph.sem(f"st{i}") for i in range(2)]
        srcs = [x.rearrange("(t p) (h d) -> h p t d", p=P, d=HEAD_DIM) for x in (q_src, k_src, v_src)]
        dst = mix.rearrange("(t p) (h d) -> h p t d", p=P, d=HEAD_DIM)
        block = ph.block()

        def heads(eng, body):
            body(0, 0)
            body(1, 1)
            with eng.Fori(1, HEADS // 2) as i:
                body(i * 2, 0)
                body(i * 2 + 1, 1)

        @block.sync
        def _(sp):
            sp.dma_start(ident[:, :], A["c_ident"]).then_inc(const_ld, 16)
            sp.dma_start(not_before[:, :], A["c_not_before"]).then_inc(const_ld, 16)
            if softmax:
                for h in range(HEADS):
                    sp.dma_start(near[:, h, :], skewed(A["near"][h], NEAR_TOP - P, 2 * P, P)).then_inc(const_ld, 16)
                for t in range(PT):
                    sp.dma_start(sel[:, t, 0:(t + 1) * P], A["sel"][t, :, 0:(t + 1) * P]).then_inc(const_ld, 16)

            def load(h, s):
                at_least(sp, pv_done, (h - 1) * PT)
                for i in range(3):
                    sp.dma_start(raw[:, s, :, i, :], srcs[i][h]).then_inc(ld[s], 16)
            heads(sp, load)

        n_const = 16 * (2 + HEADS + PT if softmax else 2)

        @block.gpsimd
        def _(pool):
            def store(h, s):
                pool.wait_ge(o_ev, h + 1)
                pool.dma_start(dst[h], stage[:, s, :, :]).then_inc(st[s], 16)
            heads(pool, store)
            for s in range(2):
                pool.wait_ge(st[s], 16 * HEADS // 2)

        @block.tensor
        def _(pe):
            pe.wait_ge(const_ld, n_const)

            def scores(h, t):
                at_least(pe, logit_done if softmax else keep_done, h * PT + t - 1)
                for b, (b0, n) in enumerate(key_blocks(t)):
                    last = nc.tensor.matmul(ps_s[:, t % 2, b, 0:n * P], qkT[:, 0, t * P:(t + 1) * P],
                                            qkT[:, 1, b0 * P:(b0 + n) * P], start=True, stop=True)
                last.then_inc(s_mm, 1)

            def head(h, s):
                pe.wait_ge(ld[s], (h - s) * 24 + 48)
                for u in range(2):
                    at_least(pe, u_ev, h * UNITS + u - 1)
                    for j in range(4):
                        last = nc.tensor.transpose(ps_t[:, u, j * P:(j + 1) * P],
                                                   raw[:, s, 4 * u + j, 0:2, :].rearrange("p a d -> p (a d)"), ident[:, :])
                    last.then_inc(tr_done, 1)
                pe.wait_ge(u_ev, h * UNITS + 2)
                scores(h, 0)
                scores(h, 1)
                for t in range(PT):
                    pe.wait_ge(w_done, h * PT + t + 1)
                    for b, (b0, n) in enumerate(key_blocks(t)):
                        u = unit_of(t) + b
                        pe.wait_ge(u_ev, h * UNITS + u - 1)
                        for j in range(n):
                            last = nc.tensor.transpose(ps_t[:, u % 2, j * P:(j + 1) * P],
                                                       w[:, t % 2, (b0 + j) * P:(b0 + j + 1) * P], ident[:, :])
                        last.then_inc(tr_done, 1)
                    if t + 2 < PT:
                        scores(h, t + 2)
                    pe.wait_ge(u_ev, h * UNITS + unit_of(t + 1))
                    if t == 0:
                        at_least(pe, o_ev, h)
                    for j in range(t + 1):
                        last = nc.tensor.matmul(ps_o[:, t * HEAD_DIM:(t + 1) * HEAD_DIM], wT[:, t % 2, j * P:(j + 1) * P],
                                                raw[:, s, j, 2, :], start=(j == 0), stop=(j == t))
                    last.then_inc(pv_done, 1)
            heads(pe, head)

        @block.scalar
        def _(act):
            def turn(h, u, dst_ap, src_ap):
                act.wait_ge(tr_done, h * UNITS + u + 1)
                nc.scalar.activation(dst_ap, src_ap, ACT.Copy).then_inc(u_ev, 1)

            def head(h, s):
                at_least(act, pv_done, h * PT)
                for u in range(2):
                    act.wait_ge(tr_done, h * UNITS + u + 1)
                    for i in range(2):
                        last = nc.scalar.activation(qkT[:, i, u * NC_COLS:(u + 1) * NC_COLS],
                                                    ps_t[i * HEAD_DIM:(i + 1) * HEAD_DIM, u, :], ACT.Copy)
                    last.then_inc(u_ev, 1)

                def weigh(t):
                    n = (t + 1) * P
                    if softmax:
                        act.wait_ge(max_done, h * PT + t + 1)
                        if t < 2:
                            at_least(act, tr_done, h * UNITS - (4 if t == 0 else 2) + 2)
                        else:
                            act.wait_ge(tr_done, h * UNITS + unit_of(t - 1))
                        if t == 0:
                            at_least(act, o_ev, h)
                        nc.scalar.activation(w[:, t % 2, 0:n], ex[:, t % 2, 0:n], ACT.Exp, bias=stat[:, 0, t:t + 1],
                                             accum_out=stat[:, 1, t:t + 1]).then_inc(w_done, 1)
                        return
                    act.wait_ge(s_mm, h * PT + t + 1)
                    at_least(act, scan_done, h * PT + t - 1)
                    for b, (b0, m) in enumerate(key_blocks(t)):
                        last = nc.scalar.activation(ex[:, t % 2, b0 * P:(b0 + m) * P], ps_s[:, t % 2, b, 0:m * P],
                                                    ACT.Sigmoid, scale=-SCALE)
                    last.then_inc(keep_done, 1)

                weigh(0)
                for t in range(PT):
                    if t + 1 < PT:
                        weigh(t + 1)
                    if t < 2:
                        at_least(act, pv_done, h * PT + t - 1)
                    else:
                        act.wait_ge(pv_done, h * PT + t - 1)
                    for b, (b0, n) in enumerate(key_blocks(t)):
                        u = unit_of(t) + b
                        turn(h, u, wT[:, t % 2, b0 * P:(b0 + n) * P], ps_t[:, u % 2, 0:n * P])
            heads(act, head)

        @block.vector
        def _(dve):
            nc.vector.memset(zero[:, :], 0.0).then_inc(set_up, 1)
            dve.wait_ge(set_up, 1)
            dve.wait_ge(const_ld, n_const)

            def head(h, s):
                for t in range(PT):
                    n = (t + 1) * P
                    if softmax:
                        dve.wait_ge(s_mm, h * PT + t + 1)
                        at_least(dve, w_done, h * PT + t - 1)
                        for b, (b0, m) in enumerate(key_blocks(t)):
                            cols = slice(b0 * P, (b0 + m) * P)
                            last = nc.vector.scalar_tensor_tensor(ex[:, t % 2, cols], ps_s[:, t % 2, b, 0:m * P], SCALE,
                                                                  sel[:, t, cols], ALU.mult, ALU.add)
                        last.then_inc(logit_done, 1)
                        dve.wait_ge(logit_done, h * PT + t + 1)
                        k0 = max(t - 1, 0) * P
                        nc.vector.tensor_tensor(ex[:, t % 2, k0:n], ex[:, t % 2, k0:n],
                                                near[:, h, 2 * P - (n - k0):2 * P], ALU.add).then_inc(scan_done, 1)
                        dve.wait_ge(scan_done, h * PT + t + 1)
                        nc.vector.tensor_reduce(stat[:, 0, t:t + 1], ex[:, t % 2, 0:n], AX_X, ALU.max,
                                                negate=True).then_inc(max_done, 1)
                        continue
                    dve.wait_ge(keep_done, h * PT + t + 1)
                    diag = ex[:, t % 2, t * P:n]
                    nc.vector.tensor_tensor(diag, diag, not_before[:, :], ALU.max).then_inc(diag_done, 1)
                    at_least(dve, w_done, h * PT + t)
                    nc.vector.memset(cp[:, n:n + 1], 1.0)
                    dve.wait_ge(diag_done, h * PT + t + 1)
                    nc.vector.tensor_tensor_scan(cp[:, 0:n][:, ::-1], ex[:, t % 2, 0:n][:, ::-1],
                                                 wide(zero[:, :], [P, n]), 1.0, ALU.mult, ALU.add).then_inc(scan_done, 1)
                    dve.wait_ge(scan_done, h * PT + t + 1)
                    if t < 2:
                        at_least(dve, tr_done, h * UNITS - 2 * (1 - t))
                    else:
                        dve.wait_ge(tr_done, h * UNITS + unit_of(t - 1))
                    nc.vector.tensor_tensor(w[:, t % 2, 0:n], cp[:, 1:n + 1], cp[:, 0:n], ALU.subtract).then_inc(w_done, 1)
                dve.wait_ge(pv_done, (h + 1) * PT)
                if not isinstance(h, int) or h >= 2:
                    dve.wait_ge(st[s], (h - s) * 8)
                if softmax:
                    nc.vector.reciprocal(stat[:, 2, :], stat[:, 1, :]).then_inc(sum_inv, 1)
                    dve.wait_ge(sum_inv, h + 1)
                    nc.vector.tensor_tensor(stage[:, s, :, :], ps_o[:, :].rearrange("p (t d) -> p t d", d=HEAD_DIM),
                                            wide(stat[:, 2, :].unsqueeze(2), [P, PT, HEAD_DIM]), ALU.mult).then_inc(o_ev, 1)
                else:
                    nc.vector.tensor_copy(stage[:, s, :, :].rearrange("p t d -> p (t d)"), ps_o[:, :]).then_inc(o_ev, 1)

            heads(dve, head)


NEAR = 400
NEAR_TOP = 260


def sample_attention(nc, name, A, q_src, k_src, v_src, pool_k, pool_v, mix, softmax):
    G4 = 4
    ROUNDS = DEC_BATCH // G4
    HP = HEADS // 2
    R = HEADS * DEC_SEQ
    ALL = PAST_LEN + DEC_SEQ
    ITEMS = 2 * DEC_BATCH
    SLOTS = 3
    with Phase(nc, name) as ph:
        ident = ph.sb("ident", [P, P])
        table = ph.sb("table", [1, DEC_BATCH * N_PAGES], I32)
        pages = ph.sb("pages", [P, SLOTS, N_PAGES, HALF])
        qk_rows = ph.sb("qk_rows", [NS, 2, HALF])
        v_new = ph.sb("v_new", [DEC_SEQ, DEC_BATCH, HALF])
        qkT = ph.sb("qkT", [P, 2, HP, NS])
        Q = ph.sb("Q", [P, DEC_BATCH, HP, P])
        kT = ph.sb("kT", [P, 2, HP, PAST_LEN])
        ex = ph.sb("ex", [P, ALL])
        cp = ph.sb("cp", [P, ALL + 1])
        w = ph.sb("w", [P, ALL])
        wT = ph.sb("wT", [P, N_PAGES + 1, P])
        own_head = ph.sb("own_head", [R, HEADS])
        late = ph.sb("late", [P, DEC_SEQ])
        zero = ph.sb("zero", [P, 1])
        tmp = ph.sb("tmp", [R, HALF])
        out = ph.sb("out", [R, DEC_BATCH, HEAD_DIM])
        if softmax:
            sel = ph.sb("sel", [P, ALL])
            near = ph.sb("near", [P, 256 + DEC_SEQ])
            stat = ph.sb("stat", [P, 4])
        ps_t = ph.ps("ps_t", [P, 2, NC_COLS])
        ps_s = ph.ps("ps_s", [P, 3, NC_COLS])
        ps_o = ph.ps("ps_o", [P, 2, NC_COLS])
        table_ld = ph.sem("table_ld")
        ld = ph.sem("ld")
        sel_ld = ph.sem("sel_ld")
        page_ld = [ph.sem(f"page_ld{i}") for i in range(SLOTS)]
        set_up = ph.sem("set_up")
        qk_tr = ph.sem("qk_tr")
        q_ready = ph.sem("q_ready")
        unit_tr = ph.sem("unit_tr")
        unit_ev = ph.sem("unit_ev")
        s_mm = ph.sem("s_mm")
        keep_done = ph.sem("keep_done")
        own = ph.sem("own")
        w_done = ph.sem("w_done")
        pv_mm = ph.sem("pv_mm")
        o_ev = ph.sem("o_ev")
        out_ready = ph.sem("out_ready")
        st = ph.sem("st")
        out_sum = ph.sem("out_sum")
        inv_done = ph.sem("inv_done")
        n_ld = 16 * (6 + (G4 if softmax else 0))
        items = [(kv, r * G4 + g) for r in range(ROUNDS) for kv in range(2) for g in range(G4)]
        KU, WU = N_PAGES, 3
        RU = G4 * KU + WU
        block = ph.block()

        @block.sync
        def _(sp):
            sp.dma_start(table[:, :], A["page_table"].rearrange("b n -> (b n)").unsqueeze(0)).then_inc(table_ld, 16)
            sp.dma_start(ident[:, :], A["c_ident"]).then_inc(ld, 16)
            sp.dma_start(own_head[:, :], A["c_own_head"]).then_inc(ld, 16)
            sp.dma_start(late[:, :], A["c_late"]).then_inc(ld, 16)
            sp.dma_start(qk_rows[:, 0, :], q_src).then_inc(ld, 16)
            sp.dma_start(qk_rows[:, 1, :], k_src).then_inc(ld, 16)
            sp.dma_start(v_new[:, :, :], v_src.rearrange("(b s) f -> s b f", s=DEC_SEQ)).then_inc(ld, 16)
            if softmax:
                for g in range(G4):
                    sp.dma_start(near[g * R:(g + 1) * R, :], A["near_sample"]).then_inc(ld, 16)
            sp.wait_ge(table_ld, 16)
            for n, (kv, b) in enumerate(items):
                if n >= SLOTS:
                    was_v, c = items[n - SLOTS]
                    if was_v:
                        sp.wait_ge(pv_mm, c + 1)
                    else:
                        sp.wait_ge(unit_tr, c // G4 * RU + (c % G4 + 1) * KU)
                for pg in range(N_PAGES):
                    row = sp.value_load(table[0:1, b * N_PAGES + pg:b * N_PAGES + pg + 1], min_val=0,
                                        max_val=pool_k.shape[0] - 1)
                    sp.dma_start(pages[:, n % SLOTS, pg, :], (pool_v if kv else pool_k)[row]
                                 ).then_inc(page_ld[n % SLOTS], 16)
            sp.wait_ge(out_ready, DEC_BATCH)
            for h in range(HEADS):
                sp.dma_start(mix[:, h * HEAD_DIM:(h + 1) * HEAD_DIM].rearrange("(b s) d -> s b d", s=DEC_SEQ),
                             out[h * DEC_SEQ:(h + 1) * DEC_SEQ, :, :]).then_inc(st, 16)
            sp.wait_ge(st, 16 * HEADS)

        if softmax:
            @block.gpsimd
            def _(pool):
                for r in range(ROUNDS):
                    at_least(pool, w_done, r)
                    for g in range(G4):
                        b = r * G4 + g
                        src = A["sel_sample"][b * DEC_SEQ:(b + 1) * DEC_SEQ, :]
                        for h in range(HEADS):
                            pool.dma_start(sel[g * R + h * DEC_SEQ:g * R + (h + 1) * DEC_SEQ, :], src).then_inc(sel_ld, 16)

        @block.tensor
        def _(pe):
            pe.wait_ge(ld, n_ld)
            for i in range(2):
                for hp in range(HP):
                    last = nc.tensor.transpose(ps_t[:, i, hp * NS:(hp + 1) * NS], qk_rows[:, i, hp * P:(hp + 1) * P],
                                               ident[0:NS, 0:NS])
            last.then_inc(qk_tr, 1)
            pe.wait_ge(q_ready, 1)
            for n, (kv, b) in enumerate(items):
                r, g = b // G4, b % G4
                pe.wait_ge(page_ld[n % SLOTS], 16 * N_PAGES * (n // SLOTS + 1))
                pg_slot = pages[:, n % SLOTS]
                if kv == 0:
                    for pg in range(N_PAGES):
                        u = r * RU + g * KU + pg
                        at_least(pe, unit_ev, u - 1)
                        for hp in range(HP):
                            last = nc.tensor.transpose(ps_t[:, u % 2, hp * P:(hp + 1) * P],
                                                       pg_slot[:, pg, hp * P:(hp + 1) * P], ident[:, :])
                        last.then_inc(unit_tr, 1)
                    pe.wait_ge(unit_ev, r * RU + (g + 1) * KU)
                    if g == 0:
                        at_least(pe, keep_done, r)
                    for hp in range(HP):
                        ends = dict(start=(g == 0 and hp == 0), stop=(g == G4 - 1 and hp == HP - 1))
                        for c in range(2):
                            nc.tensor.matmul(ps_s[:, c, :], Q[:, b, hp, :], kT[:, b % 2, hp, c * NC_COLS:(c + 1) * NC_COLS],
                                             **ends)
                        last = nc.tensor.matmul(ps_s[:, 2, 0:DEC_SEQ], Q[:, b, hp, :],
                                                qkT[:, 1, hp, b * DEC_SEQ:(b + 1) * DEC_SEQ], **ends)
                    last.then_inc(s_mm, 1)
                    continue
                if g == 0:
                    pe.wait_ge(w_done, r + 1)
                    for j in range(WU):
                        u = r * RU + G4 * KU + j
                        pe.wait_ge(unit_ev, u - 1)
                        for i in range(4 if j < 2 else 1):
                            src = w[:, (4 * j + i) * P:(4 * j + i + 1) * P] if j < 2 else w[:, PAST_LEN:ALL]
                            last = nc.tensor.transpose(ps_t[0:src.shape[1], u % 2, i * P:(i + 1) * P], src, ident[:, :])
                        last.then_inc(unit_tr, 1)
                    pe.wait_ge(unit_ev, (r + 1) * RU)
                at_least(pe, o_ev, b - 1)
                for pg in range(N_PAGES):
                    nc.tensor.matmul(ps_o[0:R, b % 2, :], wT[:, pg, g * R:(g + 1) * R], pg_slot[:, pg, :],
                                            start=(pg == 0), stop=False)
                nc.tensor.matmul(ps_o[0:R, b % 2, :], wT[0:DEC_SEQ, N_PAGES, g * R:(g + 1) * R], v_new[:, b, :],
                                 start=False, stop=True).then_inc(pv_mm, 1)

        @block.scalar
        def _(act):
            for r in range(ROUNDS):
                for g in range(G4):
                    b = r * G4 + g
                    for pg in range(N_PAGES):
                        u = r * RU + g * KU + pg
                        act.wait_ge(unit_tr, u + 1)
                        if pg == 0:
                            at_least(act, s_mm, b - 1)
                        nc.scalar.activation(kT[:, b % 2, :, pg * P:(pg + 1) * P],
                                             ps_t[:, u % 2, :].rearrange("p (h c) -> p h c", c=P), ACT.Copy
                                             ).then_inc(unit_ev, 1)
                act.wait_ge(s_mm, (r + 1) * G4)
                if softmax:
                    act.wait_ge(own, 2 * (r + 1))
                    nc.scalar.activation(cp[:, 0:ALL], ex[:, :], ACT.Exp, bias=stat[:, 0:1],
                                         accum_out=stat[:, 1:2]).then_inc(out_sum, 1)
                else:
                    at_least(act, w_done, r)
                    for c in range(3):
                        n = NC_COLS if c < 2 else DEC_SEQ
                        last = nc.scalar.activation(ex[:, c * NC_COLS:c * NC_COLS + n], ps_s[:, c, 0:n], ACT.Sigmoid,
                                                    scale=-SCALE)
                    last.then_inc(keep_done, 1)
                for j in range(WU):
                    u = r * RU + G4 * KU + j
                    act.wait_ge(unit_tr, u + 1)
                    at_least(act, pv_mm, r * G4)
                    if j < 2:
                        nc.scalar.activation(wT[:, 4 * j:4 * j + 4, :].rearrange("p a b -> p (a b)"), ps_t[:, u % 2, :],
                                             ACT.Copy).then_inc(unit_ev, 1)
                    else:
                        nc.scalar.activation(wT[0:DEC_SEQ, N_PAGES, :], ps_t[0:DEC_SEQ, u % 2, 0:P],
                                             ACT.Copy).then_inc(unit_ev, 1)

        @block.vector
        def _(dve):
            nc.vector.memset(Q[:, :, :, :], 0.0).then_inc(set_up, 1)
            nc.vector.memset(zero[:, :], 0.0).then_inc(set_up, 1)
            nc.vector.memset(cp[:, ALL:ALL + 1], 1.0).then_inc(set_up, 1)
            dve.wait_ge(set_up, 3)
            dve.wait_ge(qk_tr, 1)
            nc.vector.tensor_copy(qkT[:, 1, :, :].rearrange("p h c -> p (h c)"), ps_t[:, 1, 0:HP * NS])
            for b in range(DEC_BATCH):
                for h in range(HEADS):
                    rows = slice(64 * (h % 2), 64 * (h % 2) + 64)
                    c0 = (b % G4) * R + h * DEC_SEQ
                    q0 = (h // 2) * NS + b * DEC_SEQ
                    last = nc.vector.tensor_copy(Q[rows, b, h // 2, c0:c0 + DEC_SEQ], ps_t[rows, 0, q0:q0 + DEC_SEQ])
            last.then_inc(q_ready, 1)
            dve.wait_ge(ld, n_ld)

            def chunks():
                return [(c, NC_COLS if c < 2 else DEC_SEQ) for c in range(3)]
            for r in range(ROUNDS):
                if softmax:
                    dve.wait_ge(s_mm, (r + 1) * G4)
                    dve.wait_ge(sel_ld, 16 * HEADS * G4 * (r + 1))
                    for c, n in chunks():
                        cols = slice(c * NC_COLS, c * NC_COLS + n)
                        last = nc.vector.scalar_tensor_tensor(ex[:, cols], ps_s[:, c, 0:n], SCALE, sel[:, cols],
                                                              ALU.mult, ALU.add)
                    last.then_inc(keep_done, 1)
                    dve.wait_ge(keep_done, r + 1)
                    nc.vector.tensor_tensor(ex[:, PAST_LEN - 256:ALL], ex[:, PAST_LEN - 256:ALL], near[:, :],
                                            ALU.add).then_inc(own, 1)
                    dve.wait_ge(own, 2 * r + 1)
                    nc.vector.tensor_reduce(stat[:, 0:1], ex[:, :], AX_X, ALU.max, negate=True).then_inc(own, 1)
                    dve.wait_ge(out_sum, r + 1)
                    nc.vector.reciprocal(stat[:, 2:3], stat[:, 1:2]).then_inc(inv_done, 1)
                    dve.wait_ge(inv_done, r + 1)
                    at_least(dve, unit_tr, r * RU)
                    nc.vector.tensor_scalar(w[:, :], cp[:, 0:ALL], stat[:, 2:3], None, ALU.mult).then_inc(w_done, 1)
                else:
                    dve.wait_ge(keep_done, r + 1)
                    nc.vector.tensor_tensor(ex[:, PAST_LEN:ALL], ex[:, PAST_LEN:ALL], late[:, :], ALU.max).then_inc(own, 1)
                    dve.wait_ge(own, 2 * r + 1)
                    nc.vector.tensor_tensor_scan(cp[:, 0:ALL][:, ::-1], ex[:, :][:, ::-1], wide(zero[:, :], [P, ALL]), 1.0,
                                                 ALU.mult, ALU.add).then_inc(own, 1)
                    dve.wait_ge(own, 2 * r + 2)
                    at_least(dve, unit_tr, r * RU)
                    nc.vector.tensor_tensor(w[:, :], cp[:, 1:ALL + 1], cp[:, 0:ALL], ALU.subtract).then_inc(w_done, 1)
                for g in range(G4):
                    b = r * G4 + g
                    dve.wait_ge(pv_mm, b + 1)
                    at_least(dve, out_ready, b)
                    nc.vector.tensor_tensor(tmp[:, :].rearrange("p (h d) -> p h d", h=HEADS),
                                            ps_o[0:R, b % 2, :].rearrange("p (h d) -> p h d", h=HEADS),
                                            wide(own_head[:, :].unsqueeze(2), [R, HEADS, HEAD_DIM]), ALU.mult
                                            ).then_inc(o_ev, 1)
                    dve.wait_ge(o_ev, b + 1)
                    nc.vector.tensor_reduce(out[:, b, :], tmp[:, :].rearrange("p (h d) -> p d h", h=HEADS), AX_X,
                                            ALU.add).then_inc(out_ready, 1)


NOT_SELECTED = -1e30
CAUSAL = -3e38
TAKEN = -3.3e38
C_Q = RWKV_IN
C_K = C_Q + HALF
C_V = C_K + HALF
C_IQ = C_V + HALF
C_IW = C_IQ + IDX_HEADS * IDX_DIM
C_IK = C_IW + IDX_HEADS


def skewed(row_block, first, width, n):
    flat = row_block.rearrange("p l -> (p l)")
    return flat[0:n * (NEAR - 1)].rearrange("(p l) -> p l", l=NEAR - 1)[:, first:first + width]


def bias_tables(nc, A, D, near_sample):
    with Phase(nc, "bias") as ph:
        rel = ph.sb("rel", [REL_BUCKETS, 2, HEADS])
        diff = ph.sb("diff", [REL_BUCKETS, HEADS])
        wide_rel = ph.sb("wide_rel", [REL_BUCKETS, HEADS, P])
        onehot = ph.sb("onehot", [REL_BUCKETS, NEAR])
        rows = ph.sb("rows", [P, HEADS, NEAR])
        ps = ph.ps("ps", [P, 2, NC_COLS])
        ld = ph.sem("ld")
        own = ph.sem("own")
        mm = ph.sem("mm")
        ev = ph.sem("ev")
        st = ph.sem("st")
        st2 = ph.sem("st2")
        block = ph.block()

        @block.sync
        def _(sp):
            sp.dma_start(rel[:, 0, :], A["rel_bias"]).then_inc(ld, 16)
            sp.dma_start(rel[:, 1, :], A["rel_bias"][REL_BUCKETS - 1:REL_BUCKETS, :]
                         .broadcast_to([REL_BUCKETS, HEADS])).then_inc(ld, 16)
            sp.dma_start(onehot[:, :], A["c_onehot"]).then_inc(ld, 16)
            sp.wait_ge(ev, HEADS)
            sp.dma_start(D.rearrange("h p l -> p h l"), rows[:, :, :]).then_inc(st, 16)
            sp.wait_ge(st, 16)
            for h in range(HEADS):
                sp.dma_start(near_sample[h * DEC_SEQ:(h + 1) * DEC_SEQ, :],
                             skewed(D[h], NEAR_TOP - 256, 256 + DEC_SEQ, DEC_SEQ)).then_inc(st2, 16)
            sp.wait_ge(st2, 16 * HEADS)

        @block.vector
        def _(dve):
            dve.wait_ge(ld, 48)
            nc.vector.tensor_tensor(diff[:, :], rel[:, 0, :], rel[:, 1, :], ALU.subtract).then_inc(own, 1)
            dve.wait_ge(own, 1)
            nc.vector.tensor_copy(wide_rel[:, :, :], wide(diff[:, :].unsqueeze(2), [REL_BUCKETS, HEADS, P])
                                  ).then_inc(own, 1)
            for h in range(HEADS):
                dve.wait_ge(mm, h + 1)
                nc.vector.tensor_copy(rows[:, h, :], ps[:, h % 2, 0:NEAR]).then_inc(ev, 1)

        @block.tensor
        def _(pe):
            pe.wait_ge(own, 2)
            for h in range(HEADS):
                at_least(pe, ev, h - 1)
                nc.tensor.matmul(ps[:, h % 2, 0:NEAR], wide_rel[:, h, :], onehot[:, :], start=True, stop=True
                                 ).then_inc(mm, 1)


def qk_norm(nc, A, proj, q_out, k_out):
    N = 2 * HEADS
    with Phase(nc, "qkn") as ph:
        x = ph.sb("x", [P, 2, 2 * HALF])
        sq = ph.sb("sq", [P, 2, 2 * HALF])
        y = ph.sb("y", [P, 2, 2 * HALF])
        gain = ph.sb("gain", [P, 2, HEAD_DIM])
        stat = ph.sb("stat", [P, 3, 2, N])
        eps = ph.sb("eps", [P, 1])
        const_ld = ph.sem("const_ld")
        ld = [ph.sem(f"ld{i}") for i in range(2)]
        st = [ph.sem(f"st{i}") for i in range(2)]
        set_up = ph.sem("set_up")
        squared = ph.sem("squared")
        summed = ph.sem("summed")
        rooted = ph.sem("rooted")
        own = ph.sem("own")
        ready = ph.sem("ready")
        block = ph.block()

        @block.sync
        def _(sp):
            for i, nm in enumerate(["dsa_q_norm_g", "dsa_k_norm_g"]):
                sp.dma_start(gain[:, i, :], A[nm].broadcast_to([P, HEAD_DIM])).then_inc(const_ld, 16)
            for t in range(TT):
                at_least(sp, ready, t - 1)
                sp.dma_start(x[0:rows_of(t), t % 2, :], proj[t * P:t * P + rows_of(t), C_Q:C_V]).then_inc(ld[t % 2], 16)

        @block.gpsimd
        def _(pool):
            for t in range(TT):
                r = rows_of(t)
                pool.wait_ge(ready, t + 1)
                pool.dma_start(q_out(t), y[0:r, t % 2, 0:HALF]).then_inc(st[t % 2], 16)
                pool.dma_start(k_out(t), y[0:r, t % 2, HALF:]).then_inc(st[t % 2], 16)
            for i in range(2):
                pool.wait_ge(st[i], 32 * ((TT + 1 - i) // 2))

        @block.scalar
        def _(act):
            act.wait_ge(set_up, 1)
            for t in range(TT):
                r = rows_of(t)
                act.wait_ge(ld[t % 2], 16 * (t // 2 + 1))
                at_least(act, summed, t - 1)
                nc.scalar.activation(sq[0:r, t % 2, :], x[0:r, t % 2, :], ACT.Square).then_inc(squared, 1)
                act.wait_ge(summed, t + 1)
                nc.scalar.activation(stat[0:r, 1, t % 2, :], stat[0:r, 0, t % 2, :], ACT.Sqrt, bias=eps[0:r, :],
                                     scale=1.0 / HEAD_DIM).then_inc(rooted, 1)

        @block.vector
        def _(dve):
            nc.vector.memset(eps[:, :], RMS_EPS).then_inc(set_up, 1)
            dve.wait_ge(const_ld, 32)
            link = Chain(dve, own)
            for t in range(TT):
                r, s = rows_of(t), t % 2
                dve.wait_ge(squared, t + 1)
                nc.vector.tensor_reduce(stat[0:r, 0, s, :], sq[0:r, s, :].rearrange("p (n d) -> p n d", n=N), AX_X,
                                        ALU.add).then_inc(summed, 1)
                dve.wait_ge(rooted, t + 1)
                link(nc.vector.reciprocal(stat[0:r, 2, s, :], stat[0:r, 1, s, :]))
                if t >= 2:
                    dve.wait_ge(st[s], 32 * (t // 2))
                yv = y[0:r, s, :].rearrange("p (n d) -> p n d", n=N)
                link(nc.vector.tensor_tensor(yv, x[0:r, s, :].rearrange("p (n d) -> p n d", n=N),
                                             wide(stat[0:r, 2, s, :].unsqueeze(2), [r, N, HEAD_DIM]), ALU.mult))
                yg = y[0:r, s, :].rearrange("p (i n d) -> p i n d", i=2, n=HEADS)
                nc.vector.tensor_tensor(yg, yg, wide(gain[0:r, :, :].unsqueeze(2), [r, 2, HEADS, HEAD_DIM]), ALU.mult
                                        ).then_inc(ready, 1)


def select_keys(nc, A, proj, pool_ik, sel, sel_sample):
    T0 = TOPK // P
    ALL = PAST_LEN + DEC_SEQ
    R = IDX_HEADS * DEC_SEQ
    with Phase(nc, "idx") as ph:
        ident = ph.sb("ident", [P, P])
        iq = ph.sb("iq", [P, PT, IDX_HEADS * IDX_DIM])
        iw = ph.sb("iw", [P, PT, IDX_HEADS])
        ik = ph.sb("ik", [P, PT, IDX_DIM])
        iqT = ph.sb("iqT", [IDX_DIM, IDX_HEADS, SEQ])
        ikT = ph.sb("ikT", [IDX_DIM, SEQ])
        relu = ph.sb("relu", [P, 2, SEQ])
        score = ph.sb("score", [P, ALL])
        picked = ph.sb("picked", [P, 2, ALL])
        best = ph.sb("best", [P, 8])
        diag = ph.sb("diag", [P, 2, P])
        late = ph.sb("late", [NS, DEC_SEQ])
        early = ph.sb("early", [P, P])
        table = ph.sb("table", [1, DEC_BATCH * N_PAGES], I32)
        pages = ph.sb("pages", [P, DEC_BATCH, N_PAGES, IDX_DIM])
        s_rows = ph.sb("s_rows", [NS, (IDX_HEADS + 1) * IDX_DIM])
        w_col = ph.sb("w_col", [R, DEC_BATCH])
        w_mask = ph.sb("w_mask", [R, DEC_BATCH, NS])
        W = ph.sb("W", [R, DEC_BATCH, NS])
        s_qT = ph.sb("s_qT", [IDX_DIM, DEC_BATCH, IDX_HEADS, DEC_SEQ])
        s_kT = ph.sb("s_kT", [IDX_DIM, NS])
        b_kT = ph.sb("b_kT", [IDX_DIM, 2, PAST_LEN])
        b_relu = ph.sb("b_relu", [R, 2, ALL])
        ps = ph.ps("ps", [P, 8, NC_COLS])
        ld = ph.sem("ld")
        table_ld = ph.sem("table_ld")
        page_ld = ph.sem("page_ld")
        tr = ph.sem("tr")
        tr_ev = ph.sem("tr_ev")
        w_ready = ph.sem("w_ready")
        s_mm = ph.sem("s_mm")
        relu_done = ph.sem("relu_done")
        added = ph.sem("added")
        b_mm = ph.sem("b_mm")
        b_relu_done = ph.sem("b_relu_done")
        b_sum = ph.sem("b_sum")
        score_copied = ph.sem("score_copied")
        own = ph.sem("own")
        picked_ready = ph.sem("picked_ready")
        st = ph.sem("st")
        st_masks = ph.sem("st_masks")
        causal_ready = ph.sem("causal_ready")
        rows_ld = [ph.sem(f"rows_ld{i}") for i in range(2)]
        n_ld = 16 * (1 + 3 + 4 + 1 + 1 + IDX_HEADS)
        n_tiles = PT - T0 + 1
        block = ph.block()

        @block.sync
        def _(sp):
            sp.dma_start(table[:, :], A["page_table"].rearrange("b n -> (b n)").unsqueeze(0)).then_inc(table_ld, 16)
            sp.dma_start(ident[:, :], A["c_ident"]).then_inc(ld, 16)
            v = proj[0:SEQ, :].rearrange("(t p) n -> p t n", p=P)
            sp.dma_start(iq[:, :, :], v[:, :, C_IQ:C_IW]).then_inc(ld, 16)
            sp.dma_start(iw[:, :, :], v[:, :, C_IW:C_IK]).then_inc(ld, 16)
            sp.dma_start(ik[:, :, :], v[:, :, C_IK:ODD_IN]).then_inc(ld, 16)
            sp.dma_start(diag[:, 0, :], A["c_causal"]).then_inc(ld, 16)
            sp.dma_start(diag[:, 1, :], A["c_unselected"]).then_inc(ld, 16)
            sp.dma_start(late[:, :], A["c_late_causal"]).then_inc(ld, 16)
            sp.dma_start(w_mask[:, :, :], A["c_w_mask"]).then_inc(ld, 16)
            sp.dma_start(s_rows[:, 0:C_IW - C_IQ], proj[SEQ:TOK, C_IQ:C_IW]).then_inc(ld, 16)
            sp.dma_start(s_rows[:, C_IW - C_IQ:], proj[SEQ:TOK, C_IK:ODD_IN]).then_inc(ld, 16)
            for h in range(IDX_HEADS):
                sp.dma_start(w_col[h * DEC_SEQ:(h + 1) * DEC_SEQ, :],
                             proj[SEQ:TOK, C_IW + h:C_IW + h + 1].rearrange("(b s) o -> s (b o)", s=DEC_SEQ),
                             allow_slow_non_contiguous=True).then_inc(ld, 16)
            sp.wait_ge(table_ld, 16)
            for n in range(DEC_BATCH * N_PAGES):
                row = sp.value_load(table[0:1, n:n + 1], min_val=0, max_val=pool_ik.shape[0] - 1)
                sp.dma_start(pages[:, n // N_PAGES, n % N_PAGES, :], pool_ik[row]).then_inc(page_ld, 16)
            sp.wait_ge(ld, n_ld)
            for t in range(T0):
                sp.dma_start(sel[t, :, t * P:(t + 1) * P], diag[:, 1, :]).then_inc(st_masks, 16)
                if t:
                    sp.wait_ge(causal_ready, 1)
                    for j in range(t):
                        sp.dma_start(sel[t, :, j * P:(j + 1) * P], early[:, :]).then_inc(st_masks, 16)
            for i in range(n_tiles):
                sp.wait_ge(picked_ready, i + 1)
                if i == 0:
                    sp.dma_start(sel_sample, picked[0:NS, 0, :]).then_inc(rows_ld[0], 16)
                else:
                    t = T0 + i - 1
                    sp.dma_start(sel[t, :, 0:(t + 1) * P], picked[:, i % 2, 0:(t + 1) * P]).then_inc(rows_ld[i % 2], 16)
            sp.wait_ge(st_masks, 16 * 3)
            for s in range(2):
                sp.wait_ge(rows_ld[s], 16 * ((n_tiles + 1 - s) // 2))

        QB = SEQ // NC_COLS

        @block.tensor
        def _(pe):
            pe.wait_ge(ld, n_ld)
            u = 0

            def unit(srcs, rows):
                nonlocal u
                at_least(pe, tr_ev, u - 1)
                for j, src in enumerate(srcs):
                    n = src.shape[0]
                    last = nc.tensor.transpose(ps[0:src.shape[1], 6 + u % 2, j * n:(j + 1) * n], src, ident[0:n, 0:n])
                last.then_inc(tr, 1)
                u += 1
            unit([s_rows[:, h * IDX_DIM:(h + 1) * IDX_DIM] for h in range(IDX_HEADS + 1)], IDX_DIM)
            for b in range(DEC_BATCH):
                if b == 0:
                    pe.wait_ge(page_ld, 16 * DEC_BATCH * N_PAGES)
                for c in range(2):
                    unit([pages[:, b, 4 * c + j, :] for j in range(4)], IDX_DIM)
                pe.wait_ge(tr_ev, u)
                at_least(pe, b_relu_done, b)
                for c in range(3):
                    n = NC_COLS if c < 2 else DEC_SEQ
                    rhs = b_kT[:, b % 2, c * NC_COLS:c * NC_COLS + n] if c < 2 else s_kT[:, b * DEC_SEQ:(b + 1) * DEC_SEQ]
                    last = nc.tensor.matmul(ps[0:R, c, 0:n], s_qT[:, b].rearrange("p h q -> p (h q)"), rhs,
                                            start=True, stop=True)
                last.then_inc(b_mm, 1)
                pe.wait_ge(b_relu_done, b + 1)
                if b == 0:
                    pe.wait_ge(w_ready, 1)
                for c in range(3):
                    n = NC_COLS if c < 2 else DEC_SEQ
                    last = nc.tensor.matmul(ps[0:NS, 3 + c, 0:n], W[:, b, :], b_relu[:, b % 2, c * NC_COLS:c * NC_COLS + n],
                                            start=(b == 0), stop=(b == DEC_BATCH - 1))
                last.then_inc(b_sum, 1)
            for h in range(IDX_HEADS):
                for c in range(QB):
                    unit([iq[:, 4 * c + j, h * IDX_DIM:(h + 1) * IDX_DIM] for j in range(4)], IDX_DIM)
            for c in range(QB):
                unit([ik[:, 4 * c + j, :] for j in range(4)], IDX_DIM)
            pe.wait_ge(tr_ev, u)
            pe.wait_ge(score_copied, 1)
            n = 0
            for t in range(T0, PT):
                for h in range(IDX_HEADS):
                    at_least(pe, relu_done, n - 1)
                    for c, (b0, m) in enumerate(key_blocks(t)):
                        last = nc.tensor.matmul(ps[:, 2 * (n % 2) + c, 0:m * P], iqT[:, h, t * P:(t + 1) * P],
                                                ikT[:, b0 * P:(b0 + m) * P], start=True, stop=True)
                    last.then_inc(s_mm, 1)
                    n += 1

        @block.scalar
        def _(act):
            u = 0

            def turned(dst, cols, view=None):
                nonlocal u
                act.wait_ge(tr, u + 1)
                src = ps[0:IDX_DIM, 6 + u % 2, 0:cols]
                nc.scalar.activation(dst, view(src) if view else src, ACT.Copy).then_inc(tr_ev, 1)
                u += 1
            act.wait_ge(tr, 1)
            nc.scalar.activation(s_kT[:, :], ps[0:IDX_DIM, 6, IDX_HEADS * NS:(IDX_HEADS + 1) * NS], ACT.Copy)
            turned(s_qT[:, :, :, :], IDX_HEADS * NS, lambda x: x.rearrange("p (h b q) -> p b h q", h=IDX_HEADS, q=DEC_SEQ))
            for b in range(DEC_BATCH):
                at_least(act, b_mm, b - 1)
                for c in range(2):
                    turned(b_kT[:, b % 2, c * NC_COLS:(c + 1) * NC_COLS], NC_COLS)
                act.wait_ge(b_mm, b + 1)
                at_least(act, b_sum, b - 1)
                for c in range(3):
                    n = NC_COLS if c < 2 else DEC_SEQ
                    last = nc.scalar.activation(b_relu[:, b % 2, c * NC_COLS:c * NC_COLS + n], ps[0:R, c, 0:n], ACT.Relu)
                last.then_inc(b_relu_done, 1)
            for h in range(IDX_HEADS):
                for c in range(QB):
                    turned(iqT[:, h, c * NC_COLS:(c + 1) * NC_COLS], NC_COLS)
            for c in range(QB):
                turned(ikT[:, c * NC_COLS:(c + 1) * NC_COLS], NC_COLS)
            n = 0
            for t in range(T0, PT):
                for h in range(IDX_HEADS):
                    act.wait_ge(s_mm, n + 1)
                    at_least(act, added, n - 1)
                    for c, (b0, m) in enumerate(key_blocks(t)):
                        last = nc.scalar.activation(relu[:, n % 2, b0 * P:(b0 + m) * P], ps[:, 2 * (n % 2) + c, 0:m * P],
                                                    ACT.Relu)
                    last.then_inc(relu_done, 1)
                    n += 1

        @block.vector
        def _(dve):
            link = Chain(dve, own)
            nc.vector.memset(early[:, :], 0.0).then_inc(causal_ready, 1)
            dve.wait_ge(ld, n_ld)
            nc.vector.tensor_tensor(W[:, :, :], w_mask[:, :, :], wide(w_col[:, :].unsqueeze(2), [R, DEC_BATCH, NS]),
                                    ALU.mult).then_inc(w_ready, 1)

            def pick(i, r, width):
                row = score[0:r, 0:width]
                for _ in range(TOPK // 8):
                    link(nc.vector.max(best[0:r, :], row))
                    link(nc.vector.match_replace(row, best[0:r, :], row, TAKEN))
                if i >= 2:
                    dve.wait_ge(rows_ld[i % 2], 16 * (i // 2))
                nc.vector.tensor_scalar(picked[0:r, i % 2, 0:width], row, TAKEN, NOT_SELECTED, ALU.not_equal,
                                        ALU.mult).then_inc(picked_ready, 1)
            dve.wait_ge(b_sum, DEC_BATCH)
            for c in range(3):
                n = NC_COLS if c < 2 else DEC_SEQ
                last = nc.vector.tensor_copy(score[0:NS, c * NC_COLS:c * NC_COLS + n], ps[0:NS, 3 + c, 0:n])
            last.then_inc(score_copied, 1)
            dve.wait_ge(score_copied, 1)
            link(nc.vector.tensor_tensor(score[0:NS, PAST_LEN:ALL], score[0:NS, PAST_LEN:ALL], late[:, :], ALU.add))
            pick(0, NS, ALL)
            n = 0
            for t in range(T0, PT):
                width = (t + 1) * P
                dve.wait_ge(picked_ready, t - T0 + 1)
                for h in range(IDX_HEADS):
                    dve.wait_ge(relu_done, n + 1)
                    at_least(dve, added, n)
                    r_ = relu[:, n % 2, 0:width]
                    if h == 0:
                        nc.vector.tensor_scalar(score[:, 0:width], r_, iw[:, t, 0:1], None, ALU.mult).then_inc(added, 1)
                    else:
                        nc.vector.scalar_tensor_tensor(score[:, 0:width], r_, iw[:, t, h:h + 1], score[:, 0:width],
                                                       ALU.mult, ALU.add).then_inc(added, 1)
                    n += 1
                dve.wait_ge(added, n)
                link(nc.vector.tensor_tensor(score[:, t * P:width], score[:, t * P:width], diag[:, 0, :], ALU.add))
                pick(t - T0 + 1, P, width)


DECAY_SCALE = 0.606531
GN_EPS = 64e-5
RW = 3 * HALF
CH = 64
W_A, W_NB, W_K, W_R, W_V, W_LW, W_G, W_BONUS = range(8)


def rwkv_inputs(nc, A, proj, rw):
    with Phase(nc, "rwi") as ph:
        ident = ph.sb("ident", [P, P])
        cur = ph.sb("cur", [P, 2, RWKV_IN])
        prev = ph.sb("prev", [P, 2, RWKV_IN])
        xs = ph.sb("xs", [P, RWKV_IN])
        mu = ph.sb("mu", [P, RWKV_IN])
        par = ph.sb("par", [P, 5, HALF])
        wa2 = ph.sb("wa2", [P, HALF])
        g2 = ph.sb("g2", [P, HALF])
        tri = ph.sb("tri", [P, P])
        small = ph.sb("small", [P, 2 * P])
        smallT = ph.sb("smallT", [P, 2, P])
        z = ph.sb("z", [P, 2, HALF])
        a = ph.sb("a", [P, HALF])
        sw = ph.sb("sw", [P, HALF])
        kk = ph.sb("kk", [P, HALF])
        k2 = ph.sb("k2", [P, HALF])
        t1 = ph.sb("t1", [P, HALF])
        t2 = ph.sb("t2", [P, HALF])
        e = ph.sb("e", [P, 3, HALF])
        cx = ph.sb("cx", [P, HALF])
        stat = ph.sb("stat", [P, 4, HEADS])
        out = ph.sb("out", [P, 2, 8, HALF])
        pt = ph.ps("pt", [P, NC_COLS])
        pm = ph.ps("pm", [P, 3, NC_COLS])
        pc = ph.ps("pc", [P, NC_COLS])
        const_ld = ph.sem("const_ld")
        ld = [ph.sem(f"ld{i}") for i in range(2)]
        zeroed = ph.sem("zeroed")
        mixed = ph.sem("mixed")
        pool_own = ph.sem("pool_own")
        small_ready = ph.sem("small_ready")
        small_tr = ph.sem("small_tr")
        small_ev = ph.sem("small_ev")
        small_mm = ph.sem("small_mm")
        z_ready = ph.sem("z_ready")
        sig_ready = ph.sem("sig_ready")
        g_ready = ph.sem("g_ready")
        lw_ready = ph.sem("lw_ready")
        cum_mm = ph.sem("cum_mm")
        cx_ready = ph.sem("cx_ready")
        e_ready = ph.sem("e_ready")
        sq_ready = ph.sem("sq_ready")
        norm2 = ph.sem("norm2")
        root = ph.sem("root")
        own = ph.sem("own")
        done = ph.sem("done")
        st = [ph.sem(f"st{i}") for i in range(2)]
        n_const = 16 * (1 + 1 + 5 + 2 + 1 + 1)
        block = ph.block()

        @block.sync
        def _(sp):
            sp.dma_start(ident[:, :], A["c_ident"]).then_inc(const_ld, 16)
            sp.dma_start(tri[:, :], A["c_chunk_tri"]).then_inc(const_ld, 16)
            sp.dma_start(mu[:, :], A["rwkv_mu"].broadcast_to([P, RWKV_IN])).then_inc(const_ld, 16)
            for i, nm in enumerate(["rwkv_w0", "rwkv_a0", "rwkv_k_k", "rwkv_k_a", "rwkv_r_k"]):
                v = A[nm].rearrange("a h d -> a (h d)") if nm == "rwkv_r_k" else A[nm]
                sp.dma_start(par[:, i, :], v.broadcast_to([P, HALF])).then_inc(const_ld, 16)
            sp.dma_start(wa2[0:64, :], A["rwkv_w2"][0]).then_inc(const_ld, 16)
            sp.dma_start(wa2[64:P, :], A["rwkv_a2"][0]).then_inc(const_ld, 16)
            sp.dma_start(g2[:, :], A["rwkv_g2"][0]).then_inc(const_ld, 16)
            def store(t):
                r, s = rows_of(t), t % 2
                sp.wait_ge(done, t + 1)
                sp.dma_start(rw[t * P:t * P + r, :, :], out[0:r, s, :, :]).then_inc(st[s], 16)

            for t in range(TT):
                if t >= 2:
                    store(t - 2)
                r, s = rows_of(t), t % 2
                at_least(sp, mixed, t - 1)
                sp.dma_start(cur[0:r, s, :], proj[t * P:t * P + r, 0:RWKV_IN]).then_inc(ld[s], 16)
                if t == 0:
                    sp.dma_start(prev[1:P, s, :], proj[0:P - 1, 0:RWKV_IN]).then_inc(ld[s], 16)
                elif t < PT:
                    sp.dma_start(prev[:, s, :], proj[t * P - 1:(t + 1) * P - 1, 0:RWKV_IN]).then_inc(ld[s], 16)
                else:
                    pv = proj[SEQ:TOK, 0:RWKV_IN].rearrange("(b s) c -> s b c", s=DEC_SEQ)
                    for q in range(DEC_SEQ):
                        sp.dma_start(prev[q:NS:DEC_SEQ, s, :], pv[q - 1] if q else A["state_rwkv_shift"][0]
                                     ).then_inc(ld[s], 16)
            store(TT - 2)
            store(TT - 1)
            for s in range(2):
                sp.wait_ge(st[s], 16 * ((TT + 1 - s) // 2))

        def loaded(t):
            return 16 * (2 * (t // 2 + 1) + (3 if t == PT else 0))

        @block.gpsimd
        def _(pool):
            nc.gpsimd.memset(prev[0:1, 0, :], 0.0).then_inc(zeroed, 1)
            pool.wait_ge(zeroed, 1)
            pool.wait_ge(const_ld, n_const)
            n = 0
            for t in range(TT):
                r, s = rows_of(t), t % 2
                pool.wait_ge(ld[s], loaded(t))
                x, y = cur[0:r, s, :], prev[0:r, s, :]
                nc.gpsimd.tensor_tensor(y, y, x, ALU.subtract).then_inc(pool_own, 1)
                pool.wait_ge(pool_own, n + 1)
                nc.gpsimd.tensor_tensor(y, y, mu[0:r, :], ALU.mult).then_inc(pool_own, 1)
                pool.wait_ge(pool_own, n + 2)
                if t:
                    pool.wait_ge(done, t)
                nc.gpsimd.tensor_tensor(xs[0:r, :], x, y, ALU.add).then_inc(mixed, 1)
                n += 2

        @block.tensor
        def _(pe):
            pe.wait_ge(const_ld, n_const)
            for t in range(TT):
                r = rows_of(t)
                pe.wait_ge(small_ready, 3 * (t + 1))
                for i in range(2):
                    last = nc.tensor.transpose(pt[:, i * P:i * P + r], small[0:r, i * P:(i + 1) * P], ident[0:r, 0:r])
                last.then_inc(small_tr, 1)
                pe.wait_ge(small_ev, t + 1)
                at_least(pe, z_ready, 2 * t)
                at_least(pe, g_ready, t)
                nc.tensor.matmul(pm[0:r, 0, :], smallT[0:64, 0, 0:r], wa2[0:64, :], start=True, stop=True)
                nc.tensor.matmul(pm[0:r, 1, :], smallT[64:P, 0, 0:r], wa2[64:P, :], start=True, stop=True)
                nc.tensor.matmul(pm[0:r, 2, :], smallT[:, 1, 0:r], g2[:, :], start=True, stop=True).then_inc(small_mm, 1)
                if t < PT:
                    pe.wait_ge(lw_ready, t + 1)
                    nc.tensor.matmul(pc[:, :], tri[:, :], out[:, t % 2, W_LW, :], start=True, stop=True).then_inc(cum_mm, 1)

        @block.scalar
        def _(act):
            for t in range(TT):
                r, s = rows_of(t), t % 2
                act.wait_ge(mixed, t + 1)
                at_least(act, small_tr, t)
                x = xs[0:r, :]
                nc.scalar.activation(small[0:r, 0:64], x[:, RW:RW + 64], ACT.Tanh).then_inc(small_ready, 1)
                nc.scalar.activation(small[0:r, 64:P], x[:, RW + 64:RW + P], ACT.Copy).then_inc(small_ready, 1)
                nc.scalar.activation(small[0:r, P:], x[:, RW + P:RWKV_IN], ACT.Sigmoid).then_inc(small_ready, 1)
                act.wait_ge(z_ready, 2 * (t + 1))
                at_least(act, done, t)
                nc.scalar.activation(sw[0:r, :], z[0:r, 0, :], ACT.Sigmoid).then_inc(sig_ready, 1)
                nc.scalar.activation(a[0:r, :], z[0:r, 1, :], ACT.Sigmoid).then_inc(sig_ready, 1)
                act.wait_ge(small_mm, t + 1)
                if t >= 2:
                    act.wait_ge(st[s], 16 * (t // 2))
                nc.scalar.activation(out[0:r, s, W_G, :], pm[0:r, 2, :], ACT.Copy).then_inc(g_ready, 1)
                nc.scalar.activation(out[0:r, s, W_V, :], x[:, 2 * HALF:RW], ACT.Copy)
                act.wait_ge(sq_ready, t + 1)
                nc.scalar.activation(t1[0:r, :], kk[0:r, :], ACT.Square).then_inc(norm2, 1)
                act.wait_ge(root, 2 * t + 1)
                nc.scalar.activation(stat[0:r, 1, :], stat[0:r, 0, :], ACT.Sqrt).then_inc(root, 1)
                if t < PT:
                    act.wait_ge(cum_mm, t + 1)
                    nc.scalar.activation(e[:, 0, :], pc[:, :], ACT.Exp).then_inc(e_ready, 1)
                    nc.scalar.activation(e[:, 1, :], pc[:, :], ACT.Exp, scale=-1.0).then_inc(e_ready, 1)
                    act.wait_ge(cx_ready, t + 1)
                    nc.scalar.activation(e[:, 2, :], cx[:, :], ACT.Exp).then_inc(e_ready, 1)
                else:
                    act.wait_ge(lw_ready, t + 1)
                    nc.scalar.activation(e[0:r, 0, :], cx[0:r, :], ACT.Exp).then_inc(e_ready, 3)

        @block.vector
        def _(dve):
            link = Chain(dve, own)
            tt = nc.vector.tensor_tensor
            stt = nc.vector.scalar_tensor_tensor
            dve.wait_ge(const_ld, n_const)
            for t in range(TT):
                r, s = rows_of(t), t % 2
                o = out[0:r, s]
                heads = lambda x: x.rearrange("p (h d) -> p h d", h=HEADS)
                pr = lambda i: par[0:r, i, :]
                dve.wait_ge(mixed, t + 1)
                rr, kx = xs[0:r, 0:HALF], xs[0:r, HALF:2 * HALF]
                dve.wait_ge(small_tr, t + 1)
                nc.vector.tensor_copy(smallT[:, :, 0:r], pt[:, 0:2 * P].rearrange("p (i c) -> p i c", i=2)[:, :, 0:r]
                                      ).then_inc(small_ev, 1)
                tt(kk[0:r, :], kx, pr(2), ALU.mult).then_inc(sq_ready, 1)
                dve.wait_ge(small_mm, t + 1)
                at_least(dve, sig_ready, 2 * t)
                for i in range(2):
                    tt(z[0:r, i, :], pm[0:r, i, :], pr(i), ALU.add).then_inc(z_ready, 1)
                dve.wait_ge(sig_ready, 2 * t + 2)
                if t >= 2:
                    dve.wait_ge(st[s], 16 * (t // 2))
                lw = o[:, W_LW, :] if t < PT else cx[0:r, :]
                nc.vector.tensor_scalar(lw, sw[0:r, :], -DECAY_SCALE, None, ALU.mult).then_inc(lw_ready, 1)
                dve.wait_ge(norm2, t + 1)
                nc.vector.tensor_reduce(stat[0:r, 0, :], heads(t1[0:r, :]), AX_X, ALU.add).then_inc(root, 1)
                dve.wait_ge(root, 2 * t + 2)
                link(nc.vector.tensor_scalar(stat[0:r, 2, :], stat[0:r, 1, :], 1e-12, None, ALU.max))
                link(nc.vector.reciprocal(stat[0:r, 3, :], stat[0:r, 2, :]))
                link(tt(heads(kk[0:r, :]), heads(kk[0:r, :]), wide(stat[0:r, 3, :].unsqueeze(2), [r, HEADS, HEAD_DIM]),
                        ALU.mult))
                link(stt(t2[0:r, :], a[0:r, :], -1.0, pr(3), ALU.add, ALU.mult))
                link(stt(k2[0:r, :], t2[0:r, :], 1.0, kx, ALU.add, ALU.mult))
                link(tt(t2[0:r, :], rr, k2[0:r, :], ALU.mult))
                link(tt(t2[0:r, :], t2[0:r, :], pr(4), ALU.mult))
                link(nc.vector.tensor_reduce(stat[0:r, 2, :], heads(t2[0:r, :]), AX_X, ALU.add))
                link(tt(heads(o[:, W_BONUS, :]), heads(xs[0:r, 2 * HALF:RW]),
                        wide(stat[0:r, 2, :].unsqueeze(2), [r, HEADS, HEAD_DIM]), ALU.mult))
                if t < PT:
                    dve.wait_ge(e_ready, 3 * t + 2)
                    tt(cx[:, :], pc[:, :], o[:, W_LW, :], ALU.subtract).then_inc(cx_ready, 1)
                    dve.wait_ge(e_ready, 3 * (t + 1))
                    link(tt(o[:, W_A, :], kk[:, :], e[:, 2, :], ALU.mult))
                    link(stt(t2[:, :], kk[:, :], -1.0, a[:, :], ALU.mult, ALU.mult))
                    link(tt(o[:, W_NB, :], t2[:, :], e[:, 1, :], ALU.mult))
                    link(tt(o[:, W_K, :], k2[:, :], e[:, 1, :], ALU.mult))
                    tt(o[:, W_R, :], rr, e[:, 0, :], ALU.mult).then_inc(done, 1)
                else:
                    dve.wait_ge(e_ready, 3 * (t + 1))
                    link(nc.vector.tensor_copy(o[:, W_A, :], kk[0:r, :]))
                    link(stt(o[:, W_NB, :], kk[0:r, :], -1.0, a[0:r, :], ALU.mult, ALU.mult))
                    link(nc.vector.tensor_copy(o[:, W_K, :], k2[0:r, :]))
                    link(nc.vector.tensor_copy(o[:, W_R, :], rr))
                    nc.vector.tensor_copy(o[:, W_LW, :], e[0:r, 0, :]).then_inc(done, 1)


def rwkv_chunks(nc, A, rw, y_out, state_out):
    HP = HEADS // 2
    TR = 4
    POW = 6
    with Phase(nc, "rwc") as ph:
        ident = ph.sb("ident", [P, P])
        eye2 = ph.sb("eye2", [P, CH])
        masks = ph.sb("masks", [P, 5, P])
        halves = ph.sb("halves", [P, 2])
        x = ph.sb("x", [P, 2, 6, HALF])
        xT = ph.sb("xT", [P, HP, TR, P])
        pr = ph.sb("pr", [P, HEADS, 4, P])
        NL = ph.sb("NL", [P, 2, 2, HEADS, P])
        Y = ph.sb("Y", [P, HEADS, 2, CH])
        RT = ph.sb("RT", [P, HP, P])
        ZN = ph.sb("ZN", [P, 2, 2, HP, CH])
        y0 = ph.sb("y0", [P, 2, HALF])
        pcs = ph.sb("pcs", [P, HP, 2])
        M = ph.sb("M", [P, HP, CH])
        Ms = ph.sb("Ms", [P, HP, CH])
        mt = ph.sb("mt", [CH, HP, P])
        ps = ph.ps("ps", [P, 8, NC_COLS])
        const_ld = ph.sem("const_ld")
        ld = [ph.sem(f"ld{i}") for i in range(2)]
        tr = ph.sem("tr")
        tr_ev = ph.sem("tr_ev")
        prod_mm = ph.sem("prod_mm")
        prod_ev = ph.sem("prod_ev")
        low_mm = ph.sem("low_mm")
        low_ev = ph.sem("low_ev")
        akv_mm = ph.sem("akv_mm")
        y_set = ph.sem("y_set")
        sq_mm = ph.sem("sq_mm")
        sq_ev = ph.sem("sq_ev")
        app_mm = ph.sem("app_mm")
        app_ev = ph.sem("app_ev")
        r_mm = ph.sem("r_mm")
        r_ev = ph.sem("r_ev")
        zn_mm = ph.sem("zn_mm")
        z_ev = ph.sem("z_ev")
        zn_ev = ph.sem("zn_ev")
        y0_mm = ph.sem("y0_mm")
        y0_ev = ph.sem("y0_ev")
        pc_ev = ph.sem("pc_ev")
        step_mm = ph.sem("step_mm")
        m_own = ph.sem("m_own")
        m_ready = ph.sem("m_ready")
        y_ready = ph.sem("y_ready")
        st = [ph.sem(f"st{i}") for i in range(2)]
        end_tr = ph.sem("end_tr")
        end_cp = ph.sem("end_cp")
        end_st = ph.sem("end_st")
        n_const = 16 * 4
        block = ph.block()
        ARR = [W_A, W_R, W_NB, W_K, W_V, W_LW]
        X_A, X_R, X_NB, X_K, X_V, X_LW = range(6)

        @block.sync
        def _(sp):
            sp.dma_start(ident[:, :], A["c_ident"]).then_inc(const_ld, 16)
            sp.dma_start(eye2[:, :], A["c_eye2"]).then_inc(const_ld, 16)
            sp.dma_start(masks[:, :, :], A["c_chunk_masks"]).then_inc(const_ld, 16)
            sp.dma_start(halves[:, :], A["c_halves"]).then_inc(const_ld, 16)
            for t in range(PT):
                at_least(sp, y_ready, t - 1)
                for i, a in enumerate(ARR):
                    sp.dma_start(x[:, t % 2, i, :], rw[t * P:(t + 1) * P, a, :]).then_inc(ld[t % 2], 16)
            sp.wait_ge(end_cp, 1)
            for g in range(2):
                sp.dma_start(state_out.rearrange("(i g) v k -> g v i k", g=2)[g], mt[:, :, g * CH:(g + 1) * CH]
                             ).then_inc(end_st, 16)
            sp.wait_ge(end_st, 32)

        @block.gpsimd
        def _(pool):
            for t in range(PT):
                pool.wait_ge(y_ready, t + 1)
                pool.dma_start(y_out[t * P:(t + 1) * P, :], y0[:, t % 2, :]).then_inc(st[t % 2], 16)
            for s in range(2):
                pool.wait_ge(st[s], 16 * PT // 2)

        def sq_count(j, g):
            full = POW - 2
            before = 4 * (j - 1)
            return before + (2 * g + 2 if j <= full else g + 1)

        @block.tensor
        def _(pe):
            mm = nc.tensor.matmul
            pe.wait_ge(const_ld, n_const)
            for t in range(PT):
                s = t % 2
                hd = lambda i, h: x[:, s, i, h * CH:(h + 1) * CH]
                pe.wait_ge(ld[s], 16 * 6 * (t // 2 + 1))
                at_least(pe, low_ev, 2 * t)
                at_least(pe, sq_ev, 18 * t)
                at_least(pe, y_ready, t)
                if t:
                    pe.wait_ge(m_ready, 2 * t + 1)
                for i in range(HP):
                    for j in range(TR):
                        last = nc.tensor.transpose(ps[:, i, j * P:(j + 1) * P], x[:, s, j, i * P:(i + 1) * P], ident[:, :])
                    last.then_inc(tr, 1)
                for h in range(HEADS):
                    rows = slice(64 * (h % 2), 64 * (h % 2) + 64)
                    pe.wait_ge(tr_ev, HP * t + h // 2 + 1)
                    n = HEADS * t + h
                    at_least(pe, prod_ev, n - 3)
                    if h == 0:
                        at_least(pe, m_ready, 2 * t)
                        at_least(pe, y_ready, t)
                    b = 4 + h % 4
                    for j, q in enumerate([2, 3]):
                        last = mm(ps[:, b, j * 2 * P:(j + 1) * 2 * P], xT[rows, h // 2, q, :],
                                  xT[rows, h // 2, 0:2, :].rearrange("p a c -> p (a c)"), start=True, stop=True)
                    last.then_inc(prod_mm, 1)
                for g in range(2):
                    rows = slice(64 * g, 64 * g + 64)
                    for i in range(HP):
                        last = mm(ps[:, g, i * P:(i + 1) * P], xT[rows, i, 0, :], xT[rows, i, 2, :], start=True, stop=True)
                    last.then_inc(low_mm, 1)
                pe.wait_ge(prod_ev, HEADS * (t + 1))
                for h in range(HEADS):
                    last = mm(ps[:, 2, h * CH:(h + 1) * CH], pr[:, h, 2, :], hd(X_V, h), start=True, stop=True)
                last.then_inc(akv_mm, 1)
                pe.wait_ge(y_set, 2 * (t + 1))
                pe.wait_ge(low_ev, 2 * (t + 1))
                for j in range(POW):
                    for g in range(2):
                        hs = range(4 * g, 4 * g + 4)
                        if j:
                            pe.wait_ge(sq_ev, 18 * t + sq_count(j, g))
                        N_ = [pr[:, h, 0, :] if j == 0 else NL[:, j % 2, 0, h, :] for h in hs]
                        L_ = [NL[:, j % 2, 1, h, :] for h in hs]
                        if j + 1 < POW:
                            for i in range(4):
                                last = mm(ps[:, 2 * g, i * P:(i + 1) * P], L_[i], N_[i], start=True, stop=True)
                            last.then_inc(sq_mm, 1)
                            if j + 2 < POW:
                                for i in range(4):
                                    last = mm(ps[:, 2 * g + 1, i * P:(i + 1) * P], N_[i], L_[i], start=True, stop=True)
                                last.then_inc(sq_mm, 1)
                        at_least(pe, app_ev, 2 * POW * t + 2 * (j - 1) + g + 1)
                        for i, h in enumerate(hs):
                            last = mm(ps[:, 4 + g, i * P:(i + 1) * P], N_[i], Y[:, h].rearrange("p a c -> p (a c)"),
                                      start=True, stop=True)
                        last.then_inc(app_mm, 1)
                pe.wait_ge(app_ev, 2 * POW * (t + 1))
                for h in range(HEADS):
                    rows = slice(64 * (h % 2), 64 * (h % 2) + 64)
                    last = mm(ps[rows, 6, h // 2 * P:(h // 2 + 1) * P], Y[:, h, 0, :], pr[:, h, 1, :], start=True, stop=True)
                last.then_inc(r_mm, 1)
                for h in range(HEADS):
                    o = ps[:, 7, h * CH:(h + 1) * CH]
                    mm(o, pr[:, h, 3, :], hd(X_V, h), start=True, stop=False)
                    last = mm(o, pr[:, h, 1, :], Y[:, h, 1, :], start=False, stop=True)
                last.then_inc(y0_mm, 1)
                for i in range(HP):
                    last = mm(ps[:, 0, 2 * i:2 * i + 2], x[:, s, X_LW, i * P:(i + 1) * P], halves[:, :], start=True, stop=True)
                for c in range(2):
                    tk = slice(64 * c, 64 * c + 64)
                    for h in range(HEADS):
                        rows = slice(64 * (h % 2), 64 * (h % 2) + 64)
                        i = h // 2
                        at = lambda q: x[tk, s, q, h * CH:(h + 1) * CH]
                        mm(ps[rows, 4 + c, i * CH:(i + 1) * CH], Y[tk, h, 0, :], at(X_NB), start=True, stop=True)
                        o = ps[rows, 4 + c, (HP + i) * CH:(HP + i + 1) * CH]
                        mm(o, at(X_K), at(X_V), start=True, stop=False)
                        last = mm(o, at(X_NB), Y[tk, h, 1, :], start=False, stop=True)
                    last.then_inc(zn_mm, 1)
                pe.wait_ge(pc_ev, t + 1)
                pe.wait_ge(r_ev, t + 1)
                for c in range(2):
                    pe.wait_ge(zn_ev, 2 * t + c + 1)
                    pe.wait_ge(m_ready, 2 * t + c + 1)
                    tk = slice(64 * c, 64 * c + 64)
                    for h in range(HEADS):
                        g, i = h % 2, h // 2
                        rows = slice(64 * g, 64 * g + 64)
                        mm(ps[rows, 2 + g, i * CH:(i + 1) * CH], ZN[rows, c, 0, i, :], M[rows, i, :], start=True, stop=True)
                        last = mm(ps[tk, g, i * CH:(i + 1) * CH], RT[rows, i, tk], M[rows, i, :], start=True, stop=True)
                    last.then_inc(step_mm, 1)
            pe.wait_ge(m_ready, 2 * PT + 1)
            pe.wait_ge(y_ready, PT)
            for i in range(HP):
                last = nc.tensor.transpose(ps[0:CH, 0, i * P:(i + 1) * P], M[:, i, :], ident[:, :])
            last.then_inc(end_tr, 1)

        @block.scalar
        def _(act):
            for t in range(PT):
                cp = lambda o, i: nc.scalar.activation(o, i, ACT.Copy)
                for i in range(HP):
                    act.wait_ge(tr, HP * t + i + 1)
                    cp(xT[:, i].rearrange("p a c -> p (a c)"), ps[:, i, :]).then_inc(tr_ev, 1)
                n = 18 * t
                for j in range(1, POW):
                    for g in range(2):
                        for k in range(2 if j + 1 < POW else 1):
                            act.wait_ge(sq_mm, n + 1)
                            if j >= 2:
                                act.wait_ge(app_mm, 2 * POW * t + 2 * (j - 2) + g + 1)
                            cp(NL[:, j % 2, k, 4 * g:4 * g + 4, :].rearrange("p a c -> p (a c)"), ps[:, 2 * g + k, :]
                               ).then_inc(sq_ev, 1)
                            n += 1
                act.wait_ge(y0_mm, t + 1)
                if t >= 2:
                    act.wait_ge(st[t % 2], 16 * (t // 2))
                cp(y0[:, t % 2, :], ps[:, 7, :]).then_inc(y0_ev, 1)
                act.wait_ge(zn_mm, 2 * t + 1)
                nc.scalar.activation(pcs[:, :, :].rearrange("p a c -> p (a c)"), ps[:, 0, 0:2 * HP], ACT.Exp).then_inc(pc_ev, 1)
                for c in range(2):
                    act.wait_ge(z_ev, 2 * t + c + 1)
                    cp(ZN[:, c, 1].rearrange("p a c -> p (a c)"), ps[:, 4 + c, HP * CH:]).then_inc(zn_ev, 1)
            act.wait_ge(end_tr, 1)
            nc.scalar.activation(mt[:, :, :].rearrange("p a c -> p (a c)"), ps[0:CH, 0, :], ACT.Copy).then_inc(end_cp, 1)

        @block.vector
        def _(dve):
            tt = nc.vector.tensor_tensor
            dve.wait_ge(const_ld, n_const)
            nc.vector.memset(M[:, :, :], 0.0).then_inc(m_ready, 1)
            own = 0
            for t in range(PT):
                s = t % 2
                for h in range(HEADS):
                    dve.wait_ge(prod_mm, HEADS * t + h + 1)
                    tt(pr[:, h].rearrange("p a c -> p (a c)"), ps[:, 4 + h % 4, :],
                       masks[:, 0:4, :].rearrange("p a c -> p (a c)"), ALU.mult).then_inc(prod_ev, 1)
                low = NL[:, 0, 1].rearrange("p (i g) c -> p g i c", g=2)
                for g in range(2):
                    dve.wait_ge(low_mm, 2 * t + g + 1)
                    tt(low[:, g], ps[:, g, :].rearrange("p (i c) -> p i c", c=P),
                       wide(masks[:, 4, :].unsqueeze(1), [P, HP, P]), ALU.mult).then_inc(low_ev, 1)
                nc.vector.tensor_copy(Y[:, :, 0, :], x[:, s, X_A, :].rearrange("p (h d) -> p h d", h=HEADS)).then_inc(y_set, 1)
                dve.wait_ge(akv_mm, t + 1)
                nc.vector.tensor_copy(Y[:, :, 1, :], ps[:, 2, :].rearrange("p (h d) -> p h d", h=HEADS)).then_inc(y_set, 1)
                dve.wait_ge(y_set, 2 * (t + 1))
                for j in range(POW):
                    for g in range(2):
                        n = 2 * POW * t + 2 * j + g
                        dve.wait_ge(app_mm, n + 1)
                        yg = Y[:, 4 * g:4 * g + 4].rearrange("p h a c -> p (h a c)")
                        at_least(dve, app_ev, n - 1)
                        tt(yg, ps[:, 4 + g, :], yg, ALU.add).then_inc(app_ev, 1)
                dve.wait_ge(r_mm, t + 1)
                tt(RT[:, :, :], ps[:, 6, :].rearrange("p (i c) -> p i c", c=P), xT[:, :, 1, :], ALU.add).then_inc(r_ev, 1)
                for c in range(2):
                    dve.wait_ge(zn_mm, 2 * t + c + 1)
                    tt(ZN[:, c, 0], ps[:, 4 + c, 0:HP * CH].rearrange("p (i k) -> p i k", k=CH),
                       wide(eye2[:, :].unsqueeze(1), [P, HP, CH]), ALU.add).then_inc(z_ev, 1)
                dve.wait_ge(pc_ev, t + 1)
                for c in range(2):
                    dve.wait_ge(step_mm, 2 * t + c + 1)
                    dve.wait_ge(zn_ev, 2 * t + c + 1)
                    for g in range(2):
                        rows = slice(64 * g, 64 * g + 64)
                        last = tt(Ms[rows, :, :], ps[rows, 2 + g, 0:HP * CH].rearrange("p (i k) -> p i k", k=CH),
                                  ZN[rows, c, 1], ALU.add)
                    last.then_inc(m_own, 1)
                    own += 1
                    dve.wait_ge(m_own, own)
                    tt(M[:, :, :], Ms[:, :, :], wide(pcs[:, :, c:c + 1], [P, HP, CH]), ALU.mult).then_inc(m_ready, 1)
                dve.wait_ge(y0_ev, t + 1)
                for g in range(2):
                    yv = y0[:, s, :].rearrange("p (i g v) -> p g i v", g=2, v=CH)[:, g]
                    last = tt(yv, ps[:, g, 0:HP * CH].rearrange("p (i v) -> p i v", v=CH), yv, ALU.add)
                last.then_inc(y_ready, 1)


def rwkv_steps(nc, A, rw, y_out, state_out):
    VH = CH // 2
    BH = DEC_BATCH * HEADS
    with Phase(nc, "rws") as ph:
        S = ph.sb("S", [P, VH, CH])
        vec = ph.sb("vec", [P, DEC_SEQ, 6, CH])
        v2 = ph.sb("v2", [P, DEC_SEQ, VH])
        u = ph.sb("u", [P, VH])
        y = ph.sb("y", [P, DEC_SEQ, VH])
        t1 = ph.sb("t1", [P, VH, CH])
        ld = ph.sem("ld")
        own = ph.sem("own")
        ready = ph.sem("ready")
        st = ph.sem("st")
        n_ld = 16 * (2 + 2 * DEC_SEQ * DEC_BATCH)
        block = ph.block()

        @block.sync
        def _(sp):
            for x in range(2):
                rows = slice(x * BH, (x + 1) * BH)
                sp.dma_start(S[rows, :, :].rearrange("p v k -> p (v k)"),
                             A["state_rwkv"][0].rearrange("b h (x v) k -> x (b h) (v k)", x=2)[x]).then_inc(ld, 16)
                for b in range(DEC_BATCH):
                    for t in range(DEC_SEQ):
                        src = rw[SEQ + b * DEC_SEQ + t, 0:6, :].rearrange("a (h d) -> h a d", h=HEADS)
                        sp.dma_start(vec[x * BH + b * HEADS:x * BH + (b + 1) * HEADS, t, :, :], src).then_inc(ld, 16)
            sp.wait_ge(ready, 1)
            for x in range(2):
                rows = slice(x * BH, (x + 1) * BH)
                sp.dma_start(state_out.rearrange("b h (x v) k -> x (b h) (v k)", x=2)[x],
                             S[rows, :, :].rearrange("p v k -> p (v k)")).then_inc(st, 16)
                for b in range(DEC_BATCH):
                    dst = y_out[SEQ + b * DEC_SEQ:SEQ + (b + 1) * DEC_SEQ, :].rearrange("t (h x v) -> x h t v", h=HEADS, x=2)[x]
                    sp.dma_start(dst, y[x * BH + b * HEADS:x * BH + (b + 1) * HEADS, :, :]).then_inc(st, 16)
            sp.wait_ge(st, 16 * 2 * (1 + DEC_BATCH))

        @block.vector
        def _(dve):
            link = Chain(dve, own)
            tt = nc.vector.tensor_tensor
            shape = [P, VH, CH]
            dve.wait_ge(ld, n_ld)
            for x in range(2):
                rows = slice(x * BH, (x + 1) * BH)
                link(nc.vector.tensor_copy(v2[rows, :, :], vec[rows, :, W_V, x * VH:(x + 1) * VH]))
            for t in range(DEC_SEQ):
                key = lambda a: wide(vec[:, t, a, :].unsqueeze(1), shape)
                link(tt(t1[:, :, :], S[:, :, :], key(W_A), ALU.mult))
                link(nc.vector.tensor_reduce(u[:, :], t1[:, :, :], AX_X, ALU.add))
                link(tt(S[:, :, :], S[:, :, :], key(W_LW), ALU.mult))
                link(tt(t1[:, :, :], wide(u[:, :].unsqueeze(2), shape), key(W_NB), ALU.mult))
                link(tt(S[:, :, :], S[:, :, :], t1[:, :, :], ALU.add))
                link(tt(t1[:, :, :], wide(v2[:, t, :].unsqueeze(2), shape), key(W_K), ALU.mult))
                link(tt(S[:, :, :], S[:, :, :], t1[:, :, :], ALU.add))
                link(tt(t1[:, :, :], S[:, :, :], key(W_R), ALU.mult))
                last = nc.vector.tensor_reduce(y[:, t, :], t1[:, :, :], AX_X, ALU.add)
                if t + 1 < DEC_SEQ:
                    link(last)
            last.then_inc(ready, 1)


def rwkv_output(nc, A, rw, y_in, mix):
    with Phase(nc, "rwo") as ph:
        y = ph.sb("y", [P, 2, HALF])
        gb = ph.sb("gb", [P, 2, 2, HALF])
        par = ph.sb("par", [P, 2, HALF])
        sq = ph.sb("sq", [P, 2, HALF])
        stat = ph.sb("stat", [P, 4, HEADS])
        eps = ph.sb("eps", [P, 1])
        const_ld = ph.sem("const_ld")
        ld = [ph.sem(f"ld{i}") for i in range(2)]
        set_up = ph.sem("set_up")
        centred = ph.sem("centred")
        squared = ph.sem("squared")
        var = ph.sem("var")
        root = ph.sem("root")
        own = ph.sem("own")
        ready = ph.sem("ready")
        st = [ph.sem(f"st{i}") for i in range(2)]
        block = ph.block()

        @block.sync
        def _(sp):
            for i, nm in enumerate(["rwkv_ln_g", "rwkv_ln_b"]):
                sp.dma_start(par[:, i, :], A[nm].broadcast_to([P, HALF])).then_inc(const_ld, 16)
            for t in range(TT):
                r, s = rows_of(t), t % 2
                if t >= 2:
                    sp.wait_ge(st[s], 16 * (t // 2))
                sp.dma_start(y[0:r, s, :], y_in[t * P:t * P + r, :]).then_inc(ld[s], 16)
                sp.dma_start(gb[0:r, s, :, :], rw[t * P:t * P + r, W_G:W_BONUS + 1, :]).then_inc(ld[s], 16)

        @block.gpsimd
        def _(pool):
            for t in range(TT):
                r, s = rows_of(t), t % 2
                pool.wait_ge(ready, t + 1)
                pool.dma_start(mix[t * P:t * P + r, :], y[0:r, s, :]).then_inc(st[s], 16)
            for s in range(2):
                pool.wait_ge(st[s], 16 * ((TT + 1 - s) // 2))

        @block.scalar
        def _(act):
            act.wait_ge(set_up, 1)
            for t in range(TT):
                r, s = rows_of(t), t % 2
                act.wait_ge(centred, t + 1)
                nc.scalar.activation(sq[0:r, s, :], y[0:r, s, :], ACT.Square).then_inc(squared, 1)
                act.wait_ge(var, t + 1)
                nc.scalar.activation(stat[0:r, 2, :], stat[0:r, 1, :], ACT.Sqrt, bias=eps[0:r, :],
                                     scale=1.0 / HEAD_DIM).then_inc(root, 1)

        @block.vector
        def _(dve):
            link = Chain(dve, own)
            tt = nc.vector.tensor_tensor
            nc.vector.memset(eps[:, :], GN_EPS).then_inc(set_up, 1)
            dve.wait_ge(const_ld, 32)
            for t in range(TT):
                r, s = rows_of(t), t % 2
                yf = y[0:r, s, :]
                yv = yf.rearrange("p (h d) -> p h d", h=HEADS)
                hw = lambda i: wide(stat[0:r, i, :].unsqueeze(2), [r, HEADS, HEAD_DIM])
                dve.wait_ge(ld[s], 32 * (t // 2 + 1))
                link(nc.vector.tensor_reduce(stat[0:r, 0, :], yv, AX_X, ALU.add))
                link(nc.vector.tensor_scalar(stat[0:r, 3, :], stat[0:r, 0, :], 1.0 / HEAD_DIM, None, ALU.mult))
                tt(yv, yv, hw(3), ALU.subtract).then_inc(centred, 1)
                dve.wait_ge(squared, t + 1)
                nc.vector.tensor_reduce(stat[0:r, 1, :], sq[0:r, s, :].rearrange("p (h d) -> p h d", h=HEADS), AX_X,
                                        ALU.add).then_inc(var, 1)
                dve.wait_ge(root, t + 1)
                link(nc.vector.reciprocal(stat[0:r, 0, :], stat[0:r, 2, :]))
                link(tt(yv, yv, hw(0), ALU.mult))
                link(tt(yf, yf, par[0:r, 0, :], ALU.mult))
                link(tt(yf, yf, par[0:r, 1, :], ALU.add))
                link(tt(yf, yf, gb[0:r, s, 1, :], ALU.add))
                tt(yf, yf, gb[0:r, s, 0, :], ALU.mult).then_inc(ready, 1)


REL_BUCKETS = 32
REL_MAX_DIST = 128


def constants():
    f32 = np.float32
    k = np.arange(P)
    s = k // S5_GROUP
    r = np.arange(HEADS * DEC_SEQ)
    c = {"c_ident": np.eye(P, dtype=f32)}
    c["c_block_mask"] = (s[None, :] >= s[:, None]).astype(f32)
    c["c_not_before"] = (k[None, :] >= k[:, None]).astype(f32)
    c["c_own_head"] = (r[:, None] // DEC_SEQ == np.arange(HEADS)[None, :]).astype(f32)
    c["c_late"] = (np.arange(DEC_SEQ)[None, :] >= k[:, None] % DEC_SEQ).astype(f32)
    past = k[None, :] > k[:, None]
    c["c_causal"] = np.where(past, CAUSAL, 0).astype(f32)
    c["c_unselected"] = np.where(past, NOT_SELECTED, 0).astype(f32)
    q = np.arange(NS) % DEC_SEQ
    c["c_late_causal"] = np.where(np.arange(DEC_SEQ)[None, :] > q[:, None], CAUSAL, 0).astype(f32)
    g = np.arange(NS) // DEC_SEQ
    c["c_w_mask"] = ((np.arange(DEC_BATCH)[None, :, None] == g[None, None, :])
                     & ((r % DEC_SEQ)[:, None, None] == q[None, None, :])).astype(f32)
    exact = REL_BUCKETS // 2
    d = np.maximum(NEAR_TOP - np.arange(NEAR), 0)
    far = exact + (np.log(np.maximum(d, 1).astype(f32) / exact) / math.log(REL_MAX_DIST / exact)
                   * (REL_BUCKETS - exact)).astype(np.int32)
    bucket = np.where(d < exact, d, np.minimum(far, REL_BUCKETS - 1))
    c["c_onehot"] = (np.arange(REL_BUCKETS)[:, None] == bucket[None, :]).astype(f32)
    same = (k[:, None] // CH) == (k[None, :] // CH)
    c["c_chunk_tri"] = (same & (k[:, None] <= k[None, :])).astype(f32)
    strict, incl = same & (k[:, None] < k[None, :]), same & (k[:, None] <= k[None, :])
    below = same & (k[:, None] > k[None, :])
    c["c_chunk_masks"] = np.stack([strict, incl, strict, incl, below], 1).astype(f32)
    c["c_halves"] = (k[:, None] // CH == np.arange(2)[None, :]).astype(f32)
    c["c_eye2"] = (k[:, None] % CH == np.arange(CH)[None, :]).astype(f32)
    return c


def column_chunks(array, n_cols):
    full = n_cols // NC_COLS * NC_COLS

    def dst(t, c, width):
        rows = array[t * P:t * P + rows_of(t), :]
        if width == NC_COLS:
            return rows[:, 0:full].rearrange("p (c n) -> c p n", n=NC_COLS)[c]
        return rows[:, full:n_cols]

    return dst


def copy_rows(nc, name, pairs):
    with Phase(nc, name) as ph:
        copied = ph.sem("copied")
        block = ph.block()

        @block.sync
        def _(sp):
            for out, src in pairs:
                sp.dma_start(out, src).then_inc(copied, 16)
            sp.wait_ge(copied, 16 * len(pairs))


def by_tokens(x):
    n = len(x.shape)
    if n == 5:
        return x.rearrange("i b t h d -> (i b t) (h d)")
    return x.rearrange("i b t d -> (i b t) d") if n == 4 else x.rearrange("b t d -> (b t) d")


def build_program(nc, A, O):
    dram = lambda name, shape: nc.dram_tensor(name, shape, F32).ap()
    ident = A["c_ident"]
    tiles = lambda a: (lambda t: a[t * P:t * P + rows_of(t), :])
    both = lambda p, s: (lambda t: token_rows(p, s, t))
    chunk_of = lambda rows: (lambda t, c: rows(t)[:, c * NC_COLS:(c + 1) * NC_COLS])
    pages = lambda x: x[0].rearrange("n p h d -> n p (h d)")
    flat = lambda x: x.rearrange("a b g n -> (a b) (g n)")
    ev = dram("ev_cols", [TOK, EVEN_IN])
    od = dram("od_cols", [TOK, ODD_IN])
    mix = [dram("mix_even", [TOK, D_MODEL]), dram("mix_odd", [TOK, D_MODEL])]
    x1, x2, x3 = (dram(n, [TOK, D_MODEL]) for n in ("x_even_mixed", "x_even_done", "x_odd_mixed"))
    x0 = both(by_tokens(A["x_prompt"]), by_tokens(A["x_sample"]))
    y = both(by_tokens(O["y_prompt"]), by_tokens(O["y_sample"]))

    def ffn(i, name, src, dst):
        conv_ffn(nc, name, src, A["ffn_norm_g"][i:i + 1], A["ffn_w_in"][i], A["ffn_conv"][i], A["ffn_w_out"][i],
                 A["state_ffn_conv"][i].rearrange("b r c -> (b r) c"), dst,
                 [(O["ffn_conv_prompt"][i, 0], 0, 2),
                  (O["ffn_conv_sample"][i].rearrange("b r c -> (b r) c"), 2, 2 + 2 * DEC_BATCH)], ident)

    with nc.cleanup_on_exit():
        project(nc, "ev_in", x0, A["ev_norm_g"], A["ev_w_in"][0], EVEN_IN, column_chunks(ev, EVEN_IN), ident)
        copy_rows(nc, "ev_new", [
            (by_tokens(O["sb_k_prompt"]), ev[0:SEQ, 2 * HALF:3 * HALF]),
            (by_tokens(O["sb_v_prompt"]), ev[0:SEQ, 3 * HALF:4 * HALF]),
            (by_tokens(O["sb_k_sample"]), ev[SEQ:TOK, 2 * HALF:3 * HALF]),
            (by_tokens(O["sb_v_sample"]), ev[SEQ:TOK, 3 * HALF:4 * HALF])])
        A5 = dict(A, o_s5_re_p=flat(O["s5_re_prompt"]), o_s5_im_p=flat(O["s5_im_prompt"]),
                  o_s5_re_s=flat(O["s5_re_sample"]), o_s5_im_s=flat(O["s5_im_sample"]))
        s5(nc, A5, ev, mix[0])
        qkv = lambda a, c, rows: [a[rows, c[i]:c[i] + HALF] for i in range(3)]
        prompt, sample = slice(0, SEQ), slice(SEQ, TOK)
        cols = (HALF, 2 * HALF, 3 * HALF)
        prompt_attention(nc, "sb", A, *qkv(ev, cols, prompt), mix[0][prompt, HALF:], False)
        sample_attention(nc, "sbs", A, *qkv(ev, cols, sample), pages(A["cache_sb_k"]), pages(A["cache_sb_v"]),
                         mix[0][sample, HALF:], False)

    with nc.cleanup_on_exit():
        project(nc, "ev_out", tiles(mix[0]), None, A["ev_w_out"][0], D_MODEL, column_chunks(x1, D_MODEL), ident,
                resid=chunk_of(x0), norm=False)
        ffn(0, "ffn0", tiles(x1), tiles(x2))

    with nc.cleanup_on_exit():
        project(nc, "od_in", tiles(x2), A["od_norm_g"], A["od_w_in"][0], ODD_IN, column_chunks(od, ODD_IN), ident)
        last_rows = od[SEQ:TOK, 0:RWKV_IN].rearrange("(b s) c -> s b c", s=DEC_SEQ)[DEC_SEQ - 1]
        copy_rows(nc, "od_new", [
            (by_tokens(O["dsa_v_prompt"]), od[prompt, C_V:C_V + HALF]),
            (by_tokens(O["dsa_v_sample"]), od[sample, C_V:C_V + HALF]),
            (by_tokens(O["dsa_idx_k_prompt"]), od[prompt, C_IK:C_IK + IDX_DIM]),
            (by_tokens(O["dsa_idx_k_sample"]), od[sample, C_IK:C_IK + IDX_DIM]),
            (O["rwkv_shift_prompt"][0], od[SEQ - 1:SEQ, 0:RWKV_IN]),
            (O["rwkv_shift_sample"][0], last_rows)])
        A6 = dict(A, near=dram("near_bias", [HEADS, P, NEAR]), near_sample=dram("near_bias_sample", [NS, 260]),
                  sel=dram("selected", [PT, P, SEQ]), sel_sample=dram("selected_sample", [NS, PAST_LEN + DEC_SEQ]))
        qn = dram("q_normed", [TOK, HALF])
        kp, ks = by_tokens(O["dsa_k_prompt"]), by_tokens(O["dsa_k_sample"])

    with nc.cleanup_on_exit():
        bias_tables(nc, A, A6["near"], A6["near_sample"])
        qk_norm(nc, A, od, tiles(qn), both(kp, ks))
        select_keys(nc, A, od, A["cache_dsa_idx_k"][0], A6["sel"], A6["sel_sample"])
        prompt_attention(nc, "dsa", A6, qn[prompt, :], kp, od[prompt, C_V:C_V + HALF], mix[1][prompt, HALF:], True)
        sample_attention(nc, "dsas", A6, qn[sample, :], ks, od[sample, C_V:C_V + HALF], pages(A["cache_dsa_k"]),
                         pages(A["cache_dsa_v"]), mix[1][sample, HALF:], True)
        rw, ry = dram("rwkv_arrays", [TOK, 8, HALF]), dram("rwkv_y", [TOK, HALF])

    with nc.cleanup_on_exit():
        rwkv_inputs(nc, A, od, rw)
        rwkv_chunks(nc, A, rw, ry, O["rwkv_prompt"][0, 0])
        rwkv_steps(nc, A, rw, ry, O["rwkv_sample"][0])
        rwkv_output(nc, A, rw, ry, mix[1][:, 0:HALF])

    with nc.cleanup_on_exit():
        project(nc, "od_out", tiles(mix[1]), None, A["od_w_out"][0], D_MODEL, column_chunks(x3, D_MODEL), ident,
                resid=chunk_of(tiles(x2)), norm=False)
        ffn(1, "ffn1", tiles(x3), y)


INPUTS = [
    "x_prompt", "x_sample", "cache_sb_k", "cache_sb_v", "cache_dsa_k", "cache_dsa_v", "cache_dsa_idx_k",
    "state_s5_re", "state_s5_im", "state_rwkv", "state_rwkv_shift", "state_ffn_conv", "page_table", "rel_bias",
    "ev_norm_g", "ev_w_in", "ev_w_out", "s5_lambda_re", "s5_lambda_im", "s5_log_step", "s5_b_re", "s5_b_im",
    "s5_c_re", "s5_c_im", "s5_d", "s5_w_glu", "s5_b_glu", "od_norm_g", "od_w_in", "od_w_out", "rwkv_mu",
    "rwkv_w0", "rwkv_w2", "rwkv_a0", "rwkv_a2", "rwkv_g2", "rwkv_k_k", "rwkv_k_a", "rwkv_r_k", "rwkv_ln_g",
    "rwkv_ln_b", "dsa_q_norm_g", "dsa_k_norm_g", "ffn_norm_g", "ffn_w_in", "ffn_conv", "ffn_w_out"]
S5_G, S5_N = HALF // S5_GROUP, 64
OUTPUTS = {
    "y_prompt": (1, SEQ, D_MODEL), "y_sample": (DEC_BATCH, DEC_SEQ, D_MODEL),
    "sb_k_prompt": (1, 1, SEQ, HEADS, HEAD_DIM), "sb_v_prompt": (1, 1, SEQ, HEADS, HEAD_DIM),
    "sb_k_sample": (1, DEC_BATCH, DEC_SEQ, HEADS, HEAD_DIM), "sb_v_sample": (1, DEC_BATCH, DEC_SEQ, HEADS, HEAD_DIM),
    "dsa_k_prompt": (1, 1, SEQ, HEADS, HEAD_DIM), "dsa_v_prompt": (1, 1, SEQ, HEADS, HEAD_DIM),
    "dsa_idx_k_prompt": (1, 1, SEQ, IDX_DIM),
    "dsa_k_sample": (1, DEC_BATCH, DEC_SEQ, HEADS, HEAD_DIM), "dsa_v_sample": (1, DEC_BATCH, DEC_SEQ, HEADS, HEAD_DIM),
    "dsa_idx_k_sample": (1, DEC_BATCH, DEC_SEQ, IDX_DIM),
    "s5_re_prompt": (1, 1, S5_G, S5_N), "s5_im_prompt": (1, 1, S5_G, S5_N),
    "s5_re_sample": (1, DEC_BATCH, S5_G, S5_N), "s5_im_sample": (1, DEC_BATCH, S5_G, S5_N),
    "rwkv_prompt": (1, 1, HEADS, HEAD_DIM, HEAD_DIM), "rwkv_shift_prompt": (1, 1, RWKV_IN),
    "rwkv_sample": (1, DEC_BATCH, HEADS, HEAD_DIM, HEAD_DIM), "rwkv_shift_sample": (1, DEC_BATCH, RWKV_IN),
    "ffn_conv_prompt": (2, 1, 2, 2 * D_FF), "ffn_conv_sample": (2, DEC_BATCH, 2, 2 * D_FF)}


def kernel(**inputs):
    import concourse.bacc as bacc
    from concourse.bass_utils import run_bass_kernel_spmd

    nc = bacc.Bacc("TRN2", target_bir_lowering=False, num_devices=1)
    arrays = {n: np.ascontiguousarray(inputs[n]) for n in INPUTS}
    arrays.update(constants())
    A = {n: nc.dram_tensor(n, a.shape, mybir.dt.from_np(a.dtype), kind="ExternalInput").ap()
         for n, a in arrays.items()}
    O = {n: nc.dram_tensor("out_" + n, s, F32, kind="ExternalOutput").ap() for n, s in OUTPUTS.items()}
    build_program(nc, A, O)
    r = run_bass_kernel_spmd(nc, [arrays], core_ids=[0])
    return tuple(r.results[0]["out_" + n] for n in OUTPUTS)
```

```python
import math
from contextlib import ExitStack

import numpy as np
import concourse.bass as bass
from concourse import mybir

ALU = mybir.AluOpType
ACT = mybir.ActivationFunctionType
AX_X = mybir.AxisListType.X
F32 = mybir.dt.float32
I32 = mybir.dt.int32
F32R = mybir.dt.float32r

P = 128
D_MODEL = 1024
SEQ = 1024
DEC_BATCH = 8
DEC_SEQ = 4
NS = DEC_BATCH * DEC_SEQ
PAST_LEN = 1024
PAGE = 128
N_PAGES = PAST_LEN // PAGE
HEADS = 8
HEAD_DIM = 64
HALF = D_MODEL // 2
TOK = SEQ + NS
PT = SEQ // P
TT = PT + 1
KT = D_MODEL // P
EVEN_IN = 4 * HALF
RWKV_IN = 3 * HALF + 64 + 64 + 128
IDX_HEADS = 8
IDX_DIM = 32
ODD_IN = RWKV_IN + 3 * HALF + IDX_HEADS * IDX_DIM + IDX_HEADS + IDX_DIM
D_FF = 2816
FT = D_FF // P
TOPK = 256
RMS_EPS = 1e-6
NC_COLS = 512
SCALE = HEAD_DIM ** -0.5


def rows_of(t):
    return P if t < PT else NS


def at_least(eng, sem, value):
    if not isinstance(value, int) or value > 0:
        eng.wait_ge(sem, value)


class Phase:

    def __init__(self, nc, name):
        self.nc, self.name, self.ctx = nc, name, ExitStack()

    def __enter__(self):
        self.ctx.__enter__()
        return self

    def __exit__(self, *e):
        return self.ctx.__exit__(*e)

    def sb(self, name, shape, dt=F32):
        return self.ctx.enter_context(self.nc.sbuf_tensor(f"{self.name}_{name}", shape, dt))

    def ps(self, name, shape, dt=F32):
        return self.ctx.enter_context(self.nc.psum_tensor(f"{self.name}_{name}", shape, dt))

    def sem(self, name):
        return self.nc.alloc_semaphore(name=f"{self.name}_{name}")

    def block(self):
        return self.ctx.enter_context(self.nc.Block())


def high_part(nc, out, x):
    return nc.vector.tensor_copy(out, x)


def parts_product(nc, out, a, b, start, stop):
    for i, (p, q) in enumerate([(0, 0), (0, 1), (1, 0)]):
        last = nc.tensor.matmul(out, a[p], b[q], start=start and i == 0, stop=stop and i == 2)
    return last


class Chain:

    def __init__(self, eng, sem):
        self.eng, self.sem, self.n = eng, sem, 0

    def __call__(self, ins):
        self.n += 1
        ins.then_inc(self.sem, 1)
        self.eng.wait_ge(self.sem, self.n)


def token_rows(prompt, sample, t):
    return prompt[t * P:(t + 1) * P, :] if t < PT else sample[:, :]


NX = 4
NORM_ROWS = NX + 4


def normed_transpose(nc, ph, src, gain, xT, ident, ident_src, xT_ready, norm=True, spare=None):
    if spare is None:
        spare = ph.sb("norm_rows", [P, NORM_ROWS if norm else NX, D_MODEL])[:, :, :]
    xin = spare[:, 0:NX, :]
    if norm:
        xn, sq, gain_b = spare[:, NX:NX + 2, :], spare[:, NX + 2, :], spare[:, NX + 3, :]
    stat = ph.sb("stat", [P, TT, 4])
    epsc = ph.sb("epsc", [P, 1])
    trp = ph.ps("trp", [P, 2, NC_COLS])
    const_ld = ph.sem("const_ld")
    x_ld = [ph.sem(f"x_ld{i}") for i in range(NX)]
    ss_ready = ph.sem("ss_ready")
    root_ready = ph.sem("root_ready")
    inv_ready = ph.sem("inv_ready")
    xn_ready = ph.sem("xn_ready")
    tr_ready = ph.sem("tr_ready")
    eps_set = ph.sem("eps_set")
    high_ready = ph.sem("high_ready")

    def sync_start(sp):
        sp.dma_start(ident[:, :], ident_src).then_inc(const_ld, 16)
        if norm:
            sp.dma_start(gain_b, gain.broadcast_to([P, D_MODEL])).then_inc(const_ld, 16)

    def sync_part(sp, tiles=range(TT)):
        for t in tiles:
            if t >= NX:
                if norm:
                    sp.wait_ge(xn_ready, t - NX + 1)
                else:
                    sp.wait_ge(tr_ready, 2 * (t - NX + 1))
            sp.dma_start(xin[0:rows_of(t), t % NX, :], src(t)).then_inc(x_ld[t % NX], 16)

    def scalar_part(act, tiles=range(TT)):
        if not norm:
            return
        for t in tiles:
            if t == 0:
                act.wait_ge(eps_set, 1)
            r = rows_of(t)
            act.wait_ge(x_ld[t % NX], 16 * (t // NX + 1))
            at_least(act, ss_ready, t)
            nc.scalar.activation(sq[0:r], xin[0:r, t % NX, :], ACT.Square,
                                 accum_out=stat[0:r, t, 0:1]).then_inc(ss_ready, 1)
            act.wait_ge(ss_ready, t + 1)
            nc.scalar.activation(stat[0:r, t, 1:2], stat[0:r, t, 0:1], ACT.Sqrt, bias=epsc[0:r, :],
                                 scale=1.0 / D_MODEL).then_inc(root_ready, 1)

    def vector_start(dve):
        if norm:
            nc.vector.memset(epsc[:, :], RMS_EPS).then_inc(eps_set, 1)
        dve.wait_ge(const_ld, 32 if norm else 16)

    def vector_part(dve, tiles=range(TT)):
        for t in tiles:
            r = rows_of(t)
            if norm:
                dve.wait_ge(root_ready, t + 1)
                nc.vector.reciprocal(stat[0:r, t, 2:3], stat[0:r, t, 1:2]).then_inc(inv_ready, 1)
                dve.wait_ge(inv_ready, t + 1)
                if t >= 2:
                    dve.wait_ge(tr_ready, 2 * (t - 1))
                nc.vector.scalar_tensor_tensor(xn[0:r, t % 2, :], xin[0:r, t % NX, :], stat[0:r, t, 2:3],
                                               gain_b[0:r], ALU.mult, ALU.mult).then_inc(xn_ready, 1)
            for h in range(2):
                dve.wait_ge(tr_ready, 2 * t + h + 1)
                high, low = (xT[:, i, 4 * h:4 * h + 4, t * P:t * P + r] for i in range(2))
                turned = trp[:, h, :].rearrange("p (k c) -> p k c", c=P)[:, :, 0:r]
                high_part(nc, high, turned).then_inc(high_ready, 1)
                dve.wait_ge(high_ready, 2 * t + h + 1)
                nc.vector.tensor_tensor(low, turned, high, ALU.subtract).then_inc(xT_ready, 1)

    def tensor_part(pe, tiles=range(TT)):
        xs = xn if norm else xin
        for t in tiles:
            r = rows_of(t)
            if t == 0:
                pe.wait_ge(const_ld, 32 if norm else 16)
            if norm:
                pe.wait_ge(xn_ready, t + 1)
            else:
                pe.wait_ge(x_ld[t % NX], 16 * (t // NX + 1))
            for h in range(2):
                at_least(pe, xT_ready, 2 * (t - 1) + h + 1)
                for k in range(4):
                    last = nc.tensor.transpose(trp[:, h, k * P:k * P + r],
                                               xs[0:r, t % (2 if norm else NX), (4 * h + k) * P:(4 * h + k + 1) * P], ident[0:r, 0:r])
                last.then_inc(tr_ready, 1)

    return const_ld, sync_start, sync_part, scalar_part, vector_start, vector_part, tensor_part


def project(nc, name, src, gain, weight, n_cols, dst, ident_src, resid=None, norm=True):
    full = n_cols // NC_COLS
    rest = n_cols - full * NC_COLS
    NB = 3
    with Phase(nc, name) as ph:
        xT = ph.sb("xT", [P, 2, KT, TOK], F32R)
        w = ph.sb("w", [P, 2, KT, NC_COLS])
        w_high = ph.sb("w_high", [P, 2, KT, NC_COLS], F32R)
        w_low = ph.sb("w_low", [P, 2, KT, NC_COLS], F32R)
        stage = ph.sb("stage", [P, NB, NC_COLS])
        res = ph.sb("res", [P, NB, NC_COLS]) if resid else None
        acc = ph.ps("acc", [P, NB, NC_COLS])
        xT_ready = ph.sem("xT_ready")
        w_ld = [ph.sem(f"w_ld{i}") for i in range(2)]
        high_done = ph.sem("high_done")
        low_done = ph.sem("low_done")
        shared_done = ph.sem("shared_done")
        mm_done = ph.sem("mm_done")
        ev_done = ph.sem("ev_done")
        st_done = [ph.sem(f"st_done{i}") for i in range(NB)]
        r_ld = [ph.sem(f"r_ld{i}") for i in range(NB)]
        ident = ph.sb("ident", [P, P])
        _, s_start, t_sync, t_scalar, t_start, t_vector, t_tensor = normed_transpose(
            nc, ph, src, gain, xT, ident, ident_src, xT_ready, norm)
        w_view = weight[:, 0:full * NC_COLS].rearrange("(k p) (c n) -> c p k n", p=P, n=NC_COLS)
        loop_end = full - full % 2
        tail = [(c, NC_COLS) for c in range(loop_end, full)] + ([(full, rest)] if rest else [])
        steps = full * TT + (TT if rest else 0)
        block = ph.block()

        def led(early, late):
            for t in range(TT + NB):
                if t < TT:
                    early(t)
                if t >= NB:
                    late(t - NB)

        def load_chunk(eng, c, s, width):
            at_least(eng, low_done, c - 1)
            src_w = w_view[c] if width == NC_COLS else \
                weight[:, full * NC_COLS:n_cols].rearrange("(k p) n -> p k n", p=P)
            eng.dma_start(w[:, s, :, 0:width], src_w).then_inc(w_ld[s], 16)

        def high_parts(dve, c, s, width):
            dve.wait_ge(w_ld[s], (c // 2 + 1) * 16 if isinstance(c, int) else (c - s) * 8 + 16)
            at_least(dve, mm_done, (c - 1) * TT)
            high_part(nc, w_high[:, s, :, 0:width], w[:, s, :, 0:width]).then_inc(high_done, 1)

        def low_parts(pool, c, s, width, k=slice(0, KT)):
            pool.wait_ge(high_done, c + 1)
            nc.gpsimd.tensor_tensor(w_low[:, s, k, 0:width], w[:, s, k, 0:width], w_high[:, s, k, 0:width],
                                    ALU.subtract).then_inc(low_done, 1)

        SHARED = slice(0, KT * 3 // 8), slice(KT * 3 // 8, KT)

        @block.gpsimd
        def _(pool):
            for c in range(2):
                load_chunk(pool, c, c, NC_COLS)
            low_parts(pool, 0, 0, NC_COLS, SHARED[0])
            low_parts(pool, 1, 1, NC_COLS)
            if loop_end > 2:
                with pool.Fori(1, loop_end // 2) as i:
                    for s in range(2):
                        load_chunk(pool, i * 2 + s if s else i * 2, s, NC_COLS)
                        low_parts(pool, i * 2 + s if s else i * 2, s, NC_COLS)
            for c, width in tail:
                load_chunk(pool, c, c % 2, width)
                low_parts(pool, c, c % 2, width)

        def store_chunk(eng, c, width, tiles=range(TT)):
            for t in tiles:
                eng.wait_ge(ev_done, c * TT + t + 1)
                eng.dma_start(dst(t, c, width), stage[0:rows_of(t), t % NB, 0:width]).then_inc(st_done[t % NB], 16)

        @block.sync
        def _(sp):
            s_start(sp)
            if resid:
                for t in range(NB):
                    t_sync(sp, [t])
                    sp.dma_start(res[0:rows_of(t), t, :], resid(t, 0)).then_inc(r_ld[t], 16)
                for n in range(full * TT):
                    c, t = n // TT, n % TT
                    if n + NB < TT:
                        t_sync(sp, [n + NB])
                    sp.wait_ge(ev_done, n + 1)
                    sp.dma_start(dst(t, c, NC_COLS), stage[0:rows_of(t), t % NB, :]).then_inc(st_done[t % NB], 16)
                    if n + NB < full * TT:
                        c2, t2 = (n + NB) // TT, (n + NB) % TT
                        sp.dma_start(res[0:rows_of(t2), t2 % NB, :], resid(t2, c2)).then_inc(r_ld[t2 % NB], 16)
            else:
                led(lambda t: t_sync(sp, [t]), lambda t: store_chunk(sp, 0, NC_COLS, [t]))
                store_chunk(sp, 1, NC_COLS)
                if loop_end > 2:
                    with sp.Fori(2, loop_end) as c:
                        store_chunk(sp, c, NC_COLS)
                for c, width in tail:
                    store_chunk(sp, c, width)
            for b in range(NB):
                sp.wait_ge(st_done[b], 16 * (steps // NB))

        def evacuate(act, c, width, tiles=range(TT)):
            for t in tiles:
                r = rows_of(t)
                act.wait_ge(mm_done, c * TT + t + 1)
                if not isinstance(c, int) or c > 0 or t >= NB:
                    act.wait_ge(st_done[t % NB], (c * (TT // NB) + t // NB) * 16)
                nc.scalar.activation(stage[0:r, t % NB, 0:width], acc[0:r, t % NB, 0:width],
                                     ACT.Copy).then_inc(ev_done, 1)

        @block.scalar
        def _(act):
            if resid:
                t_scalar(act)
                return
            led(lambda t: t_scalar(act, [t]), lambda t: evacuate(act, 0, NC_COLS, [t]))
            evacuate(act, 1, NC_COLS)
            if loop_end > 2:
                with act.Fori(2, loop_end) as c:
                    evacuate(act, c, NC_COLS)
            for c, width in tail:
                evacuate(act, c, width)

        @block.vector
        def _(dve):
            t_start(dve)
            high_parts(dve, 0, 0, NC_COLS)
            dve.wait_ge(high_done, 1)
            k = SHARED[1]
            nc.vector.tensor_tensor(w_low[:, 0, k, :], w[:, 0, k, :], w_high[:, 0, k, :], ALU.subtract
                                    ).then_inc(shared_done, 1)
            t_vector(dve, [0])
            if resid:
                t_vector(dve, range(1, NB))
                for n in range(full * TT):
                    if n + NB < TT:
                        t_vector(dve, [n + NB])
                    if n + NB == TT:
                        high_parts(dve, 1, 1, NC_COLS)
                    t = n % TT
                    r = rows_of(t)
                    dve.wait_ge(mm_done, n + 1)
                    dve.wait_ge(r_ld[t % NB], 16 * (n // NB + 1))
                    at_least(dve, st_done[t % NB], 16 * (n // NB))
                    nc.vector.tensor_tensor(stage[0:r, t % NB, :], acc[0:r, t % NB, :], res[0:r, t % NB, :],
                                            ALU.add).then_inc(ev_done, 1)
                return
            t_vector(dve, range(1, TT))
            high_parts(dve, 1, 1, NC_COLS)
            if loop_end > 2:
                with dve.Fori(1, loop_end // 2) as i:
                    high_parts(dve, i * 2, 0, NC_COLS)
                    high_parts(dve, i * 2 + 1, 1, NC_COLS)
            for c, width in tail:
                high_parts(dve, c, c % 2, width)

        def products(pe, c, s, width):
            if not isinstance(c, int) or c > 0:
                pe.wait_ge(low_done, c + 1)
            for t in range(TT):
                r = rows_of(t)
                if isinstance(c, int) and c == 0:
                    if t == 0:
                        t_tensor(pe, [0, 1])
                        pe.wait_ge(low_done, 1)
                        pe.wait_ge(shared_done, 1)
                    elif t + 1 < TT:
                        t_tensor(pe, [t + 1])
                    pe.wait_ge(xT_ready, 2 * t + 2)
                at_least(pe, ev_done, c * TT + t + 1 - NB)
                for k in range(KT):
                    last = parts_product(nc, acc[0:r, t % NB, 0:width], [xT[:, i, k, t * P:t * P + r] for i in range(2)],
                                         [w_high[:, s, k, 0:width], w_low[:, s, k, 0:width]], k == 0, k == KT - 1)
                last.then_inc(mm_done, 1)

        @block.tensor
        def _(pe):
            products(pe, 0, 0, NC_COLS)
            products(pe, 1, 1, NC_COLS)
            if loop_end > 2:
                with pe.Fori(1, loop_end // 2) as i:
                    products(pe, i * 2, 0, NC_COLS)
                    products(pe, i * 2 + 1, 1, NC_COLS)
            for c, width in tail:
                products(pe, c, c % 2, width)


def conv_ffn(nc, name, src, gain, w_in, conv_w, w_out, state, dst, tails, ident_src):
    GB = SEQ + 2
    SB = 2 + DEC_SEQ
    PADDED = GB + DEC_BATCH * SB
    TAPPED = PADDED - 2
    NR = 2 * DEC_BATCH + 3
    NT = 2 + 2 * DEC_BATCH
    THIRD = TOK // 3
    NG = 4
    EV = 4
    with Phase(nc, name + "_act") as outer:
        actT = outer.sb("actT", [P, FT, PADDED])
        act_flat = actT[:, :, :].rearrange("p f c -> p (f c)")
        with Phase(nc, name + "_up") as ph:
            xT = ph.sb("xT", [P, 2, KT, TOK], F32R)
            w = ph.sb("w", [P, 2, KT, P])
            w_high = ph.sb("w_high", [P, 2, KT, P], F32R)
            w_low = ph.sb("w_low", [P, 2, KT, P], F32R)
            rows = act_flat[0:32, NORM_ROWS * D_MODEL:NORM_ROWS * D_MODEL + 2 * D_FF]
            new_rows = ph.sb("new_rows", [32, NG, NC_COLS])
            cols = ph.sb("cols", [P, 2 * FT, NT + 3])
            hb = ph.sb("hb", [P, 2, PADDED])
            cb = ph.sb("cb", [P, PADDED])
            hp = ph.ps("hp", [P, 2, 3, NC_COLS])
            xT_ready = ph.sem("xT_ready")
            rows_ld = ph.sem("rows_ld")
            cols_tr = ph.sem("cols_tr")
            cols_ready = ph.sem("cols_ready")
            high_done = [ph.sem("gate_high"), ph.sem("value_high")]
            low_done = [ph.sem("gate_low"), ph.sem("value_low")]
            w_ld = [ph.sem(f"w_ld{i}") for i in range(2)]
            mm_done = [ph.sem("gate_mm"), ph.sem("value_mm")]
            ev_done = [ph.sem("gate_ev"), ph.sem("value_ev")]
            conv_done = [ph.sem("gate_conv"), ph.sem("value_conv")]
            silu_done = ph.sem("silu_done")
            act_done = ph.sem("act_done")
            pad_set = ph.sem("pad_set")
            dve_own = ph.sem("dve_own")
            tail_tr = ph.sem("tail_tr")
            tail_ready = ph.sem("tail_ready")
            tail_st = [ph.sem(f"tail_st{i}") for i in range(NG)]
            ident = ph.sb("ident", [P, P])
            const_ld, s_start, t_sync, t_scalar, t_start, t_vector, t_tensor = normed_transpose(
                nc, ph, src, gain, xT, ident, ident_src, xT_ready, spare=act_flat[:, 0:NORM_ROWS * D_MODEL].rearrange("p (i c) -> p i c", i=NORM_ROWS))
            w_view = w_in.rearrange("(k p) (f n) -> f p k n", p=P, n=P)
            block = ph.block()

            def load(eng, j, q):
                at_least(eng, low_done[q], j)
                eng.dma_start(w[:, q], w_view[j + q * FT]).then_inc(w_ld[q], 16)

            def high_parts(dve, j, q):
                dve.wait_ge(w_ld[q], j * 16 + 16)
                at_least(dve, mm_done[q], j)
                high_part(nc, w_high[:, q], w[:, q]).then_inc(high_done[q], 1)

            def low_parts(pool, j, q):
                pool.wait_ge(high_done[q], j + 1)
                nc.gpsimd.tensor_tensor(w_low[:, q], w[:, q], w_high[:, q], ALU.subtract).then_inc(low_done[q], 1)

            @block.gpsimd
            def _(pool):
                for q in range(2):
                    load(pool, 0, q)
                for q in range(2):
                    low_parts(pool, 0, q)
                    load(pool, 1, q)
                with pool.Fori(1, FT - 1) as j:
                    for q in range(2):
                        low_parts(pool, j, q)
                        load(pool, j + 1, q)
                for q in range(2):
                    low_parts(pool, FT - 1, q)

            @block.sync
            def _(sp):
                s_start(sp)
                sp.dma_start(rows[0:2 * DEC_BATCH, :], state).then_inc(rows_ld, 16)
                sp.dma_start(rows[2 * DEC_BATCH:NR, :], conv_w).then_inc(rows_ld, 16)
                t_sync(sp)
                for g in range(11):
                    sp.wait_ge(tail_ready, g + 1)
                    for dram, r0, r1 in tails:
                        sp.dma_start(dram[:, g * NC_COLS:(g + 1) * NC_COLS], new_rows[r0:r1, g % NG, :]
                                     ).then_inc(tail_st[g % NG], 16)
                for g in range(NG):
                    sp.wait_ge(tail_st[g], 16 * len(tails) * ((11 - g + NG - 1) // NG))

            def up(pe, j, first=False):
                order = [(q, b) for q in range(2) for b in range(3)]
                if first:
                    order = [(q, b) for b in range(3) for q in range(2)]
                for q, b in order:
                    c0, n = b * THIRD, THIRD
                    if first and q == 0:
                        t_tensor(pe, range(3 * b, 3 * b + 3))
                        pe.wait_ge(xT_ready, 6 * (b + 1))
                    if b == 0:
                        pe.wait_ge(low_done[q], j + 1)
                        at_least(pe, ev_done[q], j * EV)
                    for k in range(KT):
                        last = parts_product(nc, hp[:, q, b, 0:n], [w_high[:, q, k, :], w_low[:, q, k, :]],
                                             [xT[:, i, k, c0:c0 + n] for i in range(2)], k == 0, k == KT - 1)
                    if b == 2:
                        last.then_inc(mm_done[q], 1)

            @block.tensor
            def _(pe):
                pe.wait_ge(rows_ld, 32)
                pe.wait_ge(const_ld, 32)
                for f in range(2 * FT):
                    h, c = f // FT, f % FT
                    last = nc.tensor.transpose(hp[:, h, 0, c * NR:(c + 1) * NR], rows[0:NR, f * P:(f + 1) * P],
                                               ident[0:NR, 0:NR])
                last.then_inc(cols_tr, 1)
                pe.wait_ge(cols_ready, 4)
                up(pe, 0, first=True)
                with pe.Fori(1, FT) as j:
                    up(pe, j)
                pe.wait_ge(act_done, FT)
                for g in range(11):
                    at_least(pe, tail_ready, g - 5)
                    for f in range(4):
                        last = nc.tensor.transpose(hp[0:NT, g % 6 // 3, g % 3, f * P:(f + 1) * P],
                                                   cols[:, 4 * g + f, 0:NT], ident[:, :])
                    last.then_inc(tail_tr, 1)

            def evacuate(act, j):
                for q in range(2):
                    act.wait_ge(mm_done[q], j + 1)
                    at_least(act, conv_done[q], j)
                    for b in range(3):
                        c1 = min((b + 1) * THIRD, SEQ)
                        nc.scalar.activation(hb[:, q, 2 + b * THIRD:2 + c1], hp[:, q, b, 0:c1 - b * THIRD],
                                             ACT.Copy).then_inc(ev_done[q], 1)
                    new = hb[:, q, GB:PADDED].rearrange("p (b r) -> p b r", r=SB)[:, :, 2:SB]
                    nc.scalar.activation(new, hp[:, q, 2, THIRD - NS:THIRD].rearrange("p (b r) -> p b r", r=DEC_SEQ),
                                         ACT.Copy).then_inc(ev_done[q], 1)
                act.wait_ge(conv_done[0], j + 1)
                nc.scalar.activation(actT[:, j, 0:TAPPED], actT[:, j, 0:TAPPED], ACT.Silu).then_inc(silu_done, 1)

            @block.scalar
            def _(act):
                t_scalar(act)
                evacuate(act, 0)
                with act.Fori(1, FT) as j:
                    evacuate(act, j)

            OWN = 6

            def combine(dve, j, last=False):
                for q in range(2):
                    if not last:
                        high_parts(dve, j + 1, q)
                    f = j + q * FT
                    kept = hb[:, q, GB:PADDED].rearrange("p (b r) -> p b r", r=SB)
                    dve.wait_ge(ev_done[q], j * EV + EV)
                    nc.vector.tensor_copy(kept[:, :, 0:2], cols[:, f, 0:2 * DEC_BATCH]
                                          .rearrange("p (b r) -> p b r", r=2)).then_inc(dve_own, 1)
                    dve.wait_ge(dve_own, j * OWN + 3 * q + 1)
                    y = cb[:, 0:TAPPED] if q else actT[:, j, 0:TAPPED]
                    tap = [cols[:, f, NT + i:NT + i + 1] for i in range(3)]
                    nc.vector.tensor_scalar(y, hb[:, q, 0:TAPPED], tap[0], None, ALU.mult).then_inc(dve_own, 1)
                    nc.vector.tensor_copy(cols[:, f, 0:2], hb[:, q, SEQ:SEQ + 2])
                    nc.vector.tensor_copy(cols[:, f, 2:NT].rearrange("p (b r) -> p b r", r=2), kept[:, :, DEC_SEQ:SB])
                    dve.wait_ge(dve_own, j * OWN + 3 * q + 2)
                    nc.vector.scalar_tensor_tensor(y, hb[:, q, 1:1 + TAPPED], tap[1], y,
                                                   ALU.mult, ALU.add).then_inc(dve_own, 1)
                    dve.wait_ge(dve_own, j * OWN + 3 * q + 3)
                    nc.vector.scalar_tensor_tensor(y, hb[:, q, 2:2 + TAPPED], tap[2], y,
                                                   ALU.mult, ALU.add).then_inc(conv_done[q], 1)
                dve.wait_ge(silu_done, j + 1)
                dve.wait_ge(conv_done[1], j + 1)
                nc.vector.tensor_tensor(actT[:, j, 0:TAPPED], actT[:, j, 0:TAPPED], cb[:, 0:TAPPED],
                                        ALU.mult).then_inc(act_done, 1)

            @block.vector
            def _(dve):
                for q in range(2):
                    last = nc.vector.memset(hb[:, q, 0:2], 0.0)
                last.then_inc(pad_set, 1)
                t_start(dve)
                dve.wait_ge(cols_tr, 1)
                for h in range(2):
                    turned = hp[:, h, 0, 0:FT * NR].rearrange("p (f r) -> p f r", r=NR)
                    for to, at in [(slice(0, 2 * DEC_BATCH), slice(0, 2 * DEC_BATCH)),
                                   (slice(NT, NT + 3), slice(2 * DEC_BATCH, NR))]:
                        nc.vector.tensor_copy(cols[:, h * FT:(h + 1) * FT, to], turned[:, :, at]).then_inc(cols_ready, 1)
                t_vector(dve, [0])
                for q in range(2):
                    high_parts(dve, 0, q)
                t_vector(dve, range(1, TT))
                dve.wait_ge(pad_set, 1)
                dve.wait_ge(cols_ready, 4)
                combine(dve, 0)
                with dve.Fori(1, FT - 1) as j:
                    combine(dve, j)
                combine(dve, FT - 1, last=True)
                for g in range(11):
                    dve.wait_ge(tail_tr, g + 1)
                    at_least(dve, tail_st[g % NG], 16 * len(tails) * (g // NG))
                    nc.vector.tensor_copy(new_rows[0:NT, g % NG, :],
                                          hp[0:NT, g % 6 // 3, g % 3, :]).then_inc(tail_ready, 1)

        NB = 3
        NSTG = 2
        NCH = D_MODEL // NC_COLS
        PIECE = 2
        NP = FT // PIECE
        NR2 = 2
        UNIT = 6
        units = [(k, min(k + UNIT, FT)) for k in range(0, FT, UNIT)]
        NU = len(units)
        with Phase(nc, name + "_down") as ph:
            raw = ph.sb("raw", [P, NR2, PIECE, NC_COLS])
            w_high = ph.sb("w_high", [P, FT, NC_COLS], F32R)
            w_low = ph.sb("w_low", [P, FT, NC_COLS], F32R)
            a_high = ph.sb("a_high", [P, 2, UNIT, P], F32R)
            a_low = ph.sb("a_low", [P, 2, UNIT, P], F32R)
            stage = ph.sb("stage", [P, NSTG, NC_COLS])
            acc = ph.ps("acc", [P, NB, NC_COLS])
            w_ld = [ph.sem(f"w_ld{i}") for i in range(NR2)]
            w_high_done = ph.sem("w_high_done")
            w_low_done = ph.sem("w_low_done")
            a_high_done = ph.sem("a_high_done")
            a_low_done = ph.sem("a_low_done")
            unit_mm = ph.sem("unit_mm")
            ev_done = ph.sem("ev_done")
            st_done = [ph.sem(f"st_done{i}") for i in range(NSTG)]
            r_ld = [ph.sem(f"r_ld{i}") for i in range(NSTG)]
            block = ph.block()
            groups = [(c, t) for c in range(NCH) for t in range(TT)]
            w_view = w_out.rearrange("(k p) (c n) -> c p k n", p=P, n=NC_COLS)
            piece = lambda p: slice(p * PIECE, (p + 1) * PIECE)
            pieces_of = lambda u: range(units[u][0] // PIECE, units[u][1] // PIECE)

            @block.sync
            def _(sp):
                def load_piece(c, p):
                    m = c * NP + p
                    at_least(sp, w_low_done, m - NR2 + 1)
                    sp.dma_start(raw[:, m % NR2], w_view[c, :, piece(p), :]).then_inc(w_ld[m % NR2], 16)

                def load_res(n):
                    c, t = groups[n]
                    at_least(sp, st_done[n % NSTG], 16 * (n // NSTG))
                    sp.dma_start(stage[0:rows_of(t), n % NSTG, :],
                                 src(t)[:, c * NC_COLS:(c + 1) * NC_COLS]).then_inc(r_ld[n % NSTG], 16)

                for p in range(NP):
                    load_piece(0, p)
                for n in range(NSTG):
                    load_res(n)
                for n, (c, t) in enumerate(groups):
                    if t == TT - 1 and c + 1 < NCH:
                        for p in range(NP):
                            load_piece(c + 1, p)
                    sp.wait_ge(ev_done, n + 1)
                    sp.dma_start(dst(t)[:, c * NC_COLS:(c + 1) * NC_COLS],
                                 stage[0:rows_of(t), n % NSTG, :]).then_inc(st_done[n % NSTG], 16)
                    if n + NSTG < len(groups):
                        load_res(n + NSTG)
                for b in range(NSTG):
                    sp.wait_ge(st_done[b], 16 * len(groups) // NSTG)

            def act_unit(n, u):
                t, k = groups[n][1], slice(*units[u])
                if t < PT:
                    return actT[:, k, t * P:(t + 1) * P]
                return actT[:, k, GB:PADDED].rearrange("p k (b r) -> p k b r", r=SB)[:, :, :, 0:DEC_SEQ]

            def unit_part(part, n, u):
                m = units[u][1] - units[u][0]
                x = part[:, (NU * n + u) % 2, 0:m]
                return x if groups[n][1] < PT else x[:, :, 0:NS].rearrange("p k (b r) -> p k b r", r=DEC_SEQ)

            @block.scalar
            def _(act):
                def split_unit(n, u):
                    at_least(act, unit_mm, NU * n + u - 1)
                    nc.scalar.activation(unit_part(a_high, n, u), act_unit(n, u), ACT.Copy).then_inc(a_high_done, 1)

                def split_pieces(c, u):
                    for p in pieces_of(u):
                        m = c * NP + p
                        act.wait_ge(w_ld[m % NR2], 16 * (m // NR2 + 1))
                        if c:
                            act.wait_ge(unit_mm, NU * (c * TT - 1) + u + 1)
                        nc.scalar.activation(w_high[:, piece(p), :], raw[:, m % NR2], ACT.Copy).then_inc(w_high_done, 1)

                for n, (c, t) in enumerate(groups):
                    for u in range(NU):
                        if n == 0 and u >= 2:
                            split_pieces(0, u - 2)
                        if n == 1 and u < 2:
                            split_pieces(0, NU - 2 + u)
                        split_unit(n, u)
                        if t == TT - 1 and c + 1 < NCH and u >= 2:
                            split_pieces(c + 1, u - 2)
                        if t == 0 and c and u < 2:
                            split_pieces(c, NU - 2 + u)

            @block.gpsimd
            def _(pool):
                for n in range(len(groups)):
                    for u in range(NU):
                        pool.wait_ge(a_high_done, NU * n + u + 1)
                        nc.gpsimd.tensor_tensor(unit_part(a_low, n, u), act_unit(n, u), unit_part(a_high, n, u),
                                                ALU.subtract).then_inc(a_low_done, 1)

            @block.tensor
            def _(pe):
                for n, (c, t) in enumerate(groups):
                    r = rows_of(t)
                    at_least(pe, ev_done, n + 1 - NB)
                    for u, (k0, k1) in enumerate(units):
                        pe.wait_ge(a_low_done, NU * n + u + 1)
                        for k in range(k0, k1):
                            if t == 0 and k % PIECE == 0:
                                pe.wait_ge(w_low_done, c * NP + k // PIECE + 1)
                            last = parts_product(nc, acc[0:r, n % NB, :],
                                                 [x[:, (NU * n + u) % 2, k - k0, 0:r] for x in (a_high, a_low)],
                                                 [w_high[:, k, :], w_low[:, k, :]], k == 0, k == FT - 1)
                        last.then_inc(unit_mm, 1)

            @block.vector
            def _(dve):
                def low_pieces(c, u):
                    for p in pieces_of(u):
                        m, k = c * NP + p, piece(p)
                        dve.wait_ge(w_high_done, m + 1)
                        nc.vector.tensor_tensor(w_low[:, k, :], raw[:, m % NR2], w_high[:, k, :],
                                                ALU.subtract).then_inc(w_low_done, 1)

                for n, (c, t) in enumerate(groups):
                    r = rows_of(t)
                    if t == 0:
                        for u in range(NU - 2 if c else 0, NU):
                            low_pieces(c, u)
                    if t == TT - 1 and c + 1 < NCH:
                        for u in range(NU - 2):
                            low_pieces(c + 1, u)
                    dve.wait_ge(unit_mm, NU * (n + 1))
                    dve.wait_ge(r_ld[n % NSTG], 16 * (n // NSTG + 1))
                    x = stage[0:r, n % NSTG, :]
                    nc.vector.tensor_tensor(x, acc[0:r, n % NB, :], x, ALU.add).then_inc(ev_done, 1)


S5_GROUPS = 32
S5_GROUP = 16
S5_STATE = 64
S5_STEPS = 8
S5_PAIRS = S5_GROUPS // 2
S5_CHUNKS = SEQ // S5_STEPS
PI = float(np.pi)


def wide(ap, shape):
    return ap.broadcast_to(shape)


def complex_product(nc, link, out_re, out_im, a_re, a_im, b_re, b_im, t1, t2, conj=False):
    link(nc.vector.tensor_tensor(t1, a_re, b_re, ALU.mult))
    link(nc.vector.tensor_tensor(t2, a_im, b_im, ALU.mult))
    link(nc.vector.tensor_tensor(out_re, t1, t2, ALU.add if conj else ALU.subtract))
    link(nc.vector.tensor_tensor(t1, a_re, b_im, ALU.mult))
    link(nc.vector.tensor_tensor(t2, a_im, b_re, ALU.mult))
    link(nc.vector.tensor_tensor(out_im, t1, t2, ALU.subtract if conj else ALU.add))


def s5(nc, A, proj, mix):
    NPW = 3 * S5_PAIRS
    J = S5_STEPS * S5_GROUP
    NK = S5_CHUNKS + 1
    NCOL = S5_CHUNKS + 2 * DEC_BATCH
    with Phase(nc, "s5") as keep:
        ident = keep.sb("ident", [P, P])
        Tm = keep.sb("T", [P, S5_GROUPS, J])
        WE = [keep.sb(f"WE{i}", [P, S5_PAIRS, P]) for i in range(2)]
        G = [keep.sb(f"G{i}", [P, S5_PAIRS, J]) for i in range(2)]
        R = [keep.sb(f"R{i}", [P, S5_PAIRS, NK]) for i in range(2)]
        pw = [keep.sb(f"pw{i}", [P, NPW, S5_STEPS]) for i in range(2)]
        rho = keep.sb("rho", [P, S5_PAIRS])
        with Phase(nc, "s5_setup") as ph:
            lam = ph.sb("lam", [P, 2, S5_PAIRS])
            step = ph.sb("step", [P, S5_PAIRS])
            m = ph.sb("m", [P, 24, S5_PAIRS])
            B = ph.sb("B", [P, 2, S5_PAIRS, S5_GROUP])
            bb = ph.sb("bb", [P, 2, S5_PAIRS, S5_GROUP])
            c_rows = ph.sb("c_rows", [P, 2, 4, 2, S5_STATE])
            CT = ph.sb("CT", [P, 2, S5_PAIRS, S5_GROUP])
            Bn = [ph.sb(f"Bn{i}", [P, S5_PAIRS, J]) for i in range(2)]
            t1 = ph.sb("t1", [P, S5_PAIRS * J])
            t2 = ph.sb("t2", [P, S5_PAIRS * J])
            dcol = ph.sb("dcol", [P, S5_GROUPS])
            bmask = ph.sb("bmask", [P, J])
            pst = ph.ps("pst", [P, 4, NC_COLS])
            ld = ph.sem("ld")
            own = ph.sem("own")
            angles = ph.sem("angles")
            sines = ph.sem("sines")
            exps = ph.sem("exps")
            c_tr = ph.sem("c_tr")
            ct_ready = ph.sem("ct_ready")
            maps_ready = ph.sem("maps_ready")
            bank_full = ph.sem("bank_full")
            bank_free = ph.sem("bank_free")
            masked = ph.sem("masked")
            block = ph.block()
            n_ld = 16 * (2 + 2 + 2 + 8 + S5_STEPS + 2)

            @block.sync
            def _(sp):
                for i, nm in enumerate(["s5_lambda_re", "s5_lambda_im"]):
                    sp.dma_start(lam[:, i, :], A[nm][0].rearrange("(i g) p -> (g p) i", g=2),
                                 allow_slow_non_contiguous=True).then_inc(ld, 16)
                for g in range(2):
                    sp.dma_start(step[g * 64:(g + 1) * 64, :],
                                 A["s5_log_step"].rearrange("a (i g) -> g a i", g=2)[g]
                                 .broadcast_to([64, S5_PAIRS]),
                                 allow_slow_non_contiguous=True).then_inc(ld, 16)
                for i, nm in enumerate(["s5_b_re", "s5_b_im"]):
                    sp.dma_start(B[:, i, :, :], A[nm][0].rearrange("(i g) p c -> (g p) i c", g=2)).then_inc(ld, 16)
                for i, nm in enumerate(["s5_c_re", "s5_c_im"]):
                    for dup in range(2):
                        for h in range(2):
                            sp.dma_start(c_rows[:, i, 2 * h:2 * h + 2, dup, :],
                                         A[nm][0].rearrange("(m g) c p -> (g c) m p", g=8)[:, 2 * h:2 * h + 2, :]
                                         ).then_inc(ld, 16)
                for s in range(S5_STEPS):
                    sp.dma_start(dcol[s * S5_GROUP:(s + 1) * S5_GROUP, :],
                                 A["s5_d"][0].rearrange("g c -> c g"),
                                 allow_slow_non_contiguous=True).then_inc(ld, 16)
                sp.dma_start(ident[:, :], A["c_ident"]).then_inc(ld, 16)
                sp.dma_start(bmask[:, :], A["c_block_mask"]).then_inc(ld, 16)

            @block.scalar
            def _(act):
                act.wait_ge(ld, n_ld)
                nc.scalar.activation(m[:, 0, :], step[:, :], ACT.Exp).then_inc(exps, 1)
                act.wait_ge(angles, 1)
                nc.scalar.activation(m[:, 2, :], m[:, 1, :], ACT.Exp).then_inc(exps, 1)
                act.wait_ge(angles, 2)
                nc.scalar.activation(m[:, 8, :], m[:, 6, :], ACT.Sin).then_inc(sines, 1)
                nc.scalar.activation(m[:, 9, :], m[:, 7, :], ACT.Sin).then_inc(sines, 1)

            @block.vector
            def _(dve):
                link = Chain(dve, own)
                tt = nc.vector.tensor_tensor
                tsc = nc.vector.tensor_scalar
                dve.wait_ge(ld, n_ld)
                dve.wait_ge(exps, 1)
                tt(m[:, 1, :], lam[:, 0, :], m[:, 0, :], ALU.mult).then_inc(angles, 1)
                link(tt(m[:, 3, :], lam[:, 1, :], m[:, 0, :], ALU.mult))
                two_pi_hi = float(np.float32(6.28125))
                two_pi_lo = 2 * PI - two_pi_hi
                link(tsc(m[:, 4, :], m[:, 3, :], 1 / (2 * PI), None, ALU.mult))
                link(tsc(m[:, 5, :], m[:, 4, :], 12582912.0, None, ALU.add))
                link(tsc(m[:, 4, :], m[:, 5, :], -12582912.0, None, ALU.add))
                link(nc.vector.scalar_tensor_tensor(m[:, 5, :], m[:, 4, :], -two_pi_hi, m[:, 3, :], ALU.mult, ALU.add))
                link(nc.vector.scalar_tensor_tensor(m[:, 10, :], m[:, 4, :], -two_pi_lo, m[:, 5, :], ALU.mult, ALU.add))
                link(tsc(m[:, 6, :], m[:, 10, :], 3.1415925, -3.1415925, ALU.min, ALU.max))
                link(tsc(m[:, 11, :], m[:, 10, :], PI / 2, None, ALU.add))
                link(tsc(m[:, 12, :], m[:, 11, :], PI, -2 * PI, ALU.is_gt, ALU.mult))
                link(tt(m[:, 13, :], m[:, 11, :], m[:, 12, :], ALU.add))
                tsc(m[:, 7, :], m[:, 13, :], 3.1415925, -3.1415925, ALU.min, ALU.max).then_inc(angles, 1)
                dve.wait_ge(exps, 2)
                dve.wait_ge(sines, 2)
                sin, cos, mag = m[:, 8, :], m[:, 9, :], m[:, 2, :]
                one = [pw[i][:, :, 0] for i in range(2)]
                L, V, U = (slice(k * S5_PAIRS, (k + 1) * S5_PAIRS) for k in range(3))
                link(nc.vector.reciprocal(m[:, 14, :], mag))
                link(tt(one[0][:, L], mag, cos, ALU.mult))
                link(tt(one[1][:, L], mag, sin, ALU.mult))
                link(tt(one[0][:, V], m[:, 14, :], cos, ALU.mult))
                link(nc.vector.scalar_tensor_tensor(one[1][:, V], m[:, 14, :], -1.0, sin, ALU.mult, ALU.mult))
                link(nc.vector.tensor_copy(one[0][:, U], cos))
                link(nc.vector.tensor_copy(one[1][:, U], sin))
                n = 1
                while n < S5_STEPS:
                    shape = [P, NPW, n]
                    tv = [t[:, 0:NPW * n].rearrange("p (a b) -> p a b", b=n) for t in (t1, t2)]
                    complex_product(nc, link, pw[0][:, :, n:2 * n], pw[1][:, :, n:2 * n],
                                    pw[0][:, :, 0:n], pw[1][:, :, 0:n],
                                    wide(pw[0][:, :, n - 1:n], shape), wide(pw[1][:, :, n - 1:n], shape), *tv)
                    n *= 2
                link(tt(m[:, 15, :], mag, mag, ALU.mult))
                link(tt(m[:, 16, :], m[:, 15, :], m[:, 15, :], ALU.mult))
                link(tt(rho[:, :], m[:, 16, :], m[:, 16, :], ALU.mult))
                link(nc.vector.memset(R[0][:, :, 0:1], 1.0))
                link(nc.vector.memset(R[1][:, :, 0:1], 0.0))
                for i in range(2):
                    link(nc.vector.tensor_copy(R[i][:, :, 1:2], pw[i][:, U, S5_STEPS - 1:S5_STEPS]))
                n = 1
                while n < S5_CHUNKS:
                    shape = [P, S5_PAIRS, n]
                    tv = [t[:, 0:S5_PAIRS * n].rearrange("p (a b) -> p a b", b=n) for t in (t1, t2)]
                    complex_product(nc, link, R[0][:, :, n + 1:2 * n + 1], R[1][:, :, n + 1:2 * n + 1],
                                    R[0][:, :, 1:n + 1], R[1][:, :, 1:n + 1],
                                    wide(R[0][:, :, n:n + 1], shape), wide(R[1][:, :, n:n + 1], shape), *tv)
                    n *= 2
                lr, li = lam[:, 0, :], lam[:, 1, :]
                link(tt(m[:, 15, :], lr, lr, ALU.mult))
                link(tt(m[:, 16, :], li, li, ALU.mult))
                link(tt(m[:, 17, :], m[:, 15, :], m[:, 16, :], ALU.add))
                link(nc.vector.reciprocal(m[:, 18, :], m[:, 17, :]))
                link(tsc(m[:, 19, :], one[0][:, L], -1.0, None, ALU.add))
                complex_product(nc, link, m[:, 20, :], m[:, 21, :], lr, li, m[:, 19, :], one[1][:, L],
                                m[:, 15, :], m[:, 16, :], conj=True)
                link(tt(m[:, 22, :], m[:, 20, :], m[:, 18, :], ALU.mult))
                link(tt(m[:, 23, :], m[:, 21, :], m[:, 18, :], ALU.mult))
                shape = [P, S5_PAIRS, S5_GROUP]
                tv = [t[:, 0:S5_PAIRS * S5_GROUP].rearrange("p (a b) -> p a b", b=S5_GROUP) for t in (t1, t2)]
                complex_product(nc, link, bb[:, 0], bb[:, 1], wide(m[:, 22, :].unsqueeze(2), shape),
                                wide(m[:, 23, :].unsqueeze(2), shape), B[:, 0], B[:, 1], *tv)
                shape = [P, S5_PAIRS, S5_STEPS, S5_GROUP]
                v4 = [x[:, :].rearrange("p (i s c) -> p i s c", i=S5_PAIRS, s=S5_STEPS) for x in (t1, t2)]

                def cols4(x):
                    return x[:, :, :].rearrange("p i (s c) -> p i s c", s=S5_STEPS)
                complex_product(nc, link, cols4(Bn[0]), cols4(Bn[1]),
                                wide(pw[0][:, V].unsqueeze(3), shape), wide(pw[1][:, V].unsqueeze(3), shape),
                                wide(bb[:, 0].unsqueeze(2), shape), wide(bb[:, 1].unsqueeze(2), shape), *v4)
                for i in range(2):
                    dve.wait_ge(c_tr, i + 1)
                    for g in range(2):
                        rows = slice(64 * g, 64 * g + 64)
                        src = pst[rows, i, :].rearrange("p (i g c) -> p i g c", g=2, c=S5_GROUP)[:, :, g, :]
                        last = nc.vector.tensor_copy(CT[rows, i, :, :], src)
                    last.then_inc(ct_ready, 1)
                dve.wait_ge(ct_ready, 2)
                complex_product(nc, link, cols4(G[0]), cols4(G[1]),
                                wide(pw[0][:, L].unsqueeze(3), shape), wide(pw[1][:, L].unsqueeze(3), shape),
                                wide(CT[:, 0].unsqueeze(2), shape), wide(CT[:, 1].unsqueeze(2), shape), *v4)
                tsc(G[1][:, :, :], G[1][:, :, :], -1.0, None, ALU.mult).then_inc(maps_ready, 1)
                for q in range(16):
                    dve.wait_ge(bank_full, q + 1)
                    b = pst[:, q % 4, :].rearrange("p (k c) -> p k c", c=P)
                    if q < 8:
                        nc.vector.tensor_copy(WE[q // 4][:, 4 * (q % 4):4 * (q % 4) + 4, :], b).then_inc(bank_free, 1)
                        continue
                    par, pr = q % 2, 4 * ((q - 8) // 2)
                    tt(Tm[:, :, :].rearrange("p (i g) j -> p i g j", g=2)[:, pr:pr + 4, par, :], b,
                       wide(bmask[:, :].unsqueeze(1), [P, 4, J]), ALU.mult).then_inc(bank_free, 1)
                    dve.wait_ge(bank_free, q + 1)
                    for g in range(2 * pr + par, 2 * pr + 8, 2):
                        nc.vector.scalar_tensor_tensor(Tm[:, g, :], ident[:, :], dcol[:, g:g + 1], Tm[:, g, :],
                                                       ALU.mult, ALU.add)

            @block.tensor
            def _(pe):
                pe.wait_ge(ld, n_ld)
                for i in range(2):
                    for t in range(4):
                        last = nc.tensor.transpose(pst[:, i, t * P:(t + 1) * P],
                                                   c_rows[:, i, t].rearrange("p a b -> p (a b)"), ident[:, :])
                    last.then_inc(c_tr, 1)
                pe.wait_ge(maps_ready, 1)
                for q in range(16):
                    at_least(pe, bank_free, q - 3)
                    for j in range(4):
                        o = pst[:, q % 4, j * P:(j + 1) * P]
                        if q < 8:
                            last = nc.tensor.transpose(o, Bn[q // 4][:, 4 * (q % 4) + j, :], ident[:, :])
                        else:
                            g = 2 * (4 * ((q - 8) // 2) + j) + q % 2
                            rows = slice(64 * (g % 2), 64 * (g % 2) + 64)
                            nc.tensor.matmul(o, Bn[0][rows, g // 2, :], G[0][rows, g // 2, :], start=True, stop=False)
                            last = nc.tensor.matmul(o, Bn[1][rows, g // 2, :], G[1][rows, g // 2, :], start=False, stop=True)
                    last.then_inc(bank_full, 1)

        with Phase(nc, "s5_scan") as ph:
            UT = ph.sb("UT", [P, S5_GROUPS, NCOL])
            H = [ph.sb(f"H{i}", [P, S5_PAIRS, NK]) for i in range(2)]
            h0 = [ph.sb(f"h0{i}", [P, S5_PAIRS, DEC_BATCH]) for i in range(2)]
            with Phase(nc, "s5_in") as ph2:
                flat = ph2.sb("flat", [P, 2, S5_PAIRS * NK])
                U2 = flat[:, :, :].rearrange("p a b -> p (a b)")[:, 0:S5_STEPS * HALF] \
                    .rearrange("p (s f) -> p s f", s=S5_STEPS)
                s1, s2 = flat[:, 0, :], flat[:, 1, :]
                Us = ph2.sb("Us", [2 * DEC_BATCH, S5_GROUPS, S5_STEPS, S5_GROUP])
                h_rows = ph2.sb("h_rows", [DEC_BATCH, 2, S5_GROUPS * S5_STATE])
                F = [ph2.sb(f"F{i}", [P, S5_PAIRS, NCOL]) for i in range(2)]
                turned = ph2.sb("turned", [P, 2, S5_PAIRS, NK])
                Gs = [turned[:, i] for i in range(2)]
                Ug = turned[:, :, :, :].rearrange("p a b c -> p (a b c)")[:, 0:S5_STEPS * HALF] \
                    .rearrange("p (g s c) -> p g s c", g=S5_GROUPS, s=S5_STEPS)
                hout = [ph2.sb(f"hout{i}", [P, S5_PAIRS, 1 + DEC_BATCH]) for i in range(2)]
                o_rows = ph2.sb("o_rows", [1 + DEC_BATCH, 2, S5_GROUPS * S5_STATE])
                pst = ph2.ps("pst", [P, 8, NC_COLS])
                zeroed = ph2.sem("zeroed")
                ordered = ph2.sem("ordered")
                ld = ph2.sem("ld")
                ut_tr = ph2.sem("ut_tr")
                ut_ready = ph2.sem("ut_ready")
                h_tr = ph2.sem("h_tr")
                h_ready = ph2.sem("h_ready")
                f_mm = ph2.sem("f_mm")
                f_ready = ph2.sem("f_ready")
                own = ph2.sem("own")
                out_ready = ph2.sem("out_ready")
                out_tr = ph2.sem("out_tr")
                out_cp = ph2.sem("out_cp")
                st = ph2.sem("st")
                block = ph2.block()
                n_ld = 16 * (3 + 2 * DEC_SEQ)

                @block.sync
                def _(sp):
                    sp.dma_start(U2[:, :, :], proj[0:SEQ, 0:HALF].rearrange("(k s) f -> k s f", s=S5_STEPS)
                                 ).then_inc(ld, 16)
                    for i, nm in enumerate(["state_s5_re", "state_s5_im"]):
                        sp.dma_start(h_rows[:, i, :], A[nm][0].rearrange("b g p -> b (g p)")).then_inc(ld, 16)
                    sp.wait_ge(zeroed, 1)
                    us = proj[SEQ:TOK, 0:HALF].rearrange("(b s) f -> b s f", s=DEC_SEQ)
                    for k in range(2):
                        for s in range(DEC_SEQ):
                            sp.dma_start(Us[k * DEC_BATCH:(k + 1) * DEC_BATCH, :, k * DEC_SEQ + s, :],
                                         us[:, s, :].rearrange("b (g c) -> b g c", c=S5_GROUP)).then_inc(ld, 16)
                    sp.wait_ge(out_cp, 8)
                    for i, (pn, sn) in enumerate([("o_s5_re_p", "o_s5_re_s"), ("o_s5_im_p", "o_s5_im_s")]):
                        sp.dma_start(A[pn], o_rows[0:1, i, :]).then_inc(st, 16)
                        sp.dma_start(A[sn], o_rows[1:1 + DEC_BATCH, i, :]).then_inc(st, 16)
                    sp.wait_ge(st, 64)

                @block.tensor
                def _(pe):
                    pe.wait_ge(ld, n_ld)
                    for i in range(2):
                        for j in range(S5_PAIRS):
                            last = nc.tensor.transpose(pst[:, 7, (i * S5_PAIRS + j) * 8:(i * S5_PAIRS + j + 1) * 8],
                                                       h_rows[:, i, j * P:(j + 1) * P], ident[0:8, 0:8])
                    last.then_inc(h_tr, 1)
                    for g in range(S5_GROUPS):
                        q = g % 6
                        at_least(pe, ut_ready, g - 5)
                        if g % 8 == 0:
                            pe.wait_ge(ordered, g // 8 + 1)
                        nc.tensor.transpose(pst[:, q, 0:P], Ug[:, g].rearrange("p s c -> p (s c)"), ident[:, :])
                        nc.tensor.transpose(pst[:, q, P:NCOL], Us[:, g].rearrange("p s c -> p (s c)"),
                                            ident[0:16, 0:16]).then_inc(ut_tr, 1)
                    pe.wait_ge(ut_ready, S5_GROUPS)
                    for j in range(2 * S5_PAIRS):
                        i, pr = j % 2, j // 2
                        at_least(pe, f_ready, j - 5)
                        for g in range(2):
                            rows = slice(64 * g, 64 * g + 64)
                            last = nc.tensor.matmul(pst[rows, j % 6, 0:NCOL], WE[i][:, pr, rows], UT[:, 2 * pr + g, :],
                                                    start=True, stop=True)
                        last.then_inc(f_mm, 1)
                    pe.wait_ge(out_ready, 1)
                    for n in range(8):
                        i, q = n // 4, n % 4
                        at_least(pe, out_cp, n - 3)
                        for k in range(4):
                            last = nc.tensor.transpose(pst[0:1 + DEC_BATCH, n % 4, k * P:(k + 1) * P],
                                                       hout[i][:, 4 * q + k, :], ident[:, :])
                        last.then_inc(out_tr, 1)

                @block.scalar
                def _(act):
                    act.wait_ge(h_tr, 1)
                    for i in range(2):
                        nc.scalar.activation(h0[i][:, :, :].rearrange("p a b -> p (a b)"),
                                             pst[:, 7, i * P:(i + 1) * P], ACT.Copy).then_inc(h_ready, 1)
                    for g in range(S5_GROUPS):
                        act.wait_ge(ut_tr, g + 1)
                        nc.scalar.activation(UT[:, g, :], pst[:, g % 6, 0:NCOL], ACT.Copy).then_inc(ut_ready, 1)
                    for j in range(2 * S5_PAIRS):
                        act.wait_ge(f_mm, j + 1)
                        nc.scalar.activation(F[j % 2][:, j // 2, :], pst[:, j % 6, 0:NCOL], ACT.Copy).then_inc(f_ready, 1)
                    for n in range(8):
                        act.wait_ge(out_tr, n + 1)
                        nc.scalar.activation(o_rows[:, n // 4, (n % 4) * NC_COLS:(n % 4 + 1) * NC_COLS],
                                             pst[0:1 + DEC_BATCH, n % 4, :], ACT.Copy).then_inc(out_cp, 1)

                @block.vector
                def _(dve):
                    nc.vector.memset(Us[:, :, :, :], 0.0).then_inc(zeroed, 1)
                    link = Chain(dve, own)
                    dve.wait_ge(ld, n_ld)
                    for q in range(4):
                        nc.vector.tensor_copy(Ug[:, 8 * q:8 * q + 8], U2[:, :, P * q:P * q + P]
                                              .rearrange("p s (g c) -> p g s c", c=S5_GROUP)).then_inc(ordered, 1)
                    dve.wait_ge(f_ready, 2 * S5_PAIRS)
                    for i in range(2):
                        link(nc.vector.memset(Gs[i][:, :, 0:1], 0.0))
                    K_ = S5_CHUNKS
                    tv = [t[:, 0:S5_PAIRS * K_].rearrange("p (a b) -> p a b", b=K_) for t in (s1, s2)]
                    x = [h[:, :, 0:K_] for h in H]
                    complex_product(nc, link, x[0], x[1], R[0][:, :, 0:K_], R[1][:, :, 0:K_],
                                    F[0][:, :, 0:K_], F[1][:, :, 0:K_], *tv, conj=True)
                    for i in range(2):
                        for j in range(S5_PAIRS):
                            last = nc.vector.tensor_tensor_scan(Gs[i][:, j, 1:NK], H[i][:, j, 0:K_],
                                                                wide(rho[:, j:j + 1], [P, K_]), 0.0, ALU.add, ALU.mult)
                        link(last)
                    tv = [t.rearrange("p (a b) -> p a b", b=NK) for t in (s1, s2)]
                    complex_product(nc, link, H[0][:, :, :], H[1][:, :, :], R[0][:, :, :], R[1][:, :, :],
                                    Gs[0][:, :, :], Gs[1][:, :, :], *tv)
                    shape = [P, S5_PAIRS, DEC_BATCH]
                    tv = [t[:, 0:P].rearrange("p (a b) -> p a b", b=DEC_BATCH) for t in (s1, s2)]
                    ac = [t[:, 2 * P:3 * P].rearrange("p (a b) -> p a b", b=DEC_BATCH) for t in (s1, s2)]
                    dve.wait_ge(h_ready, 2)
                    Lp = slice(0, S5_PAIRS)
                    complex_product(nc, link, hout[0][:, :, 1:], hout[1][:, :, 1:], wide(pw[0][:, Lp, 3:4], shape),
                                    wide(pw[1][:, Lp, 3:4], shape), h0[0][:, :, :], h0[1][:, :, :], *tv)
                    complex_product(nc, link, ac[0], ac[1], wide(pw[0][:, Lp, 7:8], shape),
                                    wide(pw[1][:, Lp, 7:8], shape), F[0][:, :, NCOL - 8:], F[1][:, :, NCOL - 8:], *tv)
                    for i in range(2):
                        link(nc.vector.tensor_tensor(hout[i][:, :, 1:], hout[i][:, :, 1:], ac[i], ALU.add))
                        last = nc.vector.tensor_copy(hout[i][:, :, 0:1], H[i][:, :, K_:NK])
                    last.then_inc(out_ready, 1)

            with Phase(nc, "s5_out") as ph2:
                Y = ph2.sb("Y", [P, S5_STEPS, HALF])
                Ys = ph2.sb("Ys", [DEC_BATCH, DEC_SEQ, HALF])
                w_glu = ph2.sb("w_glu", [P, 4, HALF])
                bias = ph2.sb("bias", [P, HALF])
                yT = ph2.sb("yT", [P, 2, 4, P])
                z = ph2.sb("z", [P, 2, HALF])
                zs = ph2.sb("zs", [P, 2, HALF])
                pst = ph2.ps("pst", [P, 6, NC_COLS])
                ld = ph2.sem("ld")
                y_mm = ph2.sem("y_mm")
                y_ready = ph2.sem("y_ready")
                y_tr = ph2.sem("y_tr")
                yT_ready = ph2.sem("yT_ready")
                z_mm = ph2.sem("z_mm")
                z_ready = ph2.sem("z_ready")
                sig = ph2.sem("sig")
                out_ready = ph2.sem("out_ready")
                st = ph2.sem("st")
                block = ph2.block()
                NG4 = S5_GROUPS // 4
                units = [(P, Y, s) for s in range(S5_STEPS)] + [(DEC_BATCH, Ys, s) for s in range(DEC_SEQ)]

                @block.sync
                def _(sp):
                    sp.dma_start(w_glu[:, :, :], A["s5_w_glu"][0].rearrange("(k p) n -> p k n", p=P)).then_inc(ld, 16)
                    sp.dma_start(bias[:, :], A["s5_b_glu"].broadcast_to([P, HALF])).then_inc(ld, 16)
                    mp = mix[0:SEQ, 0:HALF].rearrange("(k s) f -> k s f", s=S5_STEPS)
                    ms = mix[SEQ:TOK, 0:HALF].rearrange("(b s) f -> b s f", s=DEC_SEQ)
                    for n, (r, y, s) in enumerate(units):
                        sp.wait_ge(out_ready, n + 1)
                        sp.dma_start((mp if r == P else ms)[:, s, :], y[:, s, :]).then_inc(st, 16)
                    sp.wait_ge(st, 16 * len(units))

                @block.tensor
                def _(pe):
                    for q in range(2 * NG4):
                        at_least(pe, y_ready, q - 3)
                        r = P if q < NG4 else DEC_BATCH
                        for k in range(4):
                            g = 2 * (4 * (q % NG4 // 2) + k) + q % 2
                            o = pst[0:r, q % 4, k * J:(k + 1) * J]
                            rows = slice(64 * (g % 2), 64 * (g % 2) + 64)
                            u = UT[:, g, 0:P] if q < NG4 else UT[:, g, P:P + DEC_BATCH]
                            h = [(H[i][rows, g // 2, 0:P] if q < NG4 else h0[i][rows, g // 2, :]) for i in range(2)]
                            nc.tensor.matmul(o, u, Tm[:, g, :], start=True, stop=False)
                            nc.tensor.matmul(o, h[0], G[0][rows, g // 2, :], start=False, stop=False)
                            last = nc.tensor.matmul(o, h[1], G[1][rows, g // 2, :], start=False, stop=True)
                        last.then_inc(y_mm, 1)
                    pe.wait_ge(y_ready, 2 * NG4)
                    pe.wait_ge(ld, 32)
                    for n, (r, y, s) in enumerate(units):
                        at_least(pe, yT_ready, n - 1)
                        for k in range(4):
                            last = nc.tensor.transpose(pst[:, n % 2, k * P:k * P + r], y[0:r, s, k * P:(k + 1) * P],
                                                       ident[0:r, 0:r])
                        last.then_inc(y_tr, 1)
                        pe.wait_ge(yT_ready, n + 1)
                        at_least(pe, z_ready, n - 1)
                        for k in range(4):
                            last = nc.tensor.matmul(pst[0:r, 4 + n % 2, :], yT[:, n % 2, k, 0:r], w_glu[:, k, :],
                                                    start=(k == 0), stop=(k == 3))
                        last.then_inc(z_mm, 1)

                @block.scalar
                def _(act):
                    for q in range(2 * NG4):
                        act.wait_ge(y_mm, q + 1)
                        r, y, ns = (P, Y, S5_STEPS) if q < NG4 else (DEC_BATCH, Ys, DEC_SEQ)
                        src = pst[0:r, q % 4, :].rearrange("p (i s c) -> p i s c", i=4, s=S5_STEPS)[:, :, 0:ns, :]
                        dst = y[:, :, :].rearrange("p s (q i g c) -> p q g i s c", q=4, i=4, g=2)
                        nc.scalar.activation(dst[:, q % NG4 // 2, q % 2], src, ACT.Gelu_apprx_tanh).then_inc(y_ready, 1)
                    for n, (r, y, s) in enumerate(units):
                        act.wait_ge(z_ready, n + 1)
                        at_least(act, out_ready, n - 1)
                        nc.scalar.activation(zs[0:r, n % 2, :], z[0:r, n % 2, :], ACT.Sigmoid).then_inc(sig, 1)

                @block.vector
                def _(dve):
                    def finish(n):
                        r, y, s = units[n]
                        dve.wait_ge(sig, n + 1)
                        nc.vector.tensor_tensor(y[0:r, s, :], y[0:r, s, :], zs[0:r, n % 2, :], ALU.mult
                                                ).then_inc(out_ready, 1)
                    dve.wait_ge(ld, 32)
                    for n, (r, y, s) in enumerate(units):
                        dve.wait_ge(y_tr, n + 1)
                        at_least(dve, z_mm, n - 1)
                        nc.vector.tensor_copy(yT[:, n % 2, :, 0:r], pst[:, n % 2, :]
                                              .rearrange("p (k c) -> p k c", c=P)[:, :, 0:r]).then_inc(yT_ready, 1)
                        dve.wait_ge(z_mm, n + 1)
                        at_least(dve, sig, n - 1)
                        nc.vector.tensor_tensor(z[0:r, n % 2, :], pst[0:r, 4 + n % 2, :], bias[0:r, :], ALU.add
                                                ).then_inc(z_ready, 1)
                        if n:
                            finish(n - 1)
                    finish(len(units) - 1)


def unit_of(t):
    return 2 + (t if t < 4 else 4 + 2 * (t - 4))


def key_blocks(t):
    return [(b, min(4, t + 1 - b)) for b in range(0, t + 1, 4)]


def prompt_attention(nc, name, A, q_src, k_src, v_src, mix, softmax):
    UNITS = 14
    with Phase(nc, name) as ph:
        ident = ph.sb("ident", [P, P])
        raw = ph.sb("raw", [P, 2, PT, 3, HEAD_DIM])
        qkT = ph.sb("qkT", [HEAD_DIM, 2, SEQ])
        ex = ph.sb("ex", [P, 2, SEQ])
        cp = ph.sb("cp", [P, SEQ + 1])
        w = ph.sb("w", [P, 2, SEQ])
        wT = ph.sb("wT", [P, 2, SEQ])
        zero = ph.sb("zero", [P, 1])
        not_before = ph.sb("not_before", [P, P])
        stage = ph.sb("stage", [P, 2, PT, HEAD_DIM])
        if softmax:
            sel = ph.sb("sel", [P, PT, SEQ])
            near = ph.sb("near", [P, HEADS, 2 * P])
            stat = ph.sb("stat", [P, 4, PT])
        ps_s = ph.ps("ps_s", [P, 2, 2, NC_COLS])
        ps_t = ph.ps("ps_t", [P, 2, NC_COLS])
        ps_o = ph.ps("ps_o", [P, NC_COLS])
        const_ld = ph.sem("const_ld")
        ld = [ph.sem(f"ld{i}") for i in range(2)]
        s_mm = ph.sem("s_mm")
        keep_done = ph.sem("keep_done")
        diag_done = ph.sem("diag_done")
        scan_done = ph.sem("scan_done")
        set_up = ph.sem("set_up")
        logit_done = ph.sem("logit_done")
        max_done = ph.sem("max_done")
        sum_inv = ph.sem("sum_inv")
        w_done = ph.sem("w_done")
        tr_done = ph.sem("tr_done")
        u_ev = ph.sem("u_ev")
        pv_done = ph.sem("pv_done")
        o_ev = ph.sem("o_ev")
        st = [ph.sem(f"st{i}") for i in range(2)]
        srcs = [x.rearrange("(t p) (h d) -> h p t d", p=P, d=HEAD_DIM) for x in (q_src, k_src, v_src)]
        dst = mix.rearrange("(t p) (h d) -> h p t d", p=P, d=HEAD_DIM)
        block = ph.block()

        def heads(eng, body):
            body(0, 0)
            body(1, 1)
            with eng.Fori(1, HEADS // 2) as i:
                body(i * 2, 0)
                body(i * 2 + 1, 1)

        @block.sync
        def _(sp):
            sp.dma_start(ident[:, :], A["c_ident"]).then_inc(const_ld, 16)
            sp.dma_start(not_before[:, :], A["c_not_before"]).then_inc(const_ld, 16)
            if softmax:
                for h in range(HEADS):
                    sp.dma_start(near[:, h, :], skewed(A["near"][h], NEAR_TOP - P, 2 * P, P)).then_inc(const_ld, 16)
                for t in range(PT):
                    sp.dma_start(sel[:, t, 0:(t + 1) * P], A["sel"][t, :, 0:(t + 1) * P]).then_inc(const_ld, 16)

            def load(h, s):
                at_least(sp, pv_done, (h - 1) * PT)
                for i in range(3):
                    sp.dma_start(raw[:, s, :, i, :], srcs[i][h]).then_inc(ld[s], 16)
            heads(sp, load)

        n_const = 16 * (2 + HEADS + PT if softmax else 2)

        @block.gpsimd
        def _(pool):
            def store(h, s):
                pool.wait_ge(o_ev, h + 1)
                pool.dma_start(dst[h], stage[:, s, :, :]).then_inc(st[s], 16)
            heads(pool, store)
            for s in range(2):
                pool.wait_ge(st[s], 16 * HEADS // 2)

        @block.tensor
        def _(pe):
            pe.wait_ge(const_ld, n_const)

            def scores(h, t):
                at_least(pe, logit_done if softmax else keep_done, h * PT + t - 1)
                for b, (b0, n) in enumerate(key_blocks(t)):
                    last = nc.tensor.matmul(ps_s[:, t % 2, b, 0:n * P], qkT[:, 0, t * P:(t + 1) * P],
                                            qkT[:, 1, b0 * P:(b0 + n) * P], start=True, stop=True)
                last.then_inc(s_mm, 1)

            def values(h, s, t):
                pe.wait_ge(u_ev, h * UNITS + unit_of(t + 1))
                if t == 0:
                    at_least(pe, o_ev, h)
                for j in range(t + 1):
                    last = nc.tensor.matmul(ps_o[:, t * HEAD_DIM:(t + 1) * HEAD_DIM], wT[:, t % 2, j * P:(j + 1) * P],
                                            raw[:, s, j, 2, :], start=(j == 0), stop=(j == t))
                last.then_inc(pv_done, 1)

            def head(h, s):
                pe.wait_ge(ld[s], (h - s) * 24 + 48)
                for u in range(2):
                    at_least(pe, u_ev, h * UNITS + u - 1)
                    for j in range(4):
                        last = nc.tensor.transpose(ps_t[:, u, j * P:(j + 1) * P],
                                                   raw[:, s, 4 * u + j, 0:2, :].rearrange("p a d -> p (a d)"), ident[:, :])
                    last.then_inc(tr_done, 1)
                pe.wait_ge(u_ev, h * UNITS + 2)
                scores(h, 0)
                scores(h, 1)
                for t in range(PT):
                    pe.wait_ge(w_done, h * PT + t + 1)
                    for b, (b0, n) in enumerate(key_blocks(t)):
                        u = unit_of(t) + b
                        pe.wait_ge(u_ev, h * UNITS + u - 1)
                        for j in range(n):
                            last = nc.tensor.transpose(ps_t[:, u % 2, j * P:(j + 1) * P],
                                                       w[:, t % 2, (b0 + j) * P:(b0 + j + 1) * P], ident[:, :])
                        last.then_inc(tr_done, 1)
                    if t + 2 < PT:
                        scores(h, t + 2)
                    if t:
                        values(h, s, t - 1)
                values(h, s, PT - 1)
            heads(pe, head)

        @block.scalar
        def _(act):
            def turn(h, u, dst_ap, src_ap):
                act.wait_ge(tr_done, h * UNITS + u + 1)
                nc.scalar.activation(dst_ap, src_ap, ACT.Copy).then_inc(u_ev, 1)

            def head(h, s):
                at_least(act, pv_done, h * PT)
                for u in range(2):
                    act.wait_ge(tr_done, h * UNITS + u + 1)
                    for i in range(2):
                        last = nc.scalar.activation(qkT[:, i, u * NC_COLS:(u + 1) * NC_COLS],
                                                    ps_t[i * HEAD_DIM:(i + 1) * HEAD_DIM, u, :], ACT.Copy)
                    last.then_inc(u_ev, 1)

                def weigh(t):
                    n = (t + 1) * P
                    if softmax:
                        act.wait_ge(max_done, h * PT + t + 1)
                        if t < 2:
                            at_least(act, tr_done, h * UNITS - (4 if t == 0 else 2) + 2)
                        else:
                            act.wait_ge(tr_done, h * UNITS + unit_of(t - 1))
                        if t == 0:
                            at_least(act, o_ev, h)
                        nc.scalar.activation(w[:, t % 2, 0:n], ex[:, t % 2, 0:n], ACT.Exp, bias=stat[:, 0, t:t + 1],
                                             accum_out=stat[:, 1, t:t + 1]).then_inc(w_done, 1)
                        return
                    act.wait_ge(s_mm, h * PT + t + 1)
                    at_least(act, scan_done, h * PT + t - 1)
                    for b, (b0, m) in enumerate(key_blocks(t)):
                        last = nc.scalar.activation(ex[:, t % 2, b0 * P:(b0 + m) * P], ps_s[:, t % 2, b, 0:m * P],
                                                    ACT.Sigmoid, scale=-SCALE)
                    last.then_inc(keep_done, 1)

                weigh(0)
                for t in range(PT):
                    if t + 1 < PT:
                        weigh(t + 1)
                    if t < 2:
                        at_least(act, pv_done, h * PT + t - 1)
                    else:
                        act.wait_ge(pv_done, h * PT + t - 1)
                    for b, (b0, n) in enumerate(key_blocks(t)):
                        u = unit_of(t) + b
                        turn(h, u, wT[:, t % 2, b0 * P:(b0 + n) * P], ps_t[:, u % 2, 0:n * P])
            heads(act, head)

        @block.vector
        def _(dve):
            nc.vector.memset(zero[:, :], 0.0).then_inc(set_up, 1)
            dve.wait_ge(set_up, 1)
            dve.wait_ge(const_ld, n_const)

            def head(h, s):
                for t in range(PT):
                    n = (t + 1) * P
                    if softmax:
                        dve.wait_ge(s_mm, h * PT + t + 1)
                        at_least(dve, w_done, h * PT + t - 1)
                        for b, (b0, m) in enumerate(key_blocks(t)):
                            cols = slice(b0 * P, (b0 + m) * P)
                            last = nc.vector.scalar_tensor_tensor(ex[:, t % 2, cols], ps_s[:, t % 2, b, 0:m * P], SCALE,
                                                                  sel[:, t, cols], ALU.mult, ALU.add)
                        last.then_inc(logit_done, 1)
                        dve.wait_ge(logit_done, h * PT + t + 1)
                        k0 = max(t - 1, 0) * P
                        nc.vector.tensor_tensor(ex[:, t % 2, k0:n], ex[:, t % 2, k0:n],
                                                near[:, h, 2 * P - (n - k0):2 * P], ALU.add).then_inc(scan_done, 1)
                        dve.wait_ge(scan_done, h * PT + t + 1)
                        nc.vector.tensor_reduce(stat[:, 0, t:t + 1], ex[:, t % 2, 0:n], AX_X, ALU.max,
                                                negate=True).then_inc(max_done, 1)
                        continue
                    dve.wait_ge(keep_done, h * PT + t + 1)
                    diag = ex[:, t % 2, t * P:n]
                    nc.vector.tensor_tensor(diag, diag, not_before[:, :], ALU.max).then_inc(diag_done, 1)
                    at_least(dve, w_done, h * PT + t)
                    nc.vector.memset(cp[:, n:n + 1], 1.0)
                    dve.wait_ge(diag_done, h * PT + t + 1)
                    nc.vector.tensor_tensor_scan(cp[:, 0:n][:, ::-1], ex[:, t % 2, 0:n][:, ::-1],
                                                 wide(zero[:, :], [P, n]), 1.0, ALU.mult, ALU.add).then_inc(scan_done, 1)
                    dve.wait_ge(scan_done, h * PT + t + 1)
                    if t < 2:
                        at_least(dve, tr_done, h * UNITS - 2 * (1 - t))
                    else:
                        dve.wait_ge(tr_done, h * UNITS + unit_of(t - 1))
                    nc.vector.tensor_tensor(w[:, t % 2, 0:n], cp[:, 1:n + 1], cp[:, 0:n], ALU.subtract).then_inc(w_done, 1)
                dve.wait_ge(pv_done, (h + 1) * PT)
                if not isinstance(h, int) or h >= 2:
                    dve.wait_ge(st[s], (h - s) * 8)
                if softmax:
                    nc.vector.reciprocal(stat[:, 2, :], stat[:, 1, :]).then_inc(sum_inv, 1)
                    dve.wait_ge(sum_inv, h + 1)
                    nc.vector.tensor_tensor(stage[:, s, :, :], ps_o[:, :].rearrange("p (t d) -> p t d", d=HEAD_DIM),
                                            wide(stat[:, 2, :].unsqueeze(2), [P, PT, HEAD_DIM]), ALU.mult).then_inc(o_ev, 1)
                else:
                    nc.vector.tensor_copy(stage[:, s, :, :].rearrange("p t d -> p (t d)"), ps_o[:, :]).then_inc(o_ev, 1)

            heads(dve, head)


NEAR = 400
NEAR_TOP = 260


def sample_attention(nc, name, A, q_src, k_src, v_src, pool_k, pool_v, mix, softmax):
    G4 = 4
    ROUNDS = DEC_BATCH // G4
    HP = HEADS // 2
    R = HEADS * DEC_SEQ
    ALL = PAST_LEN + DEC_SEQ
    ITEMS = 2 * DEC_BATCH
    SLOTS = 3
    with Phase(nc, name) as ph:
        ident = ph.sb("ident", [P, P])
        table = ph.sb("table", [1, DEC_BATCH * N_PAGES], I32)
        pages = ph.sb("pages", [P, SLOTS, N_PAGES, HALF])
        qk_rows = ph.sb("qk_rows", [NS, 2, HALF])
        v_new = ph.sb("v_new", [DEC_SEQ, DEC_BATCH, HALF])
        qkT = ph.sb("qkT", [P, 2, HP, NS])
        Q = ph.sb("Q", [P, DEC_BATCH, HP, P])
        kT = ph.sb("kT", [P, 2, HP, PAST_LEN])
        ex = ph.sb("ex", [P, ALL])
        cp = ph.sb("cp", [P, ALL + 1])
        w = ph.sb("w", [P, ALL])
        wT = ph.sb("wT", [P, N_PAGES + 1, P])
        own_head = ph.sb("own_head", [R, HEADS])
        late = ph.sb("late", [P, DEC_SEQ])
        zero = ph.sb("zero", [P, 1])
        tmp = ph.sb("tmp", [R, HALF])
        out = ph.sb("out", [R, DEC_BATCH, HEAD_DIM])
        if softmax:
            sel = ph.sb("sel", [P, ALL])
            near = ph.sb("near", [P, 256 + DEC_SEQ])
            stat = ph.sb("stat", [P, 4])
        ps_t = ph.ps("ps_t", [P, 2, NC_COLS])
        ps_s = ph.ps("ps_s", [P, 3, NC_COLS])
        ps_o = ph.ps("ps_o", [P, 2, NC_COLS])
        table_ld = ph.sem("table_ld")
        ld = ph.sem("ld")
        sel_ld = ph.sem("sel_ld")
        page_ld = [ph.sem(f"page_ld{i}") for i in range(SLOTS)]
        set_up = ph.sem("set_up")
        qk_tr = ph.sem("qk_tr")
        q_ready = ph.sem("q_ready")
        unit_tr = ph.sem("unit_tr")
        unit_ev = ph.sem("unit_ev")
        s_mm = ph.sem("s_mm")
        keep_done = ph.sem("keep_done")
        own = ph.sem("own")
        w_done = ph.sem("w_done")
        pv_mm = ph.sem("pv_mm")
        o_ev = ph.sem("o_ev")
        out_ready = ph.sem("out_ready")
        st = ph.sem("st")
        out_sum = ph.sem("out_sum")
        inv_done = ph.sem("inv_done")
        n_ld = 16 * (6 + (G4 if softmax else 0))
        items = [(kv, r * G4 + g) for r in range(ROUNDS) for kv in range(2) for g in range(G4)]
        KU, WU = N_PAGES, 3
        RU = G4 * KU + WU
        block = ph.block()

        @block.sync
        def _(sp):
            sp.dma_start(table[:, :], A["page_table"].rearrange("b n -> (b n)").unsqueeze(0)).then_inc(table_ld, 16)
            sp.dma_start(ident[:, :], A["c_ident"]).then_inc(ld, 16)
            sp.dma_start(own_head[:, :], A["c_own_head"]).then_inc(ld, 16)
            sp.dma_start(late[:, :], A["c_late"]).then_inc(ld, 16)
            sp.dma_start(qk_rows[:, 0, :], q_src).then_inc(ld, 16)
            sp.dma_start(qk_rows[:, 1, :], k_src).then_inc(ld, 16)
            sp.dma_start(v_new[:, :, :], v_src.rearrange("(b s) f -> s b f", s=DEC_SEQ)).then_inc(ld, 16)
            if softmax:
                for g in range(G4):
                    sp.dma_start(near[g * R:(g + 1) * R, :], A["near_sample"]).then_inc(ld, 16)
            sp.wait_ge(table_ld, 16)
            for n, (kv, b) in enumerate(items):
                if n >= SLOTS:
                    was_v, c = items[n - SLOTS]
                    if was_v:
                        sp.wait_ge(pv_mm, c + 1)
                    else:
                        sp.wait_ge(unit_tr, c // G4 * RU + (c % G4 + 1) * KU)
                for pg in range(N_PAGES):
                    row = sp.value_load(table[0:1, b * N_PAGES + pg:b * N_PAGES + pg + 1], min_val=0,
                                        max_val=pool_k.shape[0] - 1)
                    sp.dma_start(pages[:, n % SLOTS, pg, :], (pool_v if kv else pool_k)[row]
                                 ).then_inc(page_ld[n % SLOTS], 16)
            sp.wait_ge(out_ready, DEC_BATCH)
            for h in range(HEADS):
                sp.dma_start(mix[:, h * HEAD_DIM:(h + 1) * HEAD_DIM].rearrange("(b s) d -> s b d", s=DEC_SEQ),
                             out[h * DEC_SEQ:(h + 1) * DEC_SEQ, :, :]).then_inc(st, 16)
            sp.wait_ge(st, 16 * HEADS)

        if softmax:
            @block.gpsimd
            def _(pool):
                for r in range(ROUNDS):
                    at_least(pool, w_done, r)
                    for g in range(G4):
                        b = r * G4 + g
                        src = A["sel_sample"][b * DEC_SEQ:(b + 1) * DEC_SEQ, :]
                        for h in range(HEADS):
                            pool.dma_start(sel[g * R + h * DEC_SEQ:g * R + (h + 1) * DEC_SEQ, :], src).then_inc(sel_ld, 16)

        @block.tensor
        def _(pe):
            pe.wait_ge(ld, n_ld)
            for i in range(2):
                for hp in range(HP):
                    last = nc.tensor.transpose(ps_t[:, i, hp * NS:(hp + 1) * NS], qk_rows[:, i, hp * P:(hp + 1) * P],
                                               ident[0:NS, 0:NS])
            last.then_inc(qk_tr, 1)
            pe.wait_ge(q_ready, 1)
            for n, (kv, b) in enumerate(items):
                r, g = b // G4, b % G4
                pe.wait_ge(page_ld[n % SLOTS], 16 * N_PAGES * (n // SLOTS + 1))
                pg_slot = pages[:, n % SLOTS]
                if kv == 0:
                    for pg in range(N_PAGES):
                        u = r * RU + g * KU + pg
                        at_least(pe, unit_ev, u - 1)
                        for hp in range(HP):
                            last = nc.tensor.transpose(ps_t[:, u % 2, hp * P:(hp + 1) * P],
                                                       pg_slot[:, pg, hp * P:(hp + 1) * P], ident[:, :])
                        last.then_inc(unit_tr, 1)
                    pe.wait_ge(unit_ev, r * RU + (g + 1) * KU)
                    if g == 0:
                        at_least(pe, keep_done, r)
                    for hp in range(HP):
                        ends = dict(start=(g == 0 and hp == 0), stop=(g == G4 - 1 and hp == HP - 1))
                        for c in range(2):
                            nc.tensor.matmul(ps_s[:, c, :], Q[:, b, hp, :], kT[:, b % 2, hp, c * NC_COLS:(c + 1) * NC_COLS],
                                             **ends)
                        last = nc.tensor.matmul(ps_s[:, 2, 0:DEC_SEQ], Q[:, b, hp, :],
                                                qkT[:, 1, hp, b * DEC_SEQ:(b + 1) * DEC_SEQ], **ends)
                    last.then_inc(s_mm, 1)
                    continue
                if g == 0:
                    pe.wait_ge(w_done, r + 1)
                    for j in range(WU):
                        u = r * RU + G4 * KU + j
                        pe.wait_ge(unit_ev, u - 1)
                        for i in range(4 if j < 2 else 1):
                            src = w[:, (4 * j + i) * P:(4 * j + i + 1) * P] if j < 2 else w[:, PAST_LEN:ALL]
                            last = nc.tensor.transpose(ps_t[0:src.shape[1], u % 2, i * P:(i + 1) * P], src, ident[:, :])
                        last.then_inc(unit_tr, 1)
                    pe.wait_ge(unit_ev, (r + 1) * RU)
                at_least(pe, o_ev, b - 1)
                for pg in range(N_PAGES):
                    nc.tensor.matmul(ps_o[0:R, b % 2, :], wT[:, pg, g * R:(g + 1) * R], pg_slot[:, pg, :],
                                            start=(pg == 0), stop=False)
                nc.tensor.matmul(ps_o[0:R, b % 2, :], wT[0:DEC_SEQ, N_PAGES, g * R:(g + 1) * R], v_new[:, b, :],
                                 start=False, stop=True).then_inc(pv_mm, 1)

        @block.scalar
        def _(act):
            for r in range(ROUNDS):
                for g in range(G4):
                    b = r * G4 + g
                    for pg in range(N_PAGES):
                        u = r * RU + g * KU + pg
                        act.wait_ge(unit_tr, u + 1)
                        if pg == 0:
                            at_least(act, s_mm, b - 1)
                        nc.scalar.activation(kT[:, b % 2, :, pg * P:(pg + 1) * P],
                                             ps_t[:, u % 2, :].rearrange("p (h c) -> p h c", c=P), ACT.Copy
                                             ).then_inc(unit_ev, 1)
                act.wait_ge(s_mm, (r + 1) * G4)
                if softmax:
                    act.wait_ge(own, 2 * (r + 1))
                    nc.scalar.activation(cp[:, 0:ALL], ex[:, :], ACT.Exp, bias=stat[:, 0:1],
                                         accum_out=stat[:, 1:2]).then_inc(out_sum, 1)
                else:
                    at_least(act, w_done, r)
                    for c in range(3):
                        n = NC_COLS if c < 2 else DEC_SEQ
                        last = nc.scalar.activation(ex[:, c * NC_COLS:c * NC_COLS + n], ps_s[:, c, 0:n], ACT.Sigmoid,
                                                    scale=-SCALE)
                    last.then_inc(keep_done, 1)
                for j in range(WU):
                    u = r * RU + G4 * KU + j
                    act.wait_ge(unit_tr, u + 1)
                    at_least(act, pv_mm, r * G4)
                    if j < 2:
                        nc.scalar.activation(wT[:, 4 * j:4 * j + 4, :].rearrange("p a b -> p (a b)"), ps_t[:, u % 2, :],
                                             ACT.Copy).then_inc(unit_ev, 1)
                    else:
                        nc.scalar.activation(wT[0:DEC_SEQ, N_PAGES, :], ps_t[0:DEC_SEQ, u % 2, 0:P],
                                             ACT.Copy).then_inc(unit_ev, 1)

        @block.vector
        def _(dve):
            nc.vector.memset(Q[:, :, :, :], 0.0).then_inc(set_up, 1)
            nc.vector.memset(zero[:, :], 0.0).then_inc(set_up, 1)
            nc.vector.memset(cp[:, ALL:ALL + 1], 1.0).then_inc(set_up, 1)
            dve.wait_ge(set_up, 3)
            dve.wait_ge(qk_tr, 1)
            nc.vector.tensor_copy(qkT[:, 1, :, :].rearrange("p h c -> p (h c)"), ps_t[:, 1, 0:HP * NS])
            for b in range(DEC_BATCH):
                for h in range(HEADS):
                    rows = slice(64 * (h % 2), 64 * (h % 2) + 64)
                    c0 = (b % G4) * R + h * DEC_SEQ
                    q0 = (h // 2) * NS + b * DEC_SEQ
                    last = nc.vector.tensor_copy(Q[rows, b, h // 2, c0:c0 + DEC_SEQ], ps_t[rows, 0, q0:q0 + DEC_SEQ])
            last.then_inc(q_ready, 1)
            dve.wait_ge(ld, n_ld)

            def chunks():
                return [(c, NC_COLS if c < 2 else DEC_SEQ) for c in range(3)]
            for r in range(ROUNDS):
                if softmax:
                    dve.wait_ge(s_mm, (r + 1) * G4)
                    dve.wait_ge(sel_ld, 16 * HEADS * G4 * (r + 1))
                    for c, n in chunks():
                        cols = slice(c * NC_COLS, c * NC_COLS + n)
                        last = nc.vector.scalar_tensor_tensor(ex[:, cols], ps_s[:, c, 0:n], SCALE, sel[:, cols],
                                                              ALU.mult, ALU.add)
                    last.then_inc(keep_done, 1)
                    dve.wait_ge(keep_done, r + 1)
                    nc.vector.tensor_tensor(ex[:, PAST_LEN - 256:ALL], ex[:, PAST_LEN - 256:ALL], near[:, :],
                                            ALU.add).then_inc(own, 1)
                    dve.wait_ge(own, 2 * r + 1)
                    nc.vector.tensor_reduce(stat[:, 0:1], ex[:, :], AX_X, ALU.max, negate=True).then_inc(own, 1)
                    dve.wait_ge(out_sum, r + 1)
                    nc.vector.reciprocal(stat[:, 2:3], stat[:, 1:2]).then_inc(inv_done, 1)
                    dve.wait_ge(inv_done, r + 1)
                    at_least(dve, unit_tr, r * RU)
                    nc.vector.tensor_scalar(w[:, :], cp[:, 0:ALL], stat[:, 2:3], None, ALU.mult).then_inc(w_done, 1)
                else:
                    dve.wait_ge(keep_done, r + 1)
                    nc.vector.tensor_tensor(ex[:, PAST_LEN:ALL], ex[:, PAST_LEN:ALL], late[:, :], ALU.max).then_inc(own, 1)
                    dve.wait_ge(own, 2 * r + 1)
                    nc.vector.tensor_tensor_scan(cp[:, 0:ALL][:, ::-1], ex[:, :][:, ::-1], wide(zero[:, :], [P, ALL]), 1.0,
                                                 ALU.mult, ALU.add).then_inc(own, 1)
                    dve.wait_ge(own, 2 * r + 2)
                    at_least(dve, unit_tr, r * RU)
                    nc.vector.tensor_tensor(w[:, :], cp[:, 1:ALL + 1], cp[:, 0:ALL], ALU.subtract).then_inc(w_done, 1)
                for g in range(G4):
                    b = r * G4 + g
                    dve.wait_ge(pv_mm, b + 1)
                    at_least(dve, out_ready, b)
                    nc.vector.tensor_tensor(tmp[:, :].rearrange("p (h d) -> p h d", h=HEADS),
                                            ps_o[0:R, b % 2, :].rearrange("p (h d) -> p h d", h=HEADS),
                                            wide(own_head[:, :].unsqueeze(2), [R, HEADS, HEAD_DIM]), ALU.mult
                                            ).then_inc(o_ev, 1)
                    dve.wait_ge(o_ev, b + 1)
                    nc.vector.tensor_reduce(out[:, b, :], tmp[:, :].rearrange("p (h d) -> p d h", h=HEADS), AX_X,
                                            ALU.add).then_inc(out_ready, 1)


NOT_SELECTED = -1e30
CAUSAL = -3e38
TAKEN = -3.3e38
C_Q = RWKV_IN
C_K = C_Q + HALF
C_V = C_K + HALF
C_IQ = C_V + HALF
C_IW = C_IQ + IDX_HEADS * IDX_DIM
C_IK = C_IW + IDX_HEADS


def skewed(row_block, first, width, n):
    flat = row_block.rearrange("p l -> (p l)")
    return flat[0:n * (NEAR - 1)].rearrange("(p l) -> p l", l=NEAR - 1)[:, first:first + width]


def bias_tables(nc, A, D, near_sample):
    with Phase(nc, "bias") as ph:
        rel = ph.sb("rel", [REL_BUCKETS, 2, HEADS])
        diff = ph.sb("diff", [REL_BUCKETS, HEADS])
        wide_rel = ph.sb("wide_rel", [REL_BUCKETS, HEADS, P])
        onehot = ph.sb("onehot", [REL_BUCKETS, NEAR])
        rows = ph.sb("rows", [P, HEADS, NEAR])
        ps = ph.ps("ps", [P, 2, NC_COLS])
        ld = ph.sem("ld")
        own = ph.sem("own")
        mm = ph.sem("mm")
        ev = ph.sem("ev")
        st = ph.sem("st")
        st2 = ph.sem("st2")
        block = ph.block()

        @block.sync
        def _(sp):
            sp.dma_start(rel[:, 0, :], A["rel_bias"]).then_inc(ld, 16)
            sp.dma_start(rel[:, 1, :], A["rel_bias"][REL_BUCKETS - 1:REL_BUCKETS, :]
                         .broadcast_to([REL_BUCKETS, HEADS])).then_inc(ld, 16)
            sp.dma_start(onehot[:, :], A["c_onehot"]).then_inc(ld, 16)
            sp.wait_ge(ev, HEADS)
            sp.dma_start(D.rearrange("h p l -> p h l"), rows[:, :, :]).then_inc(st, 16)
            sp.wait_ge(st, 16)
            for h in range(HEADS):
                sp.dma_start(near_sample[h * DEC_SEQ:(h + 1) * DEC_SEQ, :],
                             skewed(D[h], NEAR_TOP - 256, 256 + DEC_SEQ, DEC_SEQ)).then_inc(st2, 16)
            sp.wait_ge(st2, 16 * HEADS)

        @block.vector
        def _(dve):
            dve.wait_ge(ld, 48)
            nc.vector.tensor_tensor(diff[:, :], rel[:, 0, :], rel[:, 1, :], ALU.subtract).then_inc(own, 1)
            dve.wait_ge(own, 1)
            nc.vector.tensor_copy(wide_rel[:, :, :], wide(diff[:, :].unsqueeze(2), [REL_BUCKETS, HEADS, P])
                                  ).then_inc(own, 1)
            for h in range(HEADS):
                dve.wait_ge(mm, h + 1)
                nc.vector.tensor_copy(rows[:, h, :], ps[:, h % 2, 0:NEAR]).then_inc(ev, 1)

        @block.tensor
        def _(pe):
            pe.wait_ge(own, 2)
            for h in range(HEADS):
                at_least(pe, ev, h - 1)
                nc.tensor.matmul(ps[:, h % 2, 0:NEAR], wide_rel[:, h, :], onehot[:, :], start=True, stop=True
                                 ).then_inc(mm, 1)


def qk_norm(nc, A, proj, q_out, k_out):
    N = 2 * HEADS
    with Phase(nc, "qkn") as ph:
        x = ph.sb("x", [P, 2, 2 * HALF])
        sq = ph.sb("sq", [P, 2, 2 * HALF])
        y = ph.sb("y", [P, 2, 2 * HALF])
        gain = ph.sb("gain", [P, 2, HEAD_DIM])
        stat = ph.sb("stat", [P, 3, 2, N])
        eps = ph.sb("eps", [P, 1])
        const_ld = ph.sem("const_ld")
        ld = [ph.sem(f"ld{i}") for i in range(2)]
        st = [ph.sem(f"st{i}") for i in range(2)]
        set_up = ph.sem("set_up")
        squared = ph.sem("squared")
        summed = ph.sem("summed")
        rooted = ph.sem("rooted")
        own = ph.sem("own")
        ready = ph.sem("ready")
        block = ph.block()

        @block.sync
        def _(sp):
            for i, nm in enumerate(["dsa_q_norm_g", "dsa_k_norm_g"]):
                sp.dma_start(gain[:, i, :], A[nm].broadcast_to([P, HEAD_DIM])).then_inc(const_ld, 16)
            for t in range(TT):
                at_least(sp, ready, t - 1)
                sp.dma_start(x[0:rows_of(t), t % 2, :], proj[t * P:t * P + rows_of(t), C_Q:C_V]).then_inc(ld[t % 2], 16)

        @block.gpsimd
        def _(pool):
            for t in range(TT):
                r = rows_of(t)
                pool.wait_ge(ready, t + 1)
                pool.dma_start(q_out(t), y[0:r, t % 2, 0:HALF]).then_inc(st[t % 2], 16)
                pool.dma_start(k_out(t), y[0:r, t % 2, HALF:]).then_inc(st[t % 2], 16)
            for i in range(2):
                pool.wait_ge(st[i], 32 * ((TT + 1 - i) // 2))

        @block.scalar
        def _(act):
            act.wait_ge(set_up, 1)
            for t in range(TT):
                r = rows_of(t)
                act.wait_ge(ld[t % 2], 16 * (t // 2 + 1))
                at_least(act, summed, t - 1)
                nc.scalar.activation(sq[0:r, t % 2, :], x[0:r, t % 2, :], ACT.Square).then_inc(squared, 1)
                act.wait_ge(summed, t + 1)
                nc.scalar.activation(stat[0:r, 1, t % 2, :], stat[0:r, 0, t % 2, :], ACT.Sqrt, bias=eps[0:r, :],
                                     scale=1.0 / HEAD_DIM).then_inc(rooted, 1)

        @block.vector
        def _(dve):
            nc.vector.memset(eps[:, :], RMS_EPS).then_inc(set_up, 1)
            dve.wait_ge(const_ld, 32)
            link = Chain(dve, own)
            for t in range(TT):
                r, s = rows_of(t), t % 2
                dve.wait_ge(squared, t + 1)
                nc.vector.tensor_reduce(stat[0:r, 0, s, :], sq[0:r, s, :].rearrange("p (n d) -> p n d", n=N), AX_X,
                                        ALU.add).then_inc(summed, 1)
                dve.wait_ge(rooted, t + 1)
                link(nc.vector.reciprocal(stat[0:r, 2, s, :], stat[0:r, 1, s, :]))
                if t >= 2:
                    dve.wait_ge(st[s], 32 * (t // 2))
                yv = y[0:r, s, :].rearrange("p (n d) -> p n d", n=N)
                link(nc.vector.tensor_tensor(yv, x[0:r, s, :].rearrange("p (n d) -> p n d", n=N),
                                             wide(stat[0:r, 2, s, :].unsqueeze(2), [r, N, HEAD_DIM]), ALU.mult))
                yg = y[0:r, s, :].rearrange("p (i n d) -> p i n d", i=2, n=HEADS)
                nc.vector.tensor_tensor(yg, yg, wide(gain[0:r, :, :].unsqueeze(2), [r, 2, HEADS, HEAD_DIM]), ALU.mult
                                        ).then_inc(ready, 1)


T0 = TOPK // P
ALL_KEYS = PAST_LEN + DEC_SEQ
N_EARLY = 2


def score_keys(nc, A, proj, pool_ik, scores, scores_sample, sel):
    ALL = ALL_KEYS
    R = IDX_HEADS * DEC_SEQ
    with Phase(nc, "idx") as ph:
        ident = ph.sb("ident", [P, P])
        iq = ph.sb("iq", [P, PT, IDX_HEADS * IDX_DIM])
        iw = ph.sb("iw", [P, PT, IDX_HEADS])
        ik = ph.sb("ik", [P, PT, IDX_DIM])
        iqT = ph.sb("iqT", [IDX_DIM, IDX_HEADS, SEQ])
        ikT = ph.sb("ikT", [IDX_DIM, SEQ])
        relu = ph.sb("relu", [P, 2, SEQ])
        score = ph.sb("score", [P, 3, ALL])
        picked = ph.sb("picked", [P, N_EARLY, ALL])
        best = ph.sb("best", [P, 8])
        diag = ph.sb("diag", [P, 2, P])
        late = ph.sb("late", [NS, DEC_SEQ])
        early = ph.sb("early", [P, P])
        table = ph.sb("table", [1, DEC_BATCH * N_PAGES], I32)
        pages = ph.sb("pages", [P, DEC_BATCH, N_PAGES, IDX_DIM])
        s_rows = ph.sb("s_rows", [NS, (IDX_HEADS + 1) * IDX_DIM])
        w_col = ph.sb("w_col", [R, DEC_BATCH])
        w_mask = ph.sb("w_mask", [R, DEC_BATCH, NS])
        W = ph.sb("W", [R, DEC_BATCH, NS])
        s_qT = ph.sb("s_qT", [IDX_DIM, DEC_BATCH, IDX_HEADS, DEC_SEQ])
        s_kT = ph.sb("s_kT", [IDX_DIM, NS])
        b_kT = ph.sb("b_kT", [IDX_DIM, 2, PAST_LEN])
        b_relu = ph.sb("b_relu", [R, 2, ALL])
        ps = ph.ps("ps", [P, 8, NC_COLS])
        ld = ph.sem("ld")
        table_ld = ph.sem("table_ld")
        page_ld = ph.sem("page_ld")
        tr = ph.sem("tr")
        tr_ev = ph.sem("tr_ev")
        w_ready = ph.sem("w_ready")
        s_mm = ph.sem("s_mm")
        relu_done = ph.sem("relu_done")
        added = ph.sem("added")
        b_mm = ph.sem("b_mm")
        b_relu_done = ph.sem("b_relu_done")
        b_sum = ph.sem("b_sum")
        score_copied = ph.sem("score_copied")
        own = ph.sem("own")
        score_ready = ph.sem("score_ready")
        st = ph.sem("st")
        st_masks = ph.sem("st_masks")
        picked_ready = ph.sem("picked_ready")
        picked_st = ph.sem("picked_st")
        causal_ready = ph.sem("causal_ready")
        rows_ld = [ph.sem(f"rows_ld{i}") for i in range(3)]
        n_ld = 16 * (1 + 3 + 4 + 1 + 1 + IDX_HEADS)
        n_tiles = PT - T0 + 1
        block = ph.block()

        @block.sync
        def _(sp):
            sp.dma_start(table[:, :], A["page_table"].rearrange("b n -> (b n)").unsqueeze(0)).then_inc(table_ld, 16)
            sp.dma_start(ident[:, :], A["c_ident"]).then_inc(ld, 16)
            v = proj[0:SEQ, :].rearrange("(t p) n -> p t n", p=P)
            sp.dma_start(iq[:, :, :], v[:, :, C_IQ:C_IW]).then_inc(ld, 16)
            sp.dma_start(iw[:, :, :], v[:, :, C_IW:C_IK]).then_inc(ld, 16)
            sp.dma_start(ik[:, :, :], v[:, :, C_IK:ODD_IN]).then_inc(ld, 16)
            sp.dma_start(diag[:, 0, :], A["c_causal"]).then_inc(ld, 16)
            sp.dma_start(diag[:, 1, :], A["c_unselected"]).then_inc(ld, 16)
            sp.dma_start(late[:, :], A["c_late_causal"]).then_inc(ld, 16)
            sp.dma_start(w_mask[:, :, :], A["c_w_mask"]).then_inc(ld, 16)
            sp.dma_start(s_rows[:, 0:C_IW - C_IQ], proj[SEQ:TOK, C_IQ:C_IW]).then_inc(ld, 16)
            sp.dma_start(s_rows[:, C_IW - C_IQ:], proj[SEQ:TOK, C_IK:ODD_IN]).then_inc(ld, 16)
            for h in range(IDX_HEADS):
                sp.dma_start(w_col[h * DEC_SEQ:(h + 1) * DEC_SEQ, :],
                             proj[SEQ:TOK, C_IW + h:C_IW + h + 1].rearrange("(b s) o -> s (b o)", s=DEC_SEQ),
                             allow_slow_non_contiguous=True).then_inc(ld, 16)
            sp.wait_ge(table_ld, 16)
            for n in range(DEC_BATCH * N_PAGES):
                row = sp.value_load(table[0:1, n:n + 1], min_val=0, max_val=pool_ik.shape[0] - 1)
                sp.dma_start(pages[:, n // N_PAGES, n % N_PAGES, :], pool_ik[row]).then_inc(page_ld, 16)
            sp.wait_ge(ld, n_ld)
            for t in range(T0):
                sp.dma_start(sel[t, :, t * P:(t + 1) * P], diag[:, 1, :]).then_inc(st_masks, 16)
                if t:
                    sp.wait_ge(causal_ready, 1)
                    for j in range(t):
                        sp.dma_start(sel[t, :, j * P:(j + 1) * P], early[:, :]).then_inc(st_masks, 16)
            for i in range(N_EARLY, n_tiles):
                sp.wait_ge(score_ready, i + 1)
                if i == n_tiles - 1:
                    sp.dma_start(scores_sample, score[0:NS, i % 3, :]).then_inc(rows_ld[i % 3], 16)
                else:
                    t = T0 + i
                    sp.dma_start(scores[t, :, 0:(t + 1) * P], score[:, i % 3, 0:(t + 1) * P]).then_inc(rows_ld[i % 3], 16)
            for i in range(N_EARLY):
                t = T0 + i
                sp.wait_ge(picked_ready, i + 1)
                sp.dma_start(sel[t, :, 0:(t + 1) * P], picked[:, i, 0:(t + 1) * P]).then_inc(picked_st, 16)
            sp.wait_ge(picked_st, 16 * N_EARLY)
            sp.wait_ge(st_masks, 16 * 3)
            for s in range(3):
                sp.wait_ge(rows_ld[s], 16 * len(range(N_EARLY, n_tiles)[(s - N_EARLY) % 3::3]))

        QB = SEQ // NC_COLS
        PAIR = [(0, 1), (2, 6)]
        N_TURNED = IDX_HEADS * QB + QB
        turned_bank = lambda u: 6 + u % 2 if u < N_TURNED else 7
        groups_after = {PT - 4 + i: (2 * i, 2 * i + 1) for i in range(DEC_BATCH // 2)}

        @block.tensor
        def _(pe):
            u = 0

            def unit(srcs, rows):
                nonlocal u
                at_least(pe, tr_ev, u - 1 if u < N_TURNED else u)
                for j, src in enumerate(srcs):
                    n = src.shape[0]
                    last = nc.tensor.transpose(ps[0:src.shape[1], turned_bank(u), j * n:(j + 1) * n], src, ident[0:n, 0:n])
                last.then_inc(tr, 1)
                u += 1

            def group(b):
                if b == 0:
                    unit([s_rows[:, h * IDX_DIM:(h + 1) * IDX_DIM] for h in range(IDX_HEADS + 1)], IDX_DIM)
                    pe.wait_ge(page_ld, 16 * DEC_BATCH * N_PAGES)
                for c in range(2):
                    unit([pages[:, b, 4 * c + j, :] for j in range(4)], IDX_DIM)
                pe.wait_ge(tr_ev, u)
                at_least(pe, b_relu_done, b)
                for c in range(3):
                    n = NC_COLS if c < 2 else DEC_SEQ
                    rhs = b_kT[:, b % 2, c * NC_COLS:c * NC_COLS + n] if c < 2 else s_kT[:, b * DEC_SEQ:(b + 1) * DEC_SEQ]
                    last = nc.tensor.matmul(ps[0:R, c, 0:n], s_qT[:, b].rearrange("p h q -> p (h q)"), rhs,
                                            start=True, stop=True)
                last.then_inc(b_mm, 1)
                pe.wait_ge(b_relu_done, b + 1)
                if b == 0:
                    pe.wait_ge(w_ready, 1)
                for c in range(3):
                    n = NC_COLS if c < 2 else DEC_SEQ
                    last = nc.tensor.matmul(ps[0:NS, 3 + c, 0:n], W[:, b, :], b_relu[:, b % 2, c * NC_COLS:c * NC_COLS + n],
                                            start=(b == 0), stop=(b == DEC_BATCH - 1))
                last.then_inc(b_sum, 1)

            pe.wait_ge(ld, n_ld)
            for h in range(IDX_HEADS):
                for c in range(QB):
                    unit([iq[:, 4 * c + j, h * IDX_DIM:(h + 1) * IDX_DIM] for j in range(4)], IDX_DIM)
            for c in range(QB):
                unit([ik[:, 4 * c + j, :] for j in range(4)], IDX_DIM)
            pe.wait_ge(tr_ev, u)
            n = 0
            for t in range(T0, PT):
                for h in range(IDX_HEADS):
                    at_least(pe, relu_done, n - 1)
                    for c, (b0, m) in enumerate(key_blocks(t)):
                        last = nc.tensor.matmul(ps[:, PAIR[n % 2][c], 0:m * P], iqT[:, h, t * P:(t + 1) * P],
                                                ikT[:, b0 * P:(b0 + m) * P], start=True, stop=True)
                    last.then_inc(s_mm, 1)
                    n += 1
                if t in groups_after:
                    pe.wait_ge(relu_done, n)
                    for b in groups_after[t]:
                        group(b)

        @block.scalar
        def _(act):
            u = 0

            def turned(dst, cols, view=None):
                nonlocal u
                act.wait_ge(tr, u + 1)
                src = ps[0:IDX_DIM, turned_bank(u), 0:cols]
                nc.scalar.activation(dst, view(src) if view else src, ACT.Copy).then_inc(tr_ev, 1)
                u += 1

            def group(b):
                if b == 0:
                    act.wait_ge(tr, u + 1)
                    nc.scalar.activation(s_kT[:, :], ps[0:IDX_DIM, turned_bank(u), IDX_HEADS * NS:(IDX_HEADS + 1) * NS],
                                         ACT.Copy)
                    turned(s_qT[:, :, :, :], IDX_HEADS * NS,
                           lambda x: x.rearrange("p (h b q) -> p b h q", h=IDX_HEADS, q=DEC_SEQ))
                at_least(act, b_mm, b - 1)
                for c in range(2):
                    turned(b_kT[:, b % 2, c * NC_COLS:(c + 1) * NC_COLS], NC_COLS)
                act.wait_ge(b_mm, b + 1)
                at_least(act, b_sum, b - 1)
                for c in range(3):
                    n = NC_COLS if c < 2 else DEC_SEQ
                    last = nc.scalar.activation(b_relu[:, b % 2, c * NC_COLS:c * NC_COLS + n], ps[0:R, c, 0:n], ACT.Relu)
                last.then_inc(b_relu_done, 1)

            for h in range(IDX_HEADS):
                for c in range(QB):
                    turned(iqT[:, h, c * NC_COLS:(c + 1) * NC_COLS], NC_COLS)
            for c in range(QB):
                turned(ikT[:, c * NC_COLS:(c + 1) * NC_COLS], NC_COLS)
            n = 0
            for t in range(T0, PT):
                for h in range(IDX_HEADS):
                    act.wait_ge(s_mm, n + 1)
                    at_least(act, added, n - 1)
                    for c, (b0, m) in enumerate(key_blocks(t)):
                        last = nc.scalar.activation(relu[:, n % 2, b0 * P:(b0 + m) * P], ps[:, PAIR[n % 2][c], 0:m * P],
                                                    ACT.Relu)
                    last.then_inc(relu_done, 1)
                    n += 1
                for b in groups_after.get(t, ()):
                    group(b)

        @block.vector
        def _(dve):
            link = Chain(dve, own)
            nc.vector.memset(early[:, :], 0.0).then_inc(causal_ready, 1)
            dve.wait_ge(ld, n_ld)
            nc.vector.tensor_tensor(W[:, :, :], w_mask[:, :, :], wide(w_col[:, :].unsqueeze(2), [R, DEC_BATCH, NS]),
                                    ALU.mult).then_inc(w_ready, 1)

            link = Chain(dve, own)

            def pick(i):
                width = (T0 + i + 1) * P
                row = score[:, i % 3, 0:width]
                for _ in range(TOPK // 8):
                    link(nc.vector.max(best[:, :], row))
                    link(nc.vector.match_replace(row, best[:, :], row, TAKEN))
                nc.vector.tensor_scalar(picked[:, i, 0:width], row, TAKEN, NOT_SELECTED, ALU.not_equal,
                                        ALU.mult).then_inc(picked_ready, 1)

            def slot_stored(i):
                if i - 3 >= N_EARLY:
                    dve.wait_ge(rows_ld[i % 3], 16 * len(range(N_EARLY, i - 2)[(i - N_EARLY) % 3::3]))
                elif i >= 3:
                    dve.wait_ge(picked_ready, i - 2)

            n = 0
            for t in range(T0, PT):
                i = t - T0
                width = (t + 1) * P
                row = score[:, i % 3]
                slot_stored(i)
                for h in range(IDX_HEADS):
                    dve.wait_ge(relu_done, n + 1)
                    at_least(dve, added, n)
                    r_ = relu[:, n % 2, 0:width]
                    if h == 0:
                        nc.vector.tensor_scalar(row[:, 0:width], r_, iw[:, t, 0:1], None, ALU.mult).then_inc(added, 1)
                    else:
                        nc.vector.scalar_tensor_tensor(row[:, 0:width], r_, iw[:, t, h:h + 1], row[:, 0:width],
                                                       ALU.mult, ALU.add).then_inc(added, 1)
                    n += 1
                dve.wait_ge(added, n)
                nc.vector.tensor_tensor(row[:, t * P:width], row[:, t * P:width], diag[:, 0, :],
                                        ALU.add).then_inc(score_ready, 1)
                if t in groups_after and i - 2 < N_EARLY:
                    dve.wait_ge(score_ready, i + 1)
                    pick(i - 2)
            i = n_tiles - 1
            row = score[0:NS, i % 3]
            dve.wait_ge(b_sum, DEC_BATCH)
            slot_stored(i)
            for c in range(3):
                m = NC_COLS if c < 2 else DEC_SEQ
                last = nc.vector.tensor_copy(row[:, c * NC_COLS:c * NC_COLS + m], ps[0:NS, 3 + c, 0:m])
            last.then_inc(score_copied, 1)
            dve.wait_ge(score_copied, 1)
            nc.vector.tensor_tensor(row[:, PAST_LEN:ALL], row[:, PAST_LEN:ALL], late[:, :], ALU.add).then_inc(score_ready, 1)


def key_picker(nc, ph, scores, scores_sample, sel, sel_sample):
    SLOTS = 3
    score = ph.sb("pick_score", [P, SLOTS, ALL_KEYS])
    picked = ph.sb("picked", [P, 2, ALL_KEYS])
    best = ph.sb("best", [P, 8])
    score_ld = [ph.sem(f"score_ld{i}") for i in range(SLOTS)]
    taken = ph.sem("taken")
    picked_ready = ph.sem("picked_ready")
    picked_st = [ph.sem(f"picked_st{i}") for i in range(2)]
    jobs = [(scores[t, :, 0:(t + 1) * P], sel[t, :, 0:(t + 1) * P], P, (t + 1) * P) for t in range(T0 + N_EARLY, PT)]
    jobs.append((scores_sample, sel_sample, NS, ALL_KEYS))
    per_job = TOPK // 8
    done = 0

    def load_scores(eng, i):
        at_least(eng, picked_ready, i - SLOTS + 1)
        src, _, r, width = jobs[i]
        eng.dma_start(score[0:r, i % SLOTS, 0:width], src).then_inc(score_ld[i % SLOTS], 16)

    def store_rows(eng, i):
        eng.wait_ge(picked_ready, i + 1)
        _, dst, r, width = jobs[i]
        eng.dma_start(dst, picked[0:r, i % 2, 0:width]).then_inc(picked_st[i % 2], 16)

    def rows_stored(eng):
        for s in range(2):
            eng.wait_ge(picked_st[s], 16 * ((len(jobs) + 1 - s) // 2))

    def pick_round(dve):
        nonlocal done
        if done == PICK_ROUNDS:
            return
        i, k = done // per_job, done % per_job
        _, _, r, width = jobs[i]
        row = score[0:r, i % SLOTS, 0:width]
        if k == 0:
            dve.wait_ge(score_ld[i % SLOTS], 16 * (i // SLOTS + 1))
        at_least(dve, taken, 2 * done)
        nc.vector.max(best[0:r, :], row).then_inc(taken, 1)
        dve.wait_ge(taken, 2 * done + 1)
        nc.vector.match_replace(row, best[0:r, :], row, TAKEN).then_inc(taken, 1)
        done += 1
        if k == per_job - 1:
            dve.wait_ge(taken, 2 * done)
            if i >= 2:
                dve.wait_ge(picked_st[i % 2], 16 * (i // 2))
            nc.vector.tensor_scalar(picked[0:r, i % 2, 0:width], row, TAKEN, NOT_SELECTED, ALU.not_equal,
                                    ALU.mult).then_inc(picked_ready, 1)

    return len(jobs), load_scores, store_rows, rows_stored, pick_round


PICK_ROUNDS = (PT - T0 - N_EARLY + 1) * TOPK // 8
TILE_ROUNDS = PICK_ROUNDS // PT


DECAY_SCALE = 0.606531
GN_EPS = 64e-5
RW = 3 * HALF
CH = 64
W_A, W_NB, W_K, W_R, W_V, W_LW, W_G, W_BONUS = range(8)


def rwkv_inputs(nc, A, proj, rw):
    with Phase(nc, "rwi") as ph:
        ident = ph.sb("ident", [P, P])
        cur = ph.sb("cur", [P, 2, RWKV_IN])
        prev = ph.sb("prev", [P, 2, RWKV_IN])
        xs = ph.sb("xs", [P, 2, RWKV_IN])
        mu = ph.sb("mu", [P, RWKV_IN])
        par = ph.sb("par", [P, 5, HALF])
        wa2 = ph.sb("wa2", [P, HALF])
        g2 = ph.sb("g2", [P, HALF])
        tri = ph.sb("tri", [P, P])
        small = ph.sb("small", [P, 2 * P])
        smallT = ph.sb("smallT", [P, 2, P])
        z = ph.sb("z", [P, 2, HALF])
        a = ph.sb("a", [P, HALF])
        sw = ph.sb("sw", [P, HALF])
        kk = ph.sb("kk", [P, HALF])
        k2 = ph.sb("k2", [P, HALF])
        t1 = ph.sb("t1", [P, HALF])
        t2 = ph.sb("t2", [P, HALF])
        e = ph.sb("e", [P, 3, HALF])
        cx = ph.sb("cx", [P, HALF])
        stat = ph.sb("stat", [P, 4, HEADS])
        out = ph.sb("out", [P, 2, 8, HALF])
        pt = ph.ps("pt", [P, NC_COLS])
        pm = ph.ps("pm", [P, 3, NC_COLS])
        pc = ph.ps("pc", [P, NC_COLS])
        const_ld = ph.sem("const_ld")
        ld = [ph.sem(f"ld{i}") for i in range(2)]
        zeroed = ph.sem("zeroed")
        mixed = ph.sem("mixed")
        pool_own = ph.sem("pool_own")
        small_ready = ph.sem("small_ready")
        small_tr = ph.sem("small_tr")
        small_ev = ph.sem("small_ev")
        small_mm = ph.sem("small_mm")
        z_ready = ph.sem("z_ready")
        sig_ready = ph.sem("sig_ready")
        g_ready = ph.sem("g_ready")
        lw_ready = ph.sem("lw_ready")
        cum_mm = ph.sem("cum_mm")
        cx_ready = ph.sem("cx_ready")
        e_ready = ph.sem("e_ready")
        sq_ready = ph.sem("sq_ready")
        norm2 = ph.sem("norm2")
        root = ph.sem("root")
        own = ph.sem("own")
        done = ph.sem("done")
        st = [ph.sem(f"st{i}") for i in range(2)]
        n_const = 16 * (1 + 1 + 5 + 2 + 1 + 1)
        block = ph.block()

        @block.sync
        def _(sp):
            sp.dma_start(ident[:, :], A["c_ident"]).then_inc(const_ld, 16)
            sp.dma_start(tri[:, :], A["c_chunk_tri"]).then_inc(const_ld, 16)
            sp.dma_start(mu[:, :], A["rwkv_mu"].broadcast_to([P, RWKV_IN])).then_inc(const_ld, 16)
            for i, nm in enumerate(["rwkv_w0", "rwkv_a0", "rwkv_k_k", "rwkv_k_a", "rwkv_r_k"]):
                v = A[nm].rearrange("a h d -> a (h d)") if nm == "rwkv_r_k" else A[nm]
                sp.dma_start(par[:, i, :], v.broadcast_to([P, HALF])).then_inc(const_ld, 16)
            sp.dma_start(wa2[0:64, :], A["rwkv_w2"][0]).then_inc(const_ld, 16)
            sp.dma_start(wa2[64:P, :], A["rwkv_a2"][0]).then_inc(const_ld, 16)
            sp.dma_start(g2[:, :], A["rwkv_g2"][0]).then_inc(const_ld, 16)
            def store(t):
                r, s = rows_of(t), t % 2
                sp.wait_ge(done, t + 1)
                sp.dma_start(rw[t * P:t * P + r, :, :], out[0:r, s, :, :]).then_inc(st[s], 16)

            for t in range(TT):
                r, s = rows_of(t), t % 2
                at_least(sp, mixed, t - 1)
                sp.dma_start(cur[0:r, s, :], proj[t * P:t * P + r, 0:RWKV_IN]).then_inc(ld[s], 16)
                if t == 0:
                    sp.dma_start(prev[1:P, s, :], proj[0:P - 1, 0:RWKV_IN]).then_inc(ld[s], 16)
                elif t < PT:
                    sp.dma_start(prev[:, s, :], proj[t * P - 1:(t + 1) * P - 1, 0:RWKV_IN]).then_inc(ld[s], 16)
                else:
                    pv = proj[SEQ:TOK, 0:RWKV_IN].rearrange("(b s) c -> s b c", s=DEC_SEQ)
                    for q in range(DEC_SEQ):
                        sp.dma_start(prev[q:NS:DEC_SEQ, s, :], pv[q - 1] if q else A["state_rwkv_shift"][0]
                                     ).then_inc(ld[s], 16)
                if t >= 2:
                    store(t - 2)
            store(TT - 2)
            store(TT - 1)
            for s in range(2):
                sp.wait_ge(st[s], 16 * ((TT + 1 - s) // 2))

        def loaded(t):
            return 16 * (2 * (t // 2 + 1) + (3 if t == PT else 0))

        @block.gpsimd
        def _(pool):
            nc.gpsimd.memset(prev[0:1, 0, :], 0.0).then_inc(zeroed, 1)
            pool.wait_ge(zeroed, 1)
            pool.wait_ge(const_ld, n_const)
            n = 0
            for t in range(TT):
                r, s = rows_of(t), t % 2
                pool.wait_ge(ld[s], loaded(t))
                x, y = cur[0:r, s, :], prev[0:r, s, :]
                nc.gpsimd.tensor_tensor(y, y, x, ALU.subtract).then_inc(pool_own, 1)
                pool.wait_ge(pool_own, n + 1)
                nc.gpsimd.tensor_tensor(y, y, mu[0:r, :], ALU.mult).then_inc(pool_own, 1)
                pool.wait_ge(pool_own, n + 2)
                at_least(pool, done, t - 1)
                nc.gpsimd.tensor_tensor(xs[0:r, s, :], x, y, ALU.add).then_inc(mixed, 1)
                n += 2

        @block.tensor
        def _(pe):
            pe.wait_ge(const_ld, n_const)
            for t in range(TT):
                r = rows_of(t)
                pe.wait_ge(small_ready, 3 * (t + 1))
                for i in range(2):
                    last = nc.tensor.transpose(pt[:, i * P:i * P + r], small[0:r, i * P:(i + 1) * P], ident[0:r, 0:r])
                last.then_inc(small_tr, 1)
                pe.wait_ge(small_ev, t + 1)
                at_least(pe, z_ready, 2 * t)
                at_least(pe, g_ready, t)
                nc.tensor.matmul(pm[0:r, 0, :], smallT[0:64, 0, 0:r], wa2[0:64, :], start=True, stop=True)
                nc.tensor.matmul(pm[0:r, 1, :], smallT[64:P, 0, 0:r], wa2[64:P, :], start=True, stop=True)
                nc.tensor.matmul(pm[0:r, 2, :], smallT[:, 1, 0:r], g2[:, :], start=True, stop=True).then_inc(small_mm, 1)
                if t < PT:
                    pe.wait_ge(lw_ready, t + 1)
                    nc.tensor.matmul(pc[:, :], tri[:, :], out[:, t % 2, W_LW, :], start=True, stop=True).then_inc(cum_mm, 1)

        @block.scalar
        def _(act):
            for t in range(TT):
                r, s = rows_of(t), t % 2
                act.wait_ge(mixed, t + 1)
                at_least(act, small_tr, t)
                x = xs[0:r, s, :]
                nc.scalar.activation(small[0:r, 0:64], x[:, RW:RW + 64], ACT.Tanh).then_inc(small_ready, 1)
                nc.scalar.activation(small[0:r, 64:P], x[:, RW + 64:RW + P], ACT.Copy).then_inc(small_ready, 1)
                nc.scalar.activation(small[0:r, P:], x[:, RW + P:RWKV_IN], ACT.Sigmoid).then_inc(small_ready, 1)
                act.wait_ge(z_ready, 2 * (t + 1))
                at_least(act, done, t)
                nc.scalar.activation(sw[0:r, :], z[0:r, 0, :], ACT.Sigmoid).then_inc(sig_ready, 1)
                nc.scalar.activation(a[0:r, :], z[0:r, 1, :], ACT.Sigmoid).then_inc(sig_ready, 1)
                act.wait_ge(small_mm, t + 1)
                if t >= 2:
                    act.wait_ge(st[s], 16 * (t // 2))
                nc.scalar.activation(out[0:r, s, W_G, :], pm[0:r, 2, :], ACT.Copy).then_inc(g_ready, 1)
                nc.scalar.activation(out[0:r, s, W_V, :], x[:, 2 * HALF:RW], ACT.Copy)
                act.wait_ge(sq_ready, t + 1)
                nc.scalar.activation(t1[0:r, :], kk[0:r, :], ACT.Square).then_inc(norm2, 1)
                act.wait_ge(root, 2 * t + 1)
                nc.scalar.activation(stat[0:r, 1, :], stat[0:r, 0, :], ACT.Sqrt).then_inc(root, 1)
                if t < PT:
                    act.wait_ge(cum_mm, t + 1)
                    nc.scalar.activation(e[:, 0, :], pc[:, :], ACT.Exp).then_inc(e_ready, 1)
                    nc.scalar.activation(e[:, 1, :], pc[:, :], ACT.Exp, scale=-1.0).then_inc(e_ready, 1)
                    act.wait_ge(cx_ready, t + 1)
                    nc.scalar.activation(e[:, 2, :], cx[:, :], ACT.Exp).then_inc(e_ready, 1)
                else:
                    act.wait_ge(lw_ready, t + 1)
                    nc.scalar.activation(e[0:r, 0, :], cx[0:r, :], ACT.Exp).then_inc(e_ready, 3)

        @block.vector
        def _(dve):
            link = Chain(dve, own)
            tt = nc.vector.tensor_tensor
            stt = nc.vector.scalar_tensor_tensor
            dve.wait_ge(const_ld, n_const)
            for t in range(TT):
                r, s = rows_of(t), t % 2
                o = out[0:r, s]
                heads = lambda x: x.rearrange("p (h d) -> p h d", h=HEADS)
                pr = lambda i: par[0:r, i, :]
                dve.wait_ge(mixed, t + 1)
                rr, kx = xs[0:r, s, 0:HALF], xs[0:r, s, HALF:2 * HALF]
                dve.wait_ge(small_tr, t + 1)
                nc.vector.tensor_copy(smallT[:, :, 0:r], pt[:, 0:2 * P].rearrange("p (i c) -> p i c", i=2)[:, :, 0:r]
                                      ).then_inc(small_ev, 1)
                tt(kk[0:r, :], kx, pr(2), ALU.mult).then_inc(sq_ready, 1)
                dve.wait_ge(small_mm, t + 1)
                at_least(dve, sig_ready, 2 * t)
                for i in range(2):
                    tt(z[0:r, i, :], pm[0:r, i, :], pr(i), ALU.add).then_inc(z_ready, 1)
                dve.wait_ge(sig_ready, 2 * t + 2)
                if t >= 2:
                    dve.wait_ge(st[s], 16 * (t // 2))
                lw = o[:, W_LW, :] if t < PT else cx[0:r, :]
                nc.vector.tensor_scalar(lw, sw[0:r, :], -DECAY_SCALE, None, ALU.mult).then_inc(lw_ready, 1)
                dve.wait_ge(norm2, t + 1)
                nc.vector.tensor_reduce(stat[0:r, 0, :], heads(t1[0:r, :]), AX_X, ALU.add).then_inc(root, 1)
                dve.wait_ge(root, 2 * t + 2)
                link(nc.vector.tensor_scalar(stat[0:r, 2, :], stat[0:r, 1, :], 1e-12, None, ALU.max))
                link(nc.vector.reciprocal(stat[0:r, 3, :], stat[0:r, 2, :]))
                link(tt(heads(kk[0:r, :]), heads(kk[0:r, :]), wide(stat[0:r, 3, :].unsqueeze(2), [r, HEADS, HEAD_DIM]),
                        ALU.mult))
                link(stt(t2[0:r, :], a[0:r, :], -1.0, pr(3), ALU.add, ALU.mult))
                link(stt(k2[0:r, :], t2[0:r, :], 1.0, kx, ALU.add, ALU.mult))
                link(tt(t2[0:r, :], rr, k2[0:r, :], ALU.mult))
                link(tt(t2[0:r, :], t2[0:r, :], pr(4), ALU.mult))
                link(nc.vector.tensor_reduce(stat[0:r, 2, :], heads(t2[0:r, :]), AX_X, ALU.add))
                link(tt(heads(o[:, W_BONUS, :]), heads(xs[0:r, s, 2 * HALF:RW]),
                        wide(stat[0:r, 2, :].unsqueeze(2), [r, HEADS, HEAD_DIM]), ALU.mult))
                if t < PT:
                    dve.wait_ge(e_ready, 3 * t + 2)
                    tt(cx[:, :], pc[:, :], o[:, W_LW, :], ALU.subtract).then_inc(cx_ready, 1)
                    dve.wait_ge(e_ready, 3 * (t + 1))
                    link(tt(o[:, W_A, :], kk[:, :], e[:, 2, :], ALU.mult))
                    link(stt(t2[:, :], kk[:, :], -1.0, a[:, :], ALU.mult, ALU.mult))
                    link(tt(o[:, W_NB, :], t2[:, :], e[:, 1, :], ALU.mult))
                    link(tt(o[:, W_K, :], k2[:, :], e[:, 1, :], ALU.mult))
                    tt(o[:, W_R, :], rr, e[:, 0, :], ALU.mult).then_inc(done, 1)
                else:
                    dve.wait_ge(e_ready, 3 * (t + 1))
                    link(nc.vector.tensor_copy(o[:, W_A, :], kk[0:r, :]))
                    link(stt(o[:, W_NB, :], kk[0:r, :], -1.0, a[0:r, :], ALU.mult, ALU.mult))
                    link(nc.vector.tensor_copy(o[:, W_K, :], k2[0:r, :]))
                    link(nc.vector.tensor_copy(o[:, W_R, :], rr))
                    nc.vector.tensor_copy(o[:, W_LW, :], e[0:r, 0, :]).then_inc(done, 1)


def rwkv_steps(nc, ph, A, rw, y_out, state_out):
    VH = CH // 2
    BH = DEC_BATCH * HEADS
    S = ph.sb("s_S", [P, VH, CH])
    vec = ph.sb("s_vec", [P, DEC_SEQ, 6, CH])
    v2 = ph.sb("s_v2", [P, DEC_SEQ, VH])
    u = ph.sb("s_u", [P, VH])
    y = ph.sb("s_y", [P, DEC_SEQ, VH])
    t1 = ph.sb("s_t1", [P, VH, CH])
    ld = ph.sem("s_ld")
    own = ph.sem("s_own")
    ready = ph.sem("s_ready")
    st = ph.sem("s_st")
    n_ld = 16 * (2 + 2 * DEC_SEQ * DEC_BATCH)

    def loads(sp):
        for x in range(2):
            rows = slice(x * BH, (x + 1) * BH)
            sp.dma_start(S[rows, :, :].rearrange("p v k -> p (v k)"),
                         A["state_rwkv"][0].rearrange("b h (x v) k -> x (b h) (v k)", x=2)[x]).then_inc(ld, 16)
            for b in range(DEC_BATCH):
                for t in range(DEC_SEQ):
                    src = rw[SEQ + b * DEC_SEQ + t, 0:6, :].rearrange("a (h d) -> h a d", h=HEADS)
                    sp.dma_start(vec[x * BH + b * HEADS:x * BH + (b + 1) * HEADS, t, :, :], src).then_inc(ld, 16)

    def stores(sp):
        sp.wait_ge(ready, 1)
        for x in range(2):
            rows = slice(x * BH, (x + 1) * BH)
            sp.dma_start(state_out.rearrange("b h (x v) k -> x (b h) (v k)", x=2)[x],
                         S[rows, :, :].rearrange("p v k -> p (v k)")).then_inc(st, 16)
            for b in range(DEC_BATCH):
                dst = y_out[SEQ + b * DEC_SEQ:SEQ + (b + 1) * DEC_SEQ, :].rearrange("t (h x v) -> x h t v", h=HEADS, x=2)[x]
                sp.dma_start(dst, y[x * BH + b * HEADS:x * BH + (b + 1) * HEADS, :, :]).then_inc(st, 16)
        sp.wait_ge(st, 16 * 2 * (1 + DEC_BATCH))

    def steps(pool):
        link = Chain(pool, own)
        tt = nc.gpsimd.tensor_tensor
        shape = [P, VH, CH]

        def sum_keys(out):
            n = CH // 2
            while n > 1:
                link(tt(t1[:, :, 0:n], t1[:, :, 0:n], t1[:, :, n:2 * n], ALU.add))
                n //= 2
            return tt(out.unsqueeze(2), t1[:, :, 0:1], t1[:, :, 1:2], ALU.add)

        pool.wait_ge(ld, n_ld)
        for x in range(2):
            rows = slice(x * BH, (x + 1) * BH)
            link(nc.gpsimd.tensor_copy(v2[rows, :, :], vec[rows, :, W_V, x * VH:(x + 1) * VH]))
        for t in range(DEC_SEQ):
            key = lambda a: wide(vec[:, t, a, :].unsqueeze(1), shape)
            link(tt(t1[:, :, :], S[:, :, :], key(W_A), ALU.mult))
            link(sum_keys(u[:, :]))
            link(tt(S[:, :, :], S[:, :, :], key(W_LW), ALU.mult))
            link(tt(t1[:, :, :], wide(u[:, :].unsqueeze(2), shape), key(W_NB), ALU.mult))
            link(tt(S[:, :, :], S[:, :, :], t1[:, :, :], ALU.add))
            link(tt(t1[:, :, :], wide(v2[:, t, :].unsqueeze(2), shape), key(W_K), ALU.mult))
            link(tt(S[:, :, :], S[:, :, :], t1[:, :, :], ALU.add))
            link(tt(t1[:, :, :], S[:, :, :], key(W_R), ALU.mult))
            last = sum_keys(y[:, t, :])
            if t + 1 < DEC_SEQ:
                link(last)
        last.then_inc(ready, 1)

    return loads, steps, stores


def rwkv_chunks(nc, A, rw, y_out, state_out, sample_state_out, scores, scores_sample, sel, sel_sample):
    HP = HEADS // 2
    TR = 4
    POW = 6
    with Phase(nc, "rwc") as ph:
        ident = ph.sb("ident", [P, P])
        eye2 = ph.sb("eye2", [P, CH])
        masks = ph.sb("masks", [P, 5, P])
        halves = ph.sb("halves", [P, 2])
        x = ph.sb("x", [P, 2, 6, HALF])
        xT = ph.sb("xT", [P, HP, TR, P])
        pr = ph.sb("pr", [P, HEADS, 4, P])
        NL = ph.sb("NL", [P, 2, 2, HEADS, P])
        Y = ph.sb("Y", [P, HEADS, 2, CH])
        RT = ph.sb("RT", [P, HP, P])
        ZN = ph.sb("ZN", [P, 2, 2, HP, CH])
        y0 = ph.sb("y0", [P, 2, HALF])
        pcs = ph.sb("pcs", [P, HP, 2])
        M = ph.sb("M", [P, HP, CH])
        Ms = ph.sb("Ms", [P, HP, CH])
        mt = ph.sb("mt", [CH, HP, P])
        ps = ph.ps("ps", [P, 8, NC_COLS])
        const_ld = ph.sem("const_ld")
        ld = [ph.sem(f"ld{i}") for i in range(2)]
        tr = ph.sem("tr")
        tr_ev = ph.sem("tr_ev")
        prod_mm = ph.sem("prod_mm")
        prod_ev = ph.sem("prod_ev")
        low_mm = ph.sem("low_mm")
        low_ev = ph.sem("low_ev")
        akv_mm = ph.sem("akv_mm")
        y_set = ph.sem("y_set")
        sq_mm = ph.sem("sq_mm")
        sq_ev = ph.sem("sq_ev")
        app_mm = ph.sem("app_mm")
        app_ev = ph.sem("app_ev")
        r_mm = ph.sem("r_mm")
        r_ev = ph.sem("r_ev")
        zn_mm = ph.sem("zn_mm")
        z_ev = ph.sem("z_ev")
        zn_ev = ph.sem("zn_ev")
        y0_mm = ph.sem("y0_mm")
        y0_ev = ph.sem("y0_ev")
        pc_ev = ph.sem("pc_ev")
        step_mm = ph.sem("step_mm")
        m_own = ph.sem("m_own")
        m_ready = ph.sem("m_ready")
        y_ready = ph.sem("y_ready")
        st = [ph.sem(f"st{i}") for i in range(2)]
        end_tr = ph.sem("end_tr")
        end_cp = ph.sem("end_cp")
        end_st = ph.sem("end_st")
        n_const = 16 * 4
        sample_loads, sample_steps, sample_stores = rwkv_steps(nc, ph, A, rw, y_out, sample_state_out)
        n_jobs, load_scores, store_rows, rows_stored, pick_round = key_picker(nc, ph, scores, scores_sample, sel,
                                                                              sel_sample)
        block = ph.block()
        ARR = [W_A, W_R, W_NB, W_K, W_V, W_LW]
        X_A, X_R, X_NB, X_K, X_V, X_LW = range(6)

        @block.sync
        def _(sp):
            sp.dma_start(ident[:, :], A["c_ident"]).then_inc(const_ld, 16)
            sp.dma_start(eye2[:, :], A["c_eye2"]).then_inc(const_ld, 16)
            sp.dma_start(masks[:, :, :], A["c_chunk_masks"]).then_inc(const_ld, 16)
            sp.dma_start(halves[:, :], A["c_halves"]).then_inc(const_ld, 16)

            def store_y(t):
                sp.wait_ge(y_ready, t + 1)
                sp.dma_start(y_out[t * P:(t + 1) * P, :], y0[:, t % 2, :]).then_inc(st[t % 2], 16)

            picked_by = lambda i: -(-(i + 1) * (TOPK // 8) // TILE_ROUNDS) - 1
            for i in range(3):
                load_scores(sp, i)
            for t in range(PT):
                at_least(sp, y_ready, t - 1)
                for i, a in enumerate(ARR):
                    sp.dma_start(x[:, t % 2, i, :], rw[t * P:(t + 1) * P, a, :]).then_inc(ld[t % 2], 16)
                if t == 1:
                    sample_loads(sp)
                for i in range(n_jobs):
                    if picked_by(i) + 2 == t:
                        store_rows(sp, i)
                        if i + 3 < n_jobs:
                            load_scores(sp, i + 3)
                if t:
                    store_y(t - 1)
            for i in range(n_jobs):
                if picked_by(i) + 2 >= PT:
                    store_rows(sp, i)
            store_y(PT - 1)
            sample_stores(sp)
            rows_stored(sp)
            for s in range(2):
                sp.wait_ge(st[s], 16 * PT // 2)
            sp.wait_ge(end_cp, 1)
            for g in range(2):
                sp.dma_start(state_out.rearrange("(i g) v k -> g v i k", g=2)[g], mt[:, :, g * CH:(g + 1) * CH]
                             ).then_inc(end_st, 16)
            sp.wait_ge(end_st, 32)

        @block.gpsimd
        def _(pool):
            sample_steps(pool)

        def sq_count(j, g):
            full = POW - 2
            before = 4 * (j - 1)
            return before + (2 * g + 2 if j <= full else g + 1)

        @block.tensor
        def _(pe):
            mm = nc.tensor.matmul
            pe.wait_ge(const_ld, n_const)
            for t in range(PT):
                s = t % 2
                hd = lambda i, h: x[:, s, i, h * CH:(h + 1) * CH]
                pe.wait_ge(ld[s], 16 * 6 * (t // 2 + 1))
                at_least(pe, low_ev, 2 * t)
                at_least(pe, sq_ev, 18 * t)
                at_least(pe, y_ready, t)
                if t:
                    pe.wait_ge(m_ready, 2 * t + 1)
                for i in range(HP):
                    for j in range(TR):
                        last = nc.tensor.transpose(ps[:, i, j * P:(j + 1) * P], x[:, s, j, i * P:(i + 1) * P], ident[:, :])
                    last.then_inc(tr, 1)
                for h in range(HEADS):
                    rows = slice(64 * (h % 2), 64 * (h % 2) + 64)
                    pe.wait_ge(tr_ev, HP * t + h // 2 + 1)
                    n = HEADS * t + h
                    at_least(pe, prod_ev, n - 3)
                    if h == 0:
                        at_least(pe, m_ready, 2 * t)
                        at_least(pe, y_ready, t)
                    b = 4 + h % 4
                    for j, q in enumerate([2, 3]):
                        last = mm(ps[:, b, j * 2 * P:(j + 1) * 2 * P], xT[rows, h // 2, q, :],
                                  xT[rows, h // 2, 0:2, :].rearrange("p a c -> p (a c)"), start=True, stop=True)
                    last.then_inc(prod_mm, 1)
                for g in range(2):
                    rows = slice(64 * g, 64 * g + 64)
                    for i in range(HP):
                        last = mm(ps[:, g, i * P:(i + 1) * P], xT[rows, i, 0, :], xT[rows, i, 2, :], start=True, stop=True)
                    last.then_inc(low_mm, 1)
                pe.wait_ge(prod_ev, HEADS * (t + 1))
                for h in range(HEADS):
                    last = mm(ps[:, 2, h * CH:(h + 1) * CH], pr[:, h, 2, :], hd(X_V, h), start=True, stop=True)
                last.then_inc(akv_mm, 1)
                pe.wait_ge(y_set, 2 * (t + 1))
                pe.wait_ge(low_ev, 2 * (t + 1))
                for j in range(POW):
                    for g in range(2):
                        hs = range(4 * g, 4 * g + 4)
                        if j:
                            pe.wait_ge(sq_ev, 18 * t + sq_count(j, g))
                        N_ = [pr[:, h, 0, :] if j == 0 else NL[:, j % 2, 0, h, :] for h in hs]
                        L_ = [NL[:, j % 2, 1, h, :] for h in hs]
                        if j + 1 < POW:
                            for i in range(4):
                                last = mm(ps[:, 2 * g, i * P:(i + 1) * P], L_[i], N_[i], start=True, stop=True)
                            last.then_inc(sq_mm, 1)
                            if j + 2 < POW:
                                for i in range(4):
                                    last = mm(ps[:, 2 * g + 1, i * P:(i + 1) * P], N_[i], L_[i], start=True, stop=True)
                                last.then_inc(sq_mm, 1)
                        at_least(pe, app_ev, 2 * POW * t + 2 * (j - 1) + g + 1)
                        for i, h in enumerate(hs):
                            last = mm(ps[:, 4 + g, i * P:(i + 1) * P], N_[i], Y[:, h].rearrange("p a c -> p (a c)"),
                                      start=True, stop=True)
                        last.then_inc(app_mm, 1)
                pe.wait_ge(app_ev, 2 * POW * (t + 1))
                for h in range(HEADS):
                    rows = slice(64 * (h % 2), 64 * (h % 2) + 64)
                    last = mm(ps[rows, 6, h // 2 * P:(h // 2 + 1) * P], Y[:, h, 0, :], pr[:, h, 1, :], start=True, stop=True)
                last.then_inc(r_mm, 1)
                for h in range(HEADS):
                    o = ps[:, 7, h * CH:(h + 1) * CH]
                    mm(o, pr[:, h, 3, :], hd(X_V, h), start=True, stop=False)
                    last = mm(o, pr[:, h, 1, :], Y[:, h, 1, :], start=False, stop=True)
                last.then_inc(y0_mm, 1)
                for i in range(HP):
                    last = mm(ps[:, 0, 2 * i:2 * i + 2], x[:, s, X_LW, i * P:(i + 1) * P], halves[:, :], start=True, stop=True)
                for c in range(2):
                    tk = slice(64 * c, 64 * c + 64)
                    for h in range(HEADS):
                        rows = slice(64 * (h % 2), 64 * (h % 2) + 64)
                        i = h // 2
                        at = lambda q: x[tk, s, q, h * CH:(h + 1) * CH]
                        mm(ps[rows, 4 + c, i * CH:(i + 1) * CH], Y[tk, h, 0, :], at(X_NB), start=True, stop=True)
                        o = ps[rows, 4 + c, (HP + i) * CH:(HP + i + 1) * CH]
                        mm(o, at(X_K), at(X_V), start=True, stop=False)
                        last = mm(o, at(X_NB), Y[tk, h, 1, :], start=False, stop=True)
                    last.then_inc(zn_mm, 1)
                pe.wait_ge(pc_ev, t + 1)
                pe.wait_ge(r_ev, t + 1)
                for c in range(2):
                    pe.wait_ge(zn_ev, 2 * t + c + 1)
                    pe.wait_ge(m_ready, 2 * t + c + 1)
                    tk = slice(64 * c, 64 * c + 64)
                    for h in range(HEADS):
                        g, i = h % 2, h // 2
                        rows = slice(64 * g, 64 * g + 64)
                        mm(ps[rows, 2 + g, i * CH:(i + 1) * CH], ZN[rows, c, 0, i, :], M[rows, i, :], start=True, stop=True)
                        last = mm(ps[tk, g, i * CH:(i + 1) * CH], RT[rows, i, tk], M[rows, i, :], start=True, stop=True)
                    last.then_inc(step_mm, 1)
            pe.wait_ge(m_ready, 2 * PT + 1)
            pe.wait_ge(y_ready, PT)
            for i in range(HP):
                last = nc.tensor.transpose(ps[0:CH, 0, i * P:(i + 1) * P], M[:, i, :], ident[:, :])
            last.then_inc(end_tr, 1)

        @block.scalar
        def _(act):
            for t in range(PT):
                cp = lambda o, i: nc.scalar.activation(o, i, ACT.Copy)
                for i in range(HP):
                    act.wait_ge(tr, HP * t + i + 1)
                    cp(xT[:, i].rearrange("p a c -> p (a c)"), ps[:, i, :]).then_inc(tr_ev, 1)
                n = 18 * t
                for j in range(1, POW):
                    for g in range(2):
                        for k in range(2 if j + 1 < POW else 1):
                            act.wait_ge(sq_mm, n + 1)
                            if j >= 2:
                                act.wait_ge(app_mm, 2 * POW * t + 2 * (j - 2) + g + 1)
                            cp(NL[:, j % 2, k, 4 * g:4 * g + 4, :].rearrange("p a c -> p (a c)"), ps[:, 2 * g + k, :]
                               ).then_inc(sq_ev, 1)
                            n += 1
                act.wait_ge(y0_mm, t + 1)
                if t >= 2:
                    act.wait_ge(st[t % 2], 16 * (t // 2))
                cp(y0[:, t % 2, :], ps[:, 7, :]).then_inc(y0_ev, 1)
                act.wait_ge(zn_mm, 2 * t + 1)
                nc.scalar.activation(pcs[:, :, :].rearrange("p a c -> p (a c)"), ps[:, 0, 0:2 * HP], ACT.Exp).then_inc(pc_ev, 1)
                for c in range(2):
                    act.wait_ge(z_ev, 2 * t + c + 1)
                    cp(ZN[:, c, 1].rearrange("p a c -> p (a c)"), ps[:, 4 + c, HP * CH:]).then_inc(zn_ev, 1)
            act.wait_ge(end_tr, 1)
            nc.scalar.activation(mt[:, :, :].rearrange("p a c -> p (a c)"), ps[0:CH, 0, :], ACT.Copy).then_inc(end_cp, 1)

        @block.vector
        def _(dve):
            tt = nc.vector.tensor_tensor
            dve.wait_ge(const_ld, n_const)
            nc.vector.memset(M[:, :, :], 0.0).then_inc(m_ready, 1)
            own = 0
            for t in range(PT):
                s = t % 2
                for h in range(HEADS):
                    dve.wait_ge(prod_mm, HEADS * t + h + 1)
                    tt(pr[:, h].rearrange("p a c -> p (a c)"), ps[:, 4 + h % 4, :],
                       masks[:, 0:4, :].rearrange("p a c -> p (a c)"), ALU.mult).then_inc(prod_ev, 1)
                    if h % 4 == 3:
                        pick_round(dve)
                low = NL[:, 0, 1].rearrange("p (i g) c -> p g i c", g=2)
                for g in range(2):
                    dve.wait_ge(low_mm, 2 * t + g + 1)
                    tt(low[:, g], ps[:, g, :].rearrange("p (i c) -> p i c", c=P),
                       wide(masks[:, 4, :].unsqueeze(1), [P, HP, P]), ALU.mult).then_inc(low_ev, 1)
                nc.vector.tensor_copy(Y[:, :, 0, :], x[:, s, X_A, :].rearrange("p (h d) -> p h d", h=HEADS)).then_inc(y_set, 1)
                dve.wait_ge(akv_mm, t + 1)
                nc.vector.tensor_copy(Y[:, :, 1, :], ps[:, 2, :].rearrange("p (h d) -> p h d", h=HEADS)).then_inc(y_set, 1)
                pick_round(dve)
                dve.wait_ge(y_set, 2 * (t + 1))
                for j in range(POW):
                    for g in range(2):
                        n = 2 * POW * t + 2 * j + g
                        dve.wait_ge(app_mm, n + 1)
                        yg = Y[:, 4 * g:4 * g + 4].rearrange("p h a c -> p (h a c)")
                        at_least(dve, app_ev, n - 1)
                        tt(yg, ps[:, 4 + g, :], yg, ALU.add).then_inc(app_ev, 1)
                    if j:
                        pick_round(dve)
                for _ in range(6):
                    pick_round(dve)
                dve.wait_ge(r_mm, t + 1)
                tt(RT[:, :, :], ps[:, 6, :].rearrange("p (i c) -> p i c", c=P), xT[:, :, 1, :], ALU.add).then_inc(r_ev, 1)
                pick_round(dve)
                for c in range(2):
                    dve.wait_ge(zn_mm, 2 * t + c + 1)
                    tt(ZN[:, c, 0], ps[:, 4 + c, 0:HP * CH].rearrange("p (i k) -> p i k", k=CH),
                       wide(eye2[:, :].unsqueeze(1), [P, HP, CH]), ALU.add).then_inc(z_ev, 1)
                    pick_round(dve)
                dve.wait_ge(pc_ev, t + 1)
                for c in range(2):
                    dve.wait_ge(step_mm, 2 * t + c + 1)
                    dve.wait_ge(zn_ev, 2 * t + c + 1)
                    for g in range(2):
                        rows = slice(64 * g, 64 * g + 64)
                        last = tt(Ms[rows, :, :], ps[rows, 2 + g, 0:HP * CH].rearrange("p (i k) -> p i k", k=CH),
                                  ZN[rows, c, 1], ALU.add)
                    last.then_inc(m_own, 1)
                    own += 1
                    dve.wait_ge(m_own, own)
                    tt(M[:, :, :], Ms[:, :, :], wide(pcs[:, :, c:c + 1], [P, HP, CH]), ALU.mult).then_inc(m_ready, 1)
                    pick_round(dve)
                dve.wait_ge(y0_ev, t + 1)
                for g in range(2):
                    yv = y0[:, s, :].rearrange("p (i g v) -> p g i v", g=2, v=CH)[:, g]
                    last = tt(yv, ps[:, g, 0:HP * CH].rearrange("p (i v) -> p i v", v=CH), yv, ALU.add)
                last.then_inc(y_ready, 1)
                pick_round(dve)


def rwkv_output(nc, A, rw, y_in, mix):
    with Phase(nc, "rwo") as ph:
        y = ph.sb("y", [P, 2, HALF])
        gb = ph.sb("gb", [P, 2, 2, HALF])
        par = ph.sb("par", [P, 2, HALF])
        sq = ph.sb("sq", [P, 2, HALF])
        stat = ph.sb("stat", [P, 4, HEADS])
        eps = ph.sb("eps", [P, 1])
        const_ld = ph.sem("const_ld")
        ld = [ph.sem(f"ld{i}") for i in range(2)]
        set_up = ph.sem("set_up")
        centred = ph.sem("centred")
        squared = ph.sem("squared")
        var = ph.sem("var")
        root = ph.sem("root")
        own = ph.sem("own")
        ready = ph.sem("ready")
        st = [ph.sem(f"st{i}") for i in range(2)]
        block = ph.block()

        @block.sync
        def _(sp):
            for i, nm in enumerate(["rwkv_ln_g", "rwkv_ln_b"]):
                sp.dma_start(par[:, i, :], A[nm].broadcast_to([P, HALF])).then_inc(const_ld, 16)
            for t in range(TT):
                r, s = rows_of(t), t % 2
                if t >= 2:
                    sp.wait_ge(st[s], 16 * (t // 2))
                sp.dma_start(y[0:r, s, :], y_in[t * P:t * P + r, :]).then_inc(ld[s], 16)
                sp.dma_start(gb[0:r, s, :, :], rw[t * P:t * P + r, W_G:W_BONUS + 1, :]).then_inc(ld[s], 16)

        @block.gpsimd
        def _(pool):
            for t in range(TT):
                r, s = rows_of(t), t % 2
                pool.wait_ge(ready, t + 1)
                pool.dma_start(mix[t * P:t * P + r, :], y[0:r, s, :]).then_inc(st[s], 16)
            for s in range(2):
                pool.wait_ge(st[s], 16 * ((TT + 1 - s) // 2))

        @block.scalar
        def _(act):
            act.wait_ge(set_up, 1)
            for t in range(TT):
                r, s = rows_of(t), t % 2
                act.wait_ge(centred, t + 1)
                nc.scalar.activation(sq[0:r, s, :], y[0:r, s, :], ACT.Square).then_inc(squared, 1)
                act.wait_ge(var, t + 1)
                nc.scalar.activation(stat[0:r, 2, :], stat[0:r, 1, :], ACT.Sqrt, bias=eps[0:r, :],
                                     scale=1.0 / HEAD_DIM).then_inc(root, 1)

        @block.vector
        def _(dve):
            link = Chain(dve, own)
            tt = nc.vector.tensor_tensor
            nc.vector.memset(eps[:, :], GN_EPS).then_inc(set_up, 1)
            dve.wait_ge(const_ld, 32)
            for t in range(TT):
                r, s = rows_of(t), t % 2
                yf = y[0:r, s, :]
                yv = yf.rearrange("p (h d) -> p h d", h=HEADS)
                hw = lambda i: wide(stat[0:r, i, :].unsqueeze(2), [r, HEADS, HEAD_DIM])
                dve.wait_ge(ld[s], 32 * (t // 2 + 1))
                link(nc.vector.tensor_reduce(stat[0:r, 0, :], yv, AX_X, ALU.add))
                link(nc.vector.tensor_scalar(stat[0:r, 3, :], stat[0:r, 0, :], 1.0 / HEAD_DIM, None, ALU.mult))
                tt(yv, yv, hw(3), ALU.subtract).then_inc(centred, 1)
                dve.wait_ge(squared, t + 1)
                nc.vector.tensor_reduce(stat[0:r, 1, :], sq[0:r, s, :].rearrange("p (h d) -> p h d", h=HEADS), AX_X,
                                        ALU.add).then_inc(var, 1)
                dve.wait_ge(root, t + 1)
                link(nc.vector.reciprocal(stat[0:r, 0, :], stat[0:r, 2, :]))
                link(tt(yv, yv, hw(0), ALU.mult))
                link(tt(yf, yf, par[0:r, 0, :], ALU.mult))
                link(tt(yf, yf, par[0:r, 1, :], ALU.add))
                link(tt(yf, yf, gb[0:r, s, 1, :], ALU.add))
                tt(yf, yf, gb[0:r, s, 0, :], ALU.mult).then_inc(ready, 1)


REL_BUCKETS = 32
REL_MAX_DIST = 128


def constants():
    f32 = np.float32
    k = np.arange(P)
    s = k // S5_GROUP
    r = np.arange(HEADS * DEC_SEQ)
    c = {"c_ident": np.eye(P, dtype=f32)}
    c["c_block_mask"] = (s[None, :] >= s[:, None]).astype(f32)
    c["c_not_before"] = (k[None, :] >= k[:, None]).astype(f32)
    c["c_own_head"] = (r[:, None] // DEC_SEQ == np.arange(HEADS)[None, :]).astype(f32)
    c["c_late"] = (np.arange(DEC_SEQ)[None, :] >= k[:, None] % DEC_SEQ).astype(f32)
    past = k[None, :] > k[:, None]
    c["c_causal"] = np.where(past, CAUSAL, 0).astype(f32)
    c["c_unselected"] = np.where(past, NOT_SELECTED, 0).astype(f32)
    q = np.arange(NS) % DEC_SEQ
    c["c_late_causal"] = np.where(np.arange(DEC_SEQ)[None, :] > q[:, None], CAUSAL, 0).astype(f32)
    g = np.arange(NS) // DEC_SEQ
    c["c_w_mask"] = ((np.arange(DEC_BATCH)[None, :, None] == g[None, None, :])
                     & ((r % DEC_SEQ)[:, None, None] == q[None, None, :])).astype(f32)
    exact = REL_BUCKETS // 2
    d = np.maximum(NEAR_TOP - np.arange(NEAR), 0)
    far = exact + (np.log(np.maximum(d, 1).astype(f32) / exact) / math.log(REL_MAX_DIST / exact)
                   * (REL_BUCKETS - exact)).astype(np.int32)
    bucket = np.where(d < exact, d, np.minimum(far, REL_BUCKETS - 1))
    c["c_onehot"] = (np.arange(REL_BUCKETS)[:, None] == bucket[None, :]).astype(f32)
    same = (k[:, None] // CH) == (k[None, :] // CH)
    c["c_chunk_tri"] = (same & (k[:, None] <= k[None, :])).astype(f32)
    strict, incl = same & (k[:, None] < k[None, :]), same & (k[:, None] <= k[None, :])
    below = same & (k[:, None] > k[None, :])
    c["c_chunk_masks"] = np.stack([strict, incl, strict, incl, below], 1).astype(f32)
    c["c_halves"] = (k[:, None] // CH == np.arange(2)[None, :]).astype(f32)
    c["c_eye2"] = (k[:, None] % CH == np.arange(CH)[None, :]).astype(f32)
    return c


def column_chunks(array, n_cols):
    full = n_cols // NC_COLS * NC_COLS

    def dst(t, c, width):
        rows = array[t * P:t * P + rows_of(t), :]
        if width == NC_COLS:
            return rows[:, 0:full].rearrange("p (c n) -> c p n", n=NC_COLS)[c]
        return rows[:, full:n_cols]

    return dst


def copy_rows(nc, name, pairs):
    with Phase(nc, name) as ph:
        copied = ph.sem("copied")
        block = ph.block()

        @block.sync
        def _(sp):
            for out, src in pairs:
                sp.dma_start(out, src).then_inc(copied, 16)
            sp.wait_ge(copied, 16 * len(pairs))


def by_tokens(x):
    n = len(x.shape)
    if n == 5:
        return x.rearrange("i b t h d -> (i b t) (h d)")
    return x.rearrange("i b t d -> (i b t) d") if n == 4 else x.rearrange("b t d -> (b t) d")


def build_program(nc, A, O):
    dram = lambda name, shape: nc.dram_tensor(name, shape, F32).ap()
    ident = A["c_ident"]
    tiles = lambda a: (lambda t: a[t * P:t * P + rows_of(t), :])
    both = lambda p, s: (lambda t: token_rows(p, s, t))
    chunk_of = lambda rows: (lambda t, c: rows(t)[:, c * NC_COLS:(c + 1) * NC_COLS])
    pages = lambda x: x[0].rearrange("n p h d -> n p (h d)")
    flat = lambda x: x.rearrange("a b g n -> (a b) (g n)")
    ev = dram("ev_cols", [TOK, EVEN_IN])
    od = dram("od_cols", [TOK, ODD_IN])
    mix = [dram("mix_even", [TOK, D_MODEL]), dram("mix_odd", [TOK, D_MODEL])]
    x1, x2, x3 = (dram(n, [TOK, D_MODEL]) for n in ("x_even_mixed", "x_even_done", "x_odd_mixed"))
    x0 = both(by_tokens(A["x_prompt"]), by_tokens(A["x_sample"]))
    y = both(by_tokens(O["y_prompt"]), by_tokens(O["y_sample"]))

    def ffn(i, name, src, dst):
        conv_ffn(nc, name, src, A["ffn_norm_g"][i:i + 1], A["ffn_w_in"][i], A["ffn_conv"][i], A["ffn_w_out"][i],
                 A["state_ffn_conv"][i].rearrange("b r c -> (b r) c"), dst,
                 [(O["ffn_conv_prompt"][i, 0], 0, 2),
                  (O["ffn_conv_sample"][i].rearrange("b r c -> (b r) c"), 2, 2 + 2 * DEC_BATCH)], ident)

    with nc.cleanup_on_exit():
        project(nc, "ev_in", x0, A["ev_norm_g"], A["ev_w_in"][0], EVEN_IN, column_chunks(ev, EVEN_IN), ident)
        copy_rows(nc, "ev_new", [
            (by_tokens(O["sb_k_prompt"]), ev[0:SEQ, 2 * HALF:3 * HALF]),
            (by_tokens(O["sb_v_prompt"]), ev[0:SEQ, 3 * HALF:4 * HALF]),
            (by_tokens(O["sb_k_sample"]), ev[SEQ:TOK, 2 * HALF:3 * HALF]),
            (by_tokens(O["sb_v_sample"]), ev[SEQ:TOK, 3 * HALF:4 * HALF])])
        A5 = dict(A, o_s5_re_p=flat(O["s5_re_prompt"]), o_s5_im_p=flat(O["s5_im_prompt"]),
                  o_s5_re_s=flat(O["s5_re_sample"]), o_s5_im_s=flat(O["s5_im_sample"]))
        s5(nc, A5, ev, mix[0])
        qkv = lambda a, c, rows: [a[rows, c[i]:c[i] + HALF] for i in range(3)]
        prompt, sample = slice(0, SEQ), slice(SEQ, TOK)
        cols = (HALF, 2 * HALF, 3 * HALF)
        prompt_attention(nc, "sb", A, *qkv(ev, cols, prompt), mix[0][prompt, HALF:], False)
        sample_attention(nc, "sbs", A, *qkv(ev, cols, sample), pages(A["cache_sb_k"]), pages(A["cache_sb_v"]),
                         mix[0][sample, HALF:], False)

    with nc.cleanup_on_exit():
        project(nc, "ev_out", tiles(mix[0]), None, A["ev_w_out"][0], D_MODEL, column_chunks(x1, D_MODEL), ident,
                resid=chunk_of(x0), norm=False)
        ffn(0, "ffn0", tiles(x1), tiles(x2))

    with nc.cleanup_on_exit():
        project(nc, "od_in", tiles(x2), A["od_norm_g"], A["od_w_in"][0], ODD_IN, column_chunks(od, ODD_IN), ident)
        last_rows = od[SEQ:TOK, 0:RWKV_IN].rearrange("(b s) c -> s b c", s=DEC_SEQ)[DEC_SEQ - 1]
        copy_rows(nc, "od_new", [
            (by_tokens(O["dsa_v_prompt"]), od[prompt, C_V:C_V + HALF]),
            (by_tokens(O["dsa_v_sample"]), od[sample, C_V:C_V + HALF]),
            (by_tokens(O["dsa_idx_k_prompt"]), od[prompt, C_IK:C_IK + IDX_DIM]),
            (by_tokens(O["dsa_idx_k_sample"]), od[sample, C_IK:C_IK + IDX_DIM]),
            (O["rwkv_shift_prompt"][0], od[SEQ - 1:SEQ, 0:RWKV_IN]),
            (O["rwkv_shift_sample"][0], last_rows)])
        A6 = dict(A, near=dram("near_bias", [HEADS, P, NEAR]), near_sample=dram("near_bias_sample", [NS, 260]),
                  sel=dram("selected", [PT, P, SEQ]), sel_sample=dram("selected_sample", [NS, PAST_LEN + DEC_SEQ]))
        qn = dram("q_normed", [TOK, HALF])
        scores, scores_sample = dram("index_scores", [PT, P, SEQ]), dram("index_scores_sample", [NS, ALL_KEYS])
        rw, ry = dram("rwkv_arrays", [TOK, 8, HALF]), dram("rwkv_y", [TOK, HALF])
        kp, ks = by_tokens(O["dsa_k_prompt"]), by_tokens(O["dsa_k_sample"])

    with nc.cleanup_on_exit():
        bias_tables(nc, A, A6["near"], A6["near_sample"])
        qk_norm(nc, A, od, tiles(qn), both(kp, ks))
        score_keys(nc, A, od, A["cache_dsa_idx_k"][0], scores, scores_sample, A6["sel"])
        rwkv_inputs(nc, A, od, rw)

    with nc.cleanup_on_exit():
        rwkv_chunks(nc, A, rw, ry, O["rwkv_prompt"][0, 0], O["rwkv_sample"][0], scores, scores_sample,
                    A6["sel"], A6["sel_sample"])
        rwkv_output(nc, A, rw, ry, mix[1][:, 0:HALF])
        prompt_attention(nc, "dsa", A6, qn[prompt, :], kp, od[prompt, C_V:C_V + HALF], mix[1][prompt, HALF:], True)
        sample_attention(nc, "dsas", A6, qn[sample, :], ks, od[sample, C_V:C_V + HALF], pages(A["cache_dsa_k"]),
                         pages(A["cache_dsa_v"]), mix[1][sample, HALF:], True)

    with nc.cleanup_on_exit():
        project(nc, "od_out", tiles(mix[1]), None, A["od_w_out"][0], D_MODEL, column_chunks(x3, D_MODEL), ident,
                resid=chunk_of(tiles(x2)), norm=False)
        ffn(1, "ffn1", tiles(x3), y)


INPUTS = [
    "x_prompt", "x_sample", "cache_sb_k", "cache_sb_v", "cache_dsa_k", "cache_dsa_v", "cache_dsa_idx_k",
    "state_s5_re", "state_s5_im", "state_rwkv", "state_rwkv_shift", "state_ffn_conv", "page_table", "rel_bias",
    "ev_norm_g", "ev_w_in", "ev_w_out", "s5_lambda_re", "s5_lambda_im", "s5_log_step", "s5_b_re", "s5_b_im",
    "s5_c_re", "s5_c_im", "s5_d", "s5_w_glu", "s5_b_glu", "od_norm_g", "od_w_in", "od_w_out", "rwkv_mu",
    "rwkv_w0", "rwkv_w2", "rwkv_a0", "rwkv_a2", "rwkv_g2", "rwkv_k_k", "rwkv_k_a", "rwkv_r_k", "rwkv_ln_g",
    "rwkv_ln_b", "dsa_q_norm_g", "dsa_k_norm_g", "ffn_norm_g", "ffn_w_in", "ffn_conv", "ffn_w_out"]
S5_G, S5_N = HALF // S5_GROUP, 64
OUTPUTS = {
    "y_prompt": (1, SEQ, D_MODEL), "y_sample": (DEC_BATCH, DEC_SEQ, D_MODEL),
    "sb_k_prompt": (1, 1, SEQ, HEADS, HEAD_DIM), "sb_v_prompt": (1, 1, SEQ, HEADS, HEAD_DIM),
    "sb_k_sample": (1, DEC_BATCH, DEC_SEQ, HEADS, HEAD_DIM), "sb_v_sample": (1, DEC_BATCH, DEC_SEQ, HEADS, HEAD_DIM),
    "dsa_k_prompt": (1, 1, SEQ, HEADS, HEAD_DIM), "dsa_v_prompt": (1, 1, SEQ, HEADS, HEAD_DIM),
    "dsa_idx_k_prompt": (1, 1, SEQ, IDX_DIM),
    "dsa_k_sample": (1, DEC_BATCH, DEC_SEQ, HEADS, HEAD_DIM), "dsa_v_sample": (1, DEC_BATCH, DEC_SEQ, HEADS, HEAD_DIM),
    "dsa_idx_k_sample": (1, DEC_BATCH, DEC_SEQ, IDX_DIM),
    "s5_re_prompt": (1, 1, S5_G, S5_N), "s5_im_prompt": (1, 1, S5_G, S5_N),
    "s5_re_sample": (1, DEC_BATCH, S5_G, S5_N), "s5_im_sample": (1, DEC_BATCH, S5_G, S5_N),
    "rwkv_prompt": (1, 1, HEADS, HEAD_DIM, HEAD_DIM), "rwkv_shift_prompt": (1, 1, RWKV_IN),
    "rwkv_sample": (1, DEC_BATCH, HEADS, HEAD_DIM, HEAD_DIM), "rwkv_shift_sample": (1, DEC_BATCH, RWKV_IN),
    "ffn_conv_prompt": (2, 1, 2, 2 * D_FF), "ffn_conv_sample": (2, DEC_BATCH, 2, 2 * D_FF)}


def kernel(**inputs):
    import concourse.bacc as bacc
    from concourse.bass_utils import run_bass_kernel_spmd

    nc = bacc.Bacc("TRN2", target_bir_lowering=False, num_devices=1)
    arrays = {n: np.ascontiguousarray(inputs[n]) for n in INPUTS}
    arrays.update(constants())
    A = {n: nc.dram_tensor(n, a.shape, mybir.dt.from_np(a.dtype), kind="ExternalInput").ap()
         for n, a in arrays.items()}
    O = {n: nc.dram_tensor("out_" + n, s, F32, kind="ExternalOutput").ap() for n, s in OUTPUTS.items()}
    build_program(nc, A, O)
    r = run_bass_kernel_spmd(nc, [arrays], core_ids=[0])
    return tuple(r.results[0]["out_" + n] for n in OUTPUTS)
```
